# Optimizing a Trainium2 kernel written in Bass

```python
import jax
import jax.numpy as jnp
from jax import lax
import numpy as np
import math
import jax, jax.numpy as jnp

D_MODEL = 1024
BATCH = 1
SEQ = 512
DEPTH = 2

D_MIX = 1024
M_HEADS = 4
M_HEAD_DIM = 96
M_WIDTH = M_HEADS * M_HEAD_DIM
M_CHUNK = 128
CONV_WIDTH = 4
A_HEADS = 6
A_NOPE = 64
A_ROPE = 32
A_QK_DIM = A_NOPE + A_ROPE
A_V_DIM = 64
A_WIDTH = A_HEADS * A_V_DIM
A_Q_RANK = 256
A_KV_RANK = 128
ROPE_THETA = 10000.0
Q_BLOCK = 128
C_GROUPS = 4
C_GROUP_DIM = 64
C_WIDTH = C_GROUPS * C_GROUP_DIM
C_CHUNK = 128
IN_SIZES = (M_WIDTH, M_WIDTH, M_WIDTH, M_WIDTH, M_HEADS, M_HEADS,
            A_Q_RANK, A_KV_RANK, A_ROPE, C_WIDTH, C_WIDTH)
D_IN = 4 * M_WIDTH + 2 * M_HEADS + A_Q_RANK + A_KV_RANK + A_ROPE + 2 * C_WIDTH
N_GROUPS = 4
EXPERTS_PER_GROUP = 8
N_EXPERTS = N_GROUPS * EXPERTS_PER_GROUP
TOP_K = 2
D_EXPERT = 256
MOE_BLOCK = 256
EPS = 1e-6


def rms_norm(x, gain):
    xf = x.astype(jnp.float32)
    y = xf * lax.rsqrt(jnp.mean(xf * xf, axis=-1, keepdims=True) + EPS)
    return (y * gain.astype(jnp.float32)).astype(x.dtype)

def head_rms_norm(x, gain, n_heads):
    b, s, w = x.shape
    y = rms_norm(x.reshape(b, s, n_heads, w // n_heads), gain.reshape(n_heads, w // n_heads))
    return y.reshape(b, s, w)

def split_cols(t, sizes):
    out, off = [], 0
    for size in sizes:
        out.append(t[..., off:off + size])
        off += size
    return out

def causal_depthwise_conv(x, w, b):
    width, seq = w.shape[0], x.shape[1]
    xp = jnp.pad(x, ((0, 0), (width - 1, 0), (0, 0)))
    y = b
    for j in range(width):
        y = y + xp[:, j:j + seq] * w[j]
    return y

def mlstm_chunkwise(q, k, v, i_pre, f_pre):
    B, S, H, Dh = q.shape
    L = M_CHUNK
    N = S // L
    f32 = jnp.float32
    def to_chunks(t):
        return t.astype(f32).reshape(B, N, L, H, -1).transpose(1, 0, 3, 2, 4)
    qc = to_chunks(q)
    kc = to_chunks(k) * (Dh ** -0.5)
    vc = to_chunks(v)
    log_f = jax.nn.log_sigmoid(f_pre.astype(f32)).reshape(B, N, L, H).transpose(1, 0, 3, 2)
    log_i = i_pre.astype(f32).reshape(B, N, L, H).transpose(1, 0, 3, 2)
    bcum = jnp.cumsum(log_f, axis=-1)
    causal = jnp.tril(jnp.ones((L, L), dtype=bool))

    def step(carry, inp):
        C, n, m = carry
        qt, kt, vt, bt, it = inp
        d = bt[..., :, None] - bt[..., None, :] + it[..., None, :]
        d = jnp.where(causal, d, -jnp.inf)
        inter = bt + m[..., None]
        m_row = jnp.maximum(inter, jnp.max(d, axis=-1))
        w_intra = jnp.exp(d - m_row[..., None])
        w_inter = jnp.exp(inter - m_row)
        s = jnp.einsum('bhld,bhsd->bhls', qt, kt) * w_intra
        num = (jnp.einsum('bhls,bhsd->bhld', s, vt)
               + w_inter[..., None] * jnp.einsum('bhvk,bhlk->bhlv', C, qt))
        den = jnp.sum(s, axis=-1) + w_inter * jnp.einsum('bhk,bhlk->bhl', n, qt)
        h = num / jnp.maximum(jnp.abs(den), jnp.exp(-m_row))[..., None]
        b_last = bt[..., -1]
        g = b_last[..., None] - bt + it
        m_new = jnp.maximum(b_last + m, jnp.max(g, axis=-1))
        a = jnp.exp(b_last + m - m_new)
        wg = jnp.exp(g - m_new[..., None])
        C_new = a[..., None, None] * C + jnp.einsum('bhs,bhsv,bhsk->bhvk', wg, vt, kt)
        n_new = a[..., None] * n + jnp.einsum('bhs,bhsk->bhk', wg, kt)
        return (C_new, n_new, m_new), h

    init = (jnp.zeros((B, H, Dh, Dh), f32), jnp.zeros((B, H, Dh), f32), jnp.zeros((B, H), f32))
    _, h = lax.scan(step, init, (qc, kc, vc, bcum, log_i))
    return h.transpose(1, 0, 3, 2, 4).reshape(B, S, H, Dh).astype(v.dtype)

def rope_tables(positions):
    inv_freq = 1.0 / (ROPE_THETA ** (jnp.arange(0, A_ROPE, 2, dtype=jnp.float32) / A_ROPE))
    ang = positions.astype(jnp.float32)[..., None] * inv_freq
    return jnp.cos(ang), jnp.sin(ang)

def apply_rope(x, cos, sin):
    half = x.shape[-1] // 2
    xf = x.astype(jnp.float32)
    c, s = cos[:, :, None, :], sin[:, :, None, :]
    x1, x2 = xf[..., :half], xf[..., half:]
    return jnp.concatenate([x1 * c - x2 * s, x1 * s + x2 * c], axis=-1).astype(x.dtype)

def causal_block_attention(q, k, v):
    B, S, H, Dq = q.shape
    nb = S // Q_BLOCK
    scale = Dq ** -0.5
    qb = q.reshape(B, nb, Q_BLOCK, H, Dq).transpose(1, 0, 2, 3, 4)
    kpos = jnp.arange(S)

    def one_block(args):
        qi, idx = args
        s = jnp.einsum('blhd,bshd->bhls', qi, k, preferred_element_type=jnp.float32) * scale
        qpos = idx * Q_BLOCK + jnp.arange(Q_BLOCK)
        s = jnp.where(kpos[None, :] <= qpos[:, None], s, -jnp.inf)
        p = jax.nn.softmax(s, axis=-1).astype(v.dtype)
        return jnp.einsum('bhls,bshd->blhd', p, v)

    o = lax.map(one_block, (qb, jnp.arange(nb)))
    return o.transpose(1, 0, 2, 3, 4).reshape(B, S, H, v.shape[-1])

def mla_mixer(c_q, c_kv, k_rope, cos, sin, q_gain, kv_gain, w_uq, w_ukv, qh_gain, kh_gain):
    B, S, _ = c_q.shape
    q = (rms_norm(c_q, q_gain) @ w_uq).reshape(B, S, A_HEADS, A_QK_DIM)
    kv = (rms_norm(c_kv, kv_gain) @ w_ukv).reshape(B, S, A_HEADS, A_NOPE + A_V_DIM)
    k_nope, v = kv[..., :A_NOPE], kv[..., A_NOPE:]
    k = jnp.concatenate([k_nope, jnp.broadcast_to(k_rope[:, :, None, :], (B, S, A_HEADS, A_ROPE))], axis=-1)
    q = rms_norm(q, qh_gain)
    k = rms_norm(k, kh_gain)
    q = jnp.concatenate([q[..., :A_NOPE], apply_rope(q[..., A_NOPE:], cos, sin)], axis=-1)
    k = jnp.concatenate([k[..., :A_NOPE], apply_rope(k[..., A_NOPE:], cos, sin)], axis=-1)
    o = causal_block_attention(q, k, v)
    return o.reshape(B, S, A_WIDTH)

def chunk_spatial_gating(u, v, v_gain, w_s, b_s):
    B, S, _ = u.shape
    n = S // C_CHUNK
    v = rms_norm(v.reshape(B, S, C_GROUPS, C_GROUP_DIM), v_gain.reshape(C_GROUPS, C_GROUP_DIM))
    vc = v.reshape(B, n, C_CHUNK, C_GROUPS, C_GROUP_DIM)
    w = w_s * jnp.tril(jnp.ones((C_CHUNK, C_CHUNK), dtype=w_s.dtype))
    mixed = jnp.einsum('gts,bnsgd->bntgd', w, vc) + b_s.T[None, None, :, :, None]
    return u * mixed.reshape(B, S, C_WIDTH)

def hier_moe(x, w_group, b_group, w_expert, b_expert, w1, w3, w2):
    B, S, D = x.shape
    T = B * S
    xt = x.reshape(T, D)
    f32 = jnp.float32
    g_logits = (xt @ w_group).astype(f32)
    g_prob = jax.nn.softmax(g_logits, axis=-1)
    _, g_sel = lax.top_k(g_logits + b_group.astype(f32), 1)
    g_sel = g_sel[:, 0]
    tok = jnp.arange(T)
    g_gate = g_prob[tok, g_sel]
    e_logits = (xt @ w_expert).astype(f32).reshape(T, N_GROUPS, EXPERTS_PER_GROUP)
    e_logits = e_logits[tok, g_sel]
    e_bias = b_expert.astype(f32).reshape(N_GROUPS, EXPERTS_PER_GROUP)[g_sel]
    e_prob = jax.nn.softmax(e_logits, axis=-1)
    _, e_local = lax.top_k(e_logits + e_bias, TOP_K)
    e_w = jnp.take_along_axis(e_prob, e_local, axis=1)
    e_w = e_w / jnp.sum(e_w, axis=-1, keepdims=True)
    weights = g_gate[:, None] * e_w
    expert_id = g_sel[:, None] * EXPERTS_PER_GROUP + e_local

    A = T * TOP_K
    flat_e = expert_id.reshape(A)
    flat_tok = jnp.arange(A, dtype=jnp.int32) // TOP_K
    flat_w = weights.reshape(A)
    order = jnp.argsort(flat_e)
    se, stok, sw = flat_e[order], flat_tok[order], flat_w[order]
    counts = jnp.bincount(flat_e, length=N_EXPERTS)
    starts = jnp.cumsum(counts) - counts
    padded = ((counts + MOE_BLOCK - 1) // MOE_BLOCK) * MOE_BLOCK
    pad_ends = jnp.cumsum(padded)
    pad_starts = pad_ends - padded
    dest = pad_starts[se] + jnp.arange(A) - starts[se]
    n_blocks = -(-A // MOE_BLOCK) + N_EXPERTS
    P = n_blocks * MOE_BLOCK
    row_tok = jnp.full((P,), T, dtype=jnp.int32).at[dest].set(stok)
    row_w = jnp.zeros((P,), dtype=x.dtype).at[dest].set(sw.astype(x.dtype))
    block_start = jnp.arange(n_blocks) * MOE_BLOCK
    block_e = jnp.minimum(jnp.sum(pad_ends[None, :] <= block_start[:, None], axis=1), N_EXPERTS - 1)
    x_pad = jnp.concatenate([xt, jnp.zeros((1, D), dtype=x.dtype)], axis=0)

    def expert_block(args):
        rows, rw, e = args
        xi = x_pad[rows]
        h = jax.nn.silu(xi @ w1[e]) * (xi @ w3[e])
        return (h @ w2[e]) * rw[:, None]

    yb = lax.map(expert_block, (row_tok.reshape(n_blocks, MOE_BLOCK), row_w.reshape(n_blocks, MOE_BLOCK), block_e))
    out = jnp.zeros((T + 1, D), dtype=x.dtype).at[row_tok].add(yb.reshape(P, D))[:T]
    return out.reshape(B, S, D)

def first_inputs(seed: int = 0) -> dict:
    key = jax.random.key(seed)
    ks = jax.random.split(key, 32)
    nrm = jax.random.normal
    def gain(k, n):
        return 1.0 + 0.02 * nrm(k, (DEPTH, n), jnp.float32)
    x = nrm(ks[0], (BATCH, SEQ, D_MODEL), jnp.float32)
    offsets = jax.random.randint(ks[1], (BATCH, 1), 0, 4096, dtype=jnp.int32)
    positions = offsets + jnp.arange(SEQ, dtype=jnp.int32)[None, :]
    f_bias = jnp.linspace(3.0, 6.0, M_HEADS, dtype=jnp.float32)[None, :]
    m_gate_bias = jnp.concatenate([0.1 * nrm(ks[6], (DEPTH, M_HEADS), jnp.float32),
                                   f_bias + 0.1 * nrm(ks[7], (DEPTH, M_HEADS), jnp.float32)], axis=-1)
    return {
        'x': x,
        'positions': positions,
        'attn_norm': gain(ks[2], D_MODEL),
        'w_in': nrm(ks[3], (DEPTH, D_MODEL, D_IN), jnp.float32) * D_MODEL ** -0.5,
        'm_conv_w': nrm(ks[4], (DEPTH, CONV_WIDTH, 2 * M_WIDTH), jnp.float32) * CONV_WIDTH ** -0.5,
        'm_conv_b': 0.02 * nrm(ks[5], (DEPTH, 2 * M_WIDTH), jnp.float32),
        'm_gate_bias': m_gate_bias,
        'a_q_norm': gain(ks[8], A_Q_RANK),
        'a_kv_norm': gain(ks[9], A_KV_RANK),
        'a_w_uq': nrm(ks[10], (DEPTH, A_Q_RANK, A_HEADS * A_QK_DIM), jnp.float32) * A_Q_RANK ** -0.5,
        'a_w_ukv': nrm(ks[11], (DEPTH, A_KV_RANK, A_HEADS * (A_NOPE + A_V_DIM)), jnp.float32) * A_KV_RANK ** -0.5,
        'a_q_head_norm': gain(ks[12], A_QK_DIM),
        'a_k_head_norm': gain(ks[13], A_QK_DIM),
        'c_v_norm': gain(ks[14], C_WIDTH),
        'c_w_s': nrm(ks[15], (DEPTH, C_GROUPS, C_CHUNK, C_CHUNK), jnp.float32) * C_CHUNK ** -0.5,
        'c_b_s': 1.0 + 0.1 * nrm(ks[16], (DEPTH, C_GROUPS, C_CHUNK), jnp.float32),
        'mix_out_norm': gain(ks[17], D_MIX),
        'w_out': nrm(ks[18], (DEPTH, D_MIX, D_MODEL), jnp.float32) * (D_MIX ** -0.5) * ((2 * DEPTH) ** -0.5),
        'ffn_norm': gain(ks[19], D_MODEL),
        'w_group': nrm(ks[20], (DEPTH, D_MODEL, N_GROUPS), jnp.float32) * D_MODEL ** -0.5,
        'b_group': 0.01 * nrm(ks[21], (DEPTH, N_GROUPS), jnp.float32),
        'w_expert': nrm(ks[22], (DEPTH, D_MODEL, N_EXPERTS), jnp.float32) * D_MODEL ** -0.5,
        'b_expert': 0.01 * nrm(ks[23], (DEPTH, N_EXPERTS), jnp.float32),
        'w1': nrm(ks[24], (DEPTH, N_EXPERTS, D_MODEL, D_EXPERT), jnp.float32) * D_MODEL ** -0.5,
        'w3': nrm(ks[25], (DEPTH, N_EXPERTS, D_MODEL, D_EXPERT), jnp.float32) * D_MODEL ** -0.5,
        'w2': nrm(ks[26], (DEPTH, N_EXPERTS, D_EXPERT, D_MODEL), jnp.float32) * D_EXPERT ** -0.5 * ((2 * DEPTH) ** -0.5),
    }

def first_block(x, positions, attn_norm, w_in, m_conv_w, m_conv_b, m_gate_bias, a_q_norm, a_kv_norm,
              a_w_uq, a_w_ukv, a_q_head_norm, a_k_head_norm, c_v_norm, c_w_s, c_b_s, mix_out_norm,
              w_out, ffn_norm, w_group, b_group, w_expert, b_expert, w1, w3, w2):
    B, S, _ = x.shape
    cos, sin = rope_tables(positions)
    for l in range(DEPTH):
        h = rms_norm(x, attn_norm[l])
        proj = h @ w_in[l]
        mq, mk, mv, mo, mi, mf, cq, ckv, krope, cu, cv = split_cols(proj, IN_SIZES)
        qk = jax.nn.silu(causal_depthwise_conv(jnp.concatenate([mq, mk], axis=-1), m_conv_w[l], m_conv_b[l]))
        mq, mk = qk[..., :M_WIDTH], qk[..., M_WIDTH:]
        gb = m_gate_bias[l]
        hm = mlstm_chunkwise(mq.reshape(B, S, M_HEADS, M_HEAD_DIM),
                             mk.reshape(B, S, M_HEADS, M_HEAD_DIM),
                             mv.reshape(B, S, M_HEADS, M_HEAD_DIM),
                             mi + gb[:M_HEADS], mf + gb[M_HEADS:])
        hm = jax.nn.sigmoid(mo) * hm.reshape(B, S, M_WIDTH)
        ha = mla_mixer(cq, ckv, krope, cos, sin, a_q_norm[l], a_kv_norm[l], a_w_uq[l], a_w_ukv[l],
                       a_q_head_norm[l], a_k_head_norm[l])
        hc = chunk_spatial_gating(jax.nn.gelu(cu), jax.nn.gelu(cv), c_v_norm[l], c_w_s[l], c_b_s[l])
        g = mix_out_norm[l]
        y = jnp.concatenate([head_rms_norm(hm, g[:M_WIDTH], M_HEADS),
                             head_rms_norm(ha, g[M_WIDTH:M_WIDTH + A_WIDTH], A_HEADS),
                             head_rms_norm(hc, g[M_WIDTH + A_WIDTH:], C_GROUPS)], axis=-1)
        x = x + y @ w_out[l]
        x = x + hier_moe(rms_norm(x, ffn_norm[l]), w_group[l], b_group[l], w_expert[l], b_expert[l],
                         w1[l], w3[l], w2[l])
    return x


D_MIX_2 = D_MODEL
DN_HEADS = 4
DN_DK = 128
DN_DV = 128
DN_CONV = 4
DN_CHUNK = 64
DN_WIDTH = DN_HEADS * DN_DV
DN_KEY_WIDTH = DN_HEADS * DN_DK
GLA_HEADS = 4
GLA_DK = 64
GLA_DV = 128
GLA_GATE_RANK = 16
GLA_TAU = 16.0
GLA_CHUNK = 16
GLA_WIDTH = GLA_HEADS * GLA_DV
GLA_KEY_WIDTH = GLA_HEADS * GLA_DK
IN_SIZES_2 = (DN_KEY_WIDTH, DN_KEY_WIDTH, DN_WIDTH,
            DN_WIDTH,
            DN_HEADS, DN_HEADS,
            GLA_KEY_WIDTH, GLA_KEY_WIDTH, GLA_WIDTH,
            GLA_WIDTH,
            GLA_GATE_RANK)
D_IN_PROJ = 3 * 512 + 512 + 4 + 4 + 256 + 256 + 512 + 512 + 16
DEEPNORM_ALPHA = (2.0 * DEPTH) ** 0.25
DEEPNORM_BETA = (8.0 * DEPTH) ** -0.25
NORM_EPS = 1e-6


def _split(a, sizes):
    out, off = [], 0
    for s in sizes:
        out.append(a[..., off:off + s])
        off += s
    return out

def _to_chunks(a, chunk):
    b, t = a.shape[:2]
    a = a.reshape((b, t // chunk, chunk) + a.shape[2:])
    return jnp.moveaxis(a, 3, 1)

def _from_scan(o):
    n, b, h, c, d = o.shape
    return jnp.transpose(o, (1, 0, 3, 2, 4)).reshape(b, n * c, h, d)

def causal_short_conv(x, w):
    k, c = w.shape
    return lax.conv_general_dilated(
        x, w[:, None, :].astype(x.dtype), window_strides=(1,),
        padding=[(k - 1, 0)], dimension_numbers=("NWC", "WIO", "NWC"),
        feature_group_count=c)

def l2norm(x):
    xf = x.astype(jnp.float32)
    return xf * lax.rsqrt(jnp.sum(xf * xf, axis=-1, keepdims=True) + NORM_EPS)

def head_rms_norm_2(o, g):
    of = o.astype(jnp.float32)
    of = of * lax.rsqrt(jnp.mean(of * of, axis=-1, keepdims=True) + NORM_EPS)
    return of * g.astype(jnp.float32)

def layer_norm(x, g, b):
    xf = x.astype(jnp.float32)
    mu = jnp.mean(xf, axis=-1, keepdims=True)
    var = jnp.mean(jnp.square(xf - mu), axis=-1, keepdims=True)
    y = (xf - mu) * lax.rsqrt(var + NORM_EPS) * g.astype(jnp.float32) + b.astype(jnp.float32)
    return y.astype(x.dtype)

def gated_delta_rule_chunked(q, k, v, g, beta):
    f32 = jnp.float32
    q, k, v, g, beta = (a.astype(f32) for a in (q, k, v, g, beta))
    b_, t, h, dk = q.shape
    dv = v.shape[-1]
    c = DN_CHUNK
    qc, kc, vc = (_to_chunks(a, c) for a in (q, k, v))
    gc, bc = _to_chunks(g, c), _to_chunks(beta, c)
    G = jnp.cumsum(gc, axis=-1)
    pos = jnp.arange(c)
    causal = pos[:, None] >= pos[None, :]
    strict = pos[:, None] > pos[None, :]
    diff = G[..., :, None] - G[..., None, :]
    decay = jnp.where(causal, jnp.exp(jnp.where(causal, diff, 0.0)), 0.0)
    k_beta = kc * bc[..., None]
    kk = jnp.einsum("bhnid,bhnjd->bhnij", k_beta, kc)
    lower = jnp.eye(c, dtype=f32) + jnp.where(strict, kk * decay, 0.0)
    rhs = jnp.concatenate([vc * bc[..., None], k_beta * jnp.exp(G)[..., None]], axis=-1)
    uw = lax.linalg.triangular_solve(lower, rhs, left_side=True, lower=True)
    u, w = uw[..., :dv], uw[..., dv:]
    attn = jnp.einsum("bhnid,bhnjd->bhnij", qc, kc) * decay
    xs = tuple(jnp.moveaxis(a, 2, 0) for a in (qc, kc, u, w, G, attn))
    s0 = jnp.zeros((b_, h, dk, dv), f32)

    def step(S, inp):
        q_n, k_n, u_n, w_n, g_n, a_n = inp
        v_new = u_n - jnp.einsum("bhid,bhde->bhie", w_n, S)
        o_n = (jnp.einsum("bhid,bhde->bhie", q_n * jnp.exp(g_n)[..., None], S)
               + jnp.einsum("bhij,bhje->bhie", a_n, v_new))
        g_last = g_n[..., -1]
        k_dec = k_n * jnp.exp(g_last[..., None] - g_n)[..., None]
        S = S * jnp.exp(g_last)[..., None, None] + jnp.einsum("bhid,bhie->bhde", k_dec, v_new)
        return S, o_n

    _, o = lax.scan(step, s0, xs)
    return _from_scan(o)

def gla_chunked(q, k, v, gk):
    f32 = jnp.float32
    q, k, v, gk = (a.astype(f32) for a in (q, k, v, gk))
    b_, t, h, dk = q.shape
    dv = v.shape[-1]
    c = GLA_CHUNK
    qc, kc, vc, gc = (_to_chunks(a, c) for a in (q, k, v, gk))
    Bc = jnp.cumsum(gc, axis=-2)
    pos = jnp.arange(c)
    causal = (pos[:, None] >= pos[None, :])[..., None]
    diff = Bc[..., :, None, :] - Bc[..., None, :, :]
    dec = jnp.where(causal, jnp.exp(jnp.where(causal, diff, 0.0)), 0.0)
    attn = jnp.einsum("bhnid,bhnjd,bhnijd->bhnij", qc, kc, dec)
    xs = tuple(jnp.moveaxis(a, 2, 0) for a in (qc, kc, vc, Bc, attn))
    s0 = jnp.zeros((b_, h, dk, dv), f32)

    def step(S, inp):
        q_n, k_n, v_n, b_n, a_n = inp
        o_n = (jnp.einsum("bhid,bhde->bhie", q_n * jnp.exp(b_n), S)
               + jnp.einsum("bhij,bhje->bhie", a_n, v_n))
        b_last = b_n[..., -1:, :]
        k_dec = k_n * jnp.exp(b_last - b_n)
        S = S * jnp.exp(b_last[..., 0, :])[..., None] + jnp.einsum("bhid,bhie->bhde", k_dec, v_n)
        return S, o_n

    _, o = lax.scan(step, s0, xs)
    return _from_scan(o)

def hybrid_layer(x, w_in, conv_w, dn_a_log, dn_dt_bias, gla_gate_w2, gla_gate_b,
                 dn_norm_g, gla_norm_g, w_out, ln_g, ln_b):
    bsz, t, _ = x.shape
    proj = jnp.einsum("btd,de->bte", x, w_in)
    (dn_q, dn_k, dn_v, dn_z, dn_b, dn_a,
     g_q, g_k, g_v, g_z, g_r) = _split(proj, IN_SIZES_2)

    dn_qkv = jax.nn.silu(causal_short_conv(jnp.concatenate([dn_q, dn_k, dn_v], axis=-1), conv_w))
    cq, ck, cv = _split(dn_qkv, (DN_KEY_WIDTH, DN_KEY_WIDTH, DN_WIDTH))
    q = l2norm(cq.reshape(bsz, t, DN_HEADS, DN_DK)) * (DN_DK ** -0.5)
    k = l2norm(ck.reshape(bsz, t, DN_HEADS, DN_DK))
    v = cv.reshape(bsz, t, DN_HEADS, DN_DV)
    beta = jax.nn.sigmoid(dn_b.astype(jnp.float32))
    g = -jnp.exp(dn_a_log.astype(jnp.float32)) * jax.nn.softplus(
        dn_a.astype(jnp.float32) + dn_dt_bias.astype(jnp.float32))
    o_dn = gated_delta_rule_chunked(q, k, v, g, beta)
    o_dn = head_rms_norm_2(o_dn, dn_norm_g) * jax.nn.silu(
        dn_z.reshape(bsz, t, DN_HEADS, DN_DV).astype(jnp.float32))

    gq = g_q.reshape(bsz, t, GLA_HEADS, GLA_DK) * (GLA_DK ** -0.5)
    gk = g_k.reshape(bsz, t, GLA_HEADS, GLA_DK)
    gv = g_v.reshape(bsz, t, GLA_HEADS, GLA_DV)
    gate_logits = jnp.einsum("btr,re->bte", g_r, gla_gate_w2) + gla_gate_b
    log_f = (jax.nn.log_sigmoid(gate_logits.astype(jnp.float32)) / GLA_TAU).reshape(
        bsz, t, GLA_HEADS, GLA_DK)
    o_gla = gla_chunked(gq, gk, gv, log_f)
    o_gla = head_rms_norm_2(o_gla, gla_norm_g) * jax.nn.silu(
        g_z.reshape(bsz, t, GLA_HEADS, GLA_DV).astype(jnp.float32))

    o = jnp.concatenate([o_dn.reshape(bsz, t, DN_WIDTH),
                         o_gla.reshape(bsz, t, GLA_WIDTH)], axis=-1).astype(x.dtype)
    y = jnp.einsum("bte,ed->btd", o, w_out)
    return layer_norm(DEEPNORM_ALPHA * x + y, ln_g, ln_b)

def second_inputs(seed: int = 0) -> dict:
    key = jax.random.key(seed)
    ks = jax.random.split(key, 12)
    f32 = jnp.float32
    x = jax.random.normal(ks[0], (BATCH, SEQ, D_MODEL), f32)
    col_scale = jnp.concatenate([
        jnp.ones((2 * DN_KEY_WIDTH,), f32),
        jnp.full((DN_WIDTH,), DEEPNORM_BETA, f32),
        jnp.ones((DN_WIDTH + 2 * DN_HEADS + 2 * GLA_KEY_WIDTH,), f32),
        jnp.full((GLA_WIDTH,), DEEPNORM_BETA, f32),
        jnp.ones((GLA_WIDTH + GLA_GATE_RANK,), f32)])
    w_in = jax.random.normal(ks[1], (DEPTH, D_MODEL, D_IN_PROJ), f32) * (D_MODEL ** -0.5) * col_scale
    conv_w = jax.random.normal(ks[2], (DEPTH, DN_CONV, DN_KEY_WIDTH * 2 + DN_WIDTH), f32) * (DN_CONV ** -0.5)
    dn_a_log = jnp.log(jax.random.uniform(ks[3], (DEPTH, DN_HEADS), f32, 1.0, 16.0))
    dt = jnp.exp(jax.random.uniform(ks[4], (DEPTH, DN_HEADS), f32, math.log(1e-3), math.log(1e-1)))
    dn_dt_bias = dt + jnp.log(-jnp.expm1(-dt))
    gla_gate_w2 = jax.random.normal(ks[5], (DEPTH, GLA_GATE_RANK, GLA_KEY_WIDTH), f32) * (GLA_GATE_RANK ** -0.5)
    gla_gate_b = 0.1 * jax.random.normal(ks[6], (DEPTH, GLA_KEY_WIDTH), f32)
    dn_norm_g = 1.0 + 0.02 * jax.random.normal(ks[7], (DEPTH, DN_DV), f32)
    gla_norm_g = 1.0 + 0.02 * jax.random.normal(ks[8], (DEPTH, GLA_DV), f32)
    w_out = jax.random.normal(ks[9], (DEPTH, D_MIX_2, D_MODEL), f32) * (D_MIX_2 ** -0.5) * DEEPNORM_BETA
    ln_g = 1.0 + 0.02 * jax.random.normal(ks[10], (DEPTH, D_MODEL), f32)
    ln_b = 0.02 * jax.random.normal(ks[11], (DEPTH, D_MODEL), f32)
    return {"x": x, "w_in": w_in, "conv_w": conv_w, "dn_a_log": dn_a_log,
            "dn_dt_bias": dn_dt_bias, "gla_gate_w2": gla_gate_w2, "gla_gate_b": gla_gate_b,
            "dn_norm_g": dn_norm_g, "gla_norm_g": gla_norm_g, "w_out": w_out,
            "ln_g": ln_g, "ln_b": ln_b}

def second_block(x, w_in, conv_w, dn_a_log, dn_dt_bias, gla_gate_w2, gla_gate_b,
              dn_norm_g, gla_norm_g, w_out, ln_g, ln_b):
    h = x
    for l in range(DEPTH):
        h = hybrid_layer(h, w_in[l], conv_w[l], dn_a_log[l], dn_dt_bias[l],
                         gla_gate_w2[l], gla_gate_b[l], dn_norm_g[l], gla_norm_g[l],
                         w_out[l], ln_g[l], ln_b[l])
    return h


def setup_inputs(seed=0):
    out = dict(first_inputs(seed))
    for name, value in second_inputs(seed + 1).items():
        if name != "x":
            out[name + "_2"] = value
    return out


def reference(
    x, positions, attn_norm, w_in, m_conv_w, m_conv_b, m_gate_bias, a_q_norm, a_kv_norm, a_w_uq,
    a_w_ukv, a_q_head_norm, a_k_head_norm, c_v_norm, c_w_s, c_b_s, mix_out_norm, w_out,
    ffn_norm, w_group, b_group, w_expert, b_expert, w1, w3, w2, w_in_2, conv_w_2, dn_a_log_2,
    dn_dt_bias_2, gla_gate_w2_2, gla_gate_b_2, dn_norm_g_2, gla_norm_g_2, w_out_2, ln_g_2,
    ln_b_2,
):
    x = first_block(
        x, positions, attn_norm, w_in, m_conv_w, m_conv_b, m_gate_bias, a_q_norm, a_kv_norm,
        a_w_uq, a_w_ukv, a_q_head_norm, a_k_head_norm, c_v_norm, c_w_s, c_b_s, mix_out_norm,
        w_out, ffn_norm, w_group, b_group, w_expert, b_expert, w1, w3, w2,
    )
    return second_block(
        x, w_in_2, conv_w_2, dn_a_log_2, dn_dt_bias_2, gla_gate_w2_2, gla_gate_b_2, dn_norm_g_2,
        gla_norm_g_2, w_out_2, ln_g_2, ln_b_2,
    )


_drawn_inputs = setup_inputs


def setup_inputs(seed=0):
    import zlib

    import numpy as np

    out = dict(_drawn_inputs(seed))
    spreads = {}
    factors = {'m_conv_b': 3.524,
     'a_q_norm': 3.674,
     'a_q_head_norm': 4.794,
     'a_k_head_norm': 3.794,
     'c_v_norm': 7.804,
     'mix_out_norm': 2.816,
     'b_group': 8.0,
     'b_expert': 4.661,
     'gla_gate_b_2': 5.212,
     'dn_norm_g_2': 8.0,
     'gla_norm_g_2': 8.0}
    for name, (base, spread) in spreads.items():
        noise = np.random.default_rng([zlib.crc32(name.encode()), seed]).standard_normal(out[name].shape)
        drawn = base * np.exp(spread * noise) if base else spread * noise
        out[name] = jnp.asarray(drawn.astype(out[name].dtype))
    for name, factor in factors.items():
        out[name] = (out[name] * factor).astype(out[name].dtype)
    return out
```

```python
from contextlib import ExitStack

import numpy as np
import concourse.bass as bass
from concourse import mybir

ALU = mybir.AluOpType
ACT = mybir.ActivationFunctionType
AX = mybir.AxisListType
F32 = mybir.dt.float32
I32 = mybir.dt.int32

P = 128
S, D, L = 512, 1024, 2
T = S // P
KD = D // P
EPS = 1e-6
BIG = 1e30

MH, MD = 4, 96
MW = MH * MD
AH, NOPE, ROPE, AQ, AV = 6, 64, 32, 96, 64
AW = AH * AV
QR, KVR = 256, 128
CG, CD = 4, 64
CW = CG * CD
D_IN = 4 * MW + 2 * MH + QR + KVR + ROPE + 2 * CW
NAT0 = 2 * MW
NATW = D_IN - NAT0
NCH = 4
NCW = NATW // NCH
O_MV, O_MO, O_I, O_F = 0, MW, 2 * MW, 2 * MW + MH
O_CQ = O_F + MH
O_CKV = O_CQ + QR
O_KR = O_CKV + KVR
O_CU = O_KR + ROPE
O_CV = O_CU + CW
NG, EG = 4, 8
NE = NG * EG
FE = 256
RW = NG + NE

DH, DK = 4, 128
DW = DH * DK
GH, GK, GV = 4, 64, 128
GW = GH * GV
GKW = GH * GK
GR = 16
TAU = 16.0
D_IN2 = 3 * DW + DW + 2 * DH + 2 * GKW + 2 * GW + GR
ALPHA = (2.0 * L) ** 0.25
LEVELS = 7
O2_Z, O2_B, O2_A = 0, DW, DW + DH
O2_GV = DW + 2 * DH
O2_GZ = O2_GV + GW
O2_GR = O2_GZ + GW
NATW2 = O2_GR + GR
NCW2 = NATW2 // 4

PC = {}
PB = {}
PC2 = {}
PB2 = {}


def pack_offsets(table, items):
    at = 0
    for name, n in items:
        table[name] = at
        at += n
    return at


PCN = pack_offsets(PC, [("attn", KD), ("ffn", KD), ("mix", KD), ("qg", 2), ("kvg", 1), ("cb", CG),
                        ("cw", 8 * 4), ("cbias", 8), ("bi", 1), ("bf", 1)])
PBN = pack_offsets(PB, [("qh", AQ), ("kh", AQ), ("cv", CW), ("bg", NG), ("be", NE)])
PC2N = pack_offsets(PC2, [("cw", 12 * 4), ("dng", 1), ("glag", 1), ("gb", 2)])
PB2N = pack_offsets(PB2, [("lng", D), ("lnb", D), ("alog", DH), ("dtb", DH)])

CN = {}
CNN = pack_offsets(CN, [("ident", P), ("upper", P), ("neg", P), ("low", P), ("w4", NG), ("w32", NE),
                        ("freq", ROPE // 2), ("sel", MH * P), ("lvl", LEVELS * P), ("lvlt", LEVELS * P)])


def constants():
    c = np.zeros((P, CNN), np.float32)
    i, j = np.arange(P)[:, None], np.arange(P)[None, :]
    c[:, CN["ident"]:CN["ident"] + P] = i == j
    c[:, CN["upper"]:CN["upper"] + P] = i <= j
    c[:, CN["neg"]:CN["neg"] + P] = np.where(j <= i, 0.0, -BIG)
    c[:, CN["low"]:CN["low"] + P] = j < i
    c[:, CN["w4"]:CN["w4"] + NG] = NG - np.arange(NG)
    c[:, CN["w32"]:CN["w32"] + NE] = NE - np.arange(NE)
    half = np.arange(0, ROPE, 2, dtype=np.float32) / np.float32(ROPE)
    c[:, CN["freq"]:CN["freq"] + ROPE // 2] = np.float32(1.0) / (np.float32(10000.0) ** half)
    for h in range(MH):
        c[h, CN["sel"] + h * P:CN["sel"] + (h + 1) * P] = 1.0
    for n in range(LEVELS):
        b = 1 << n
        m = ((i // (2 * b)) == (j // (2 * b))) & ((i // b) % 2 == 1) & ((j // b) % 2 == 0)
        c[:, CN["lvl"] + n * P:CN["lvl"] + (n + 1) * P] = m
        c[:, CN["lvlt"] + n * P:CN["lvlt"] + (n + 1) * P] = m.T
    return c


def bank_plan(uses):
    first, at = {}, 0
    for name, n in uses:
        first[name] = at
        at += n
    per = [len(range(b, at, 8)) for b in range(8)]
    return first, per


def att(n, step):
    return "heads", (n // T) * (2 + 3 * T) + 2 + 3 * (n % T) + step


def turned(h, c):
    return "heads", h * (2 + 3 * T) + c


PLAN1, BANK1 = bank_plan([
    ("xT", KD), ("qk", 8), ("nat", NCH * T), ("grow", 2), ("gcol", 1), ("cT", 3), ("uq", 2 * T),
    ("ukv", 2 * T), ("wsT", 1), ("csg", 2)]
    + [(f"m{k}", 6) for k in range(MH)]
    + [("heads", AH * (2 + 3 * T))]
    + [("yT", KD), ("wo", 2 * T), ("fT", KD), ("route", 1)])

TILES2 = []
for t_ in range(T):
    TILES2 += [(f"{n}{t_}", 1) for n in ("gb", "kk", "qk", "lt")]
    TILES2 += [(f"lv{t_}", 3 * (LEVELS - 1) - 1), (f"u{t_}", 1), (f"wT{t_}", 1)]
    TILES2 += [(f"ws{t_}", 1)] * (t_ > 0) + [(f"o{t_}", 1)] + [(f"sk{t_}", 1)] * (t_ < T - 1)
GLA2 = []
for t_ in range(T):
    GLA2 += [(f"ga{t_}", 2), (f"go{t_}", 1)] + [(f"gs{t_}", 1)] * (t_ < T - 1)

PLAN2, BANK2 = bank_plan(
    [("xT", KD), ("T", 16), ("nat", 16), ("l2", 8), ("vn", T), ("gc", 1), ("kn", T)] + TILES2
    + [("grT", 1), ("gl", 2), ("kd", 2)] + GLA2 + [("yT", KD), ("wo", 2 * T)])

PER2 = {
    "prm": 48, "w_in0": 64, "w_in1": 48, "w_in2": 48, "tanh": 12, "beta_tanh": 1, "sq": 8, "l2r": 8, "g_e": 1,
    "g_ln": 1, "g_exp": 1, "eg": 4, "decay": 4, "gg_e": 1, "gg_ln": 1, "e_last": 1, "e_start": 1, "e_own": 1,
    "e_ownk": 1, "e_cross": 1, "z_tanh": 1, "ln_sq": 4, "ltm": 24, "rs_y": 1, "ln_rs": 4, "conv": 12, "silu": 12,
    "beta": 1, "g_abs": 1, "l2n": 8, "gcum_in": 1, "gcol": 1, "g_rep": 4, "d_arg": 4, "lm": 4, "inv": 24, "kb": 4,
    "vnew": 4, "state": 3, "tile": 4, "gg_abs": 1, "x_last": 1, "kd": 1, "x_own": 1, "x_cross": 1, "gla_in": 1,
    "gstate": 3, "ss_y": 1, "y": 1, "ln_mean": 4, "ln_done": 4,
}
PER1 = {
    "const": 16, "x_in": 32, "prm": 32, "w_in0": 48, "w_in1": 48, "w_in2": 32, "w_small": 64, "trig": 0,
    "ss_x": 1, "qk_tanh": 8, "gate_ln": 1, "ss_c": 1, "gate_em": 1, "mo_tanh": 1, "gelu_tanh": 1, "wsT_raw": 1,
    "m_e": 12, "ss_f": 1, "r_exp": 1, "zero": 0, "rs_x": 1, "vaug": 1, "rs_c": 1, "gelu_arg": 1, "rs_v": 1,
    "k_rope": 1, "rs_q": 1, "rs_k": 1, "rs_y": 1, "rs_f": 1, "angles": 0, "xn": 4, "qk_conv": 8, "qk_silu": 8,
    "gate_abs": 1, "gate_mx": 1, "cqn": 8, "ss_v": 1, "cvn": 1, "ss_q": 1, "ss_k": 1, "qk_rope": 2, "m_w": 16,
    "m_h": 4, "a_max": 24, "ss_y": 1, "y_norm": 1, "fn": 4, "r_shift": 1, "routed": 1, "x_moe": 1,
}


class Signals:

    def __init__(self, nc, ctx, prefix, per):
        self.nc, self.ctx, self.prefix, self.per = nc, ctx, prefix, per
        self.sems = {}
        self.counted = {}

    def sem(self, name):
        if name not in self.sems:
            self.sems[name] = self.ctx.enter_context(self.nc.semaphore(self.prefix + name))
        return self.sems[name]

    def did(self, name, n=1):
        self.counted[name] = self.counted.get(name, 0) + n
        return self.sem(name), n

    def after(self, layer, name, n):
        return self.sem(name), layer * self.per.get(name, 0) + n


class Banks:

    def __init__(self, nc, ctx, prefix, sg, plan, per):
        self.psum = [ctx.enter_context(nc.psum_tensor(f"{prefix}bank{b}", [P, 512], F32)) for b in range(8)]
        self.sg, self.plan, self.per = sg, plan, per

    def turn(self, layer, stage, i):
        n = self.plan[stage] + i
        return n % 8, layer * self.per[n % 8] + n // 8

    def filled(self, layer, stage, i=0):
        b, before = self.turn(layer, stage, i)
        return self.sg.sem(f"bank_full{b}"), before + 1

    def emptied(self, layer, stage, i=0):
        b, before = self.turn(layer, stage, i)
        return self.sg.sem(f"bank_free{b}"), before + 1

    def vacant(self, layer, stage, i=0):
        b, before = self.turn(layer, stage, i)
        return self.sg.sem(f"bank_free{b}"), before

    def writer(self, layer, stage, i=0):
        b, _ = self.turn(layer, stage, i)
        return self.psum[b], (self.sg.sem(f"bank_full{b}"), 1)

    def reader(self, layer, stage, i=0):
        b, _ = self.turn(layer, stage, i)
        return self.psum[b], (self.sg.sem(f"bank_free{b}"), 1)


def block_one(nc, A, x):
    ctx = ExitStack()
    with ctx:
        def sb(name, shape, dt=F32):
            return ctx.enter_context(nc.sbuf_tensor("b1_" + name, shape, dt))

        cn = sb("cn", [P, CN["lvl"]])
        prm = sb("prm", [P, PCN])
        prb = sb("prb", [P, PBN])
        actT = sb("actT", [P, KD, S])
        nat = sb("nat", [P, T, D])
        proj = sb("proj", [P, T, NATW])
        ring = [sb(f"ring{n}", [P, KD * 512]) for n in range(3)]
        qkc = sb("qkc", [MD, 8, S])
        work = sb("work", [P, 2, T, S])
        ebuf = sb("ebuf", [P, 2, S])
        vaug = sb("vaug", [P, T, MH, MD + 1])
        qa = sb("qa", [P, T, AH, AQ])
        ka = sb("ka", [P, T, AH, AQ])
        va = sb("va", [P, T, AH, AV])
        w_uq = sb("w_uq", [P, 2, AH * AQ])
        w_ukv = sb("w_ukv", [P, AH * (NOPE + AV)])
        w_s = sb("w_s", [P, CG, P])
        w_sT = sb("w_sT", [P, CG, P])
        w_r = sb("w_r", [P, KD, RW])
        zero = sb("zero", [MH, S])
        rg = sb("rg", [P, 8, T, NG])
        asum = sb("asum", [P, 3, AH * T])
        ss = sb("ss", [P, 136])
        ms = sb("ms", [P, 136])
        rs = sb("rs", [P, 136])
        half = sb("half", [P, 64])
        cols = sb("cols", [P, 2, T, MH])
        nd = sb("nd", [P, T, MD + 1])
        den = sb("den", [P, 2, T])
        trig = sb("trig", [P, 2, T, ROPE // 2])
        ang = sb("ang", [P, 4, T, ROPE // 2])
        posi = sb("posi", [P, T], I32)
        posf = sb("posf", [P, T])
        mx = sb("mx", [P, 8])
        lg = sb("lg", [P, T, RW])
        r1 = sb("r1", [P, 6, T, NE])
        rsm = sb("rsm", [P, 16, T])
        gate = sb("gate", [P, T, NE])

        headT = work[0:AQ, 0, :, :]
        prob = work[:, 1, 0:2, :]
        probT = work[:, 1, 2:4, :]
        cT = actT[:, 0:3, :]
        rows = actT[0:MH, 3:8, :]
        rp = work[:, :, :, :].rearrange("p a t s -> p (a t s)")[:, 0:4 * T * AH * ROPE // 2].rearrange(
            "p (n t h d) -> p n t h d", n=4, t=T, h=AH)
        th = ebuf
        hmoe = nat[:, :, :].rearrange("p t d -> p (t d)")[:, 0:2 * 2 * S].rearrange(
            "p (b f s) -> p b f s", b=2, f=2)
        ident = cn[:, CN["ident"]:CN["ident"] + P]
        upper = cn[:, CN["upper"]:CN["upper"] + P]
        neg = cn[:, CN["neg"]:CN["neg"] + P]
        w4 = cn[:, CN["w4"]:CN["w4"] + NG]
        w32 = cn[:, CN["w32"]:CN["w32"] + NE]
        freq = cn[:, CN["freq"]:CN["freq"] + ROPE // 2]

        sg = Signals(nc, ctx, "b1_", PER1)
        banks = Banks(nc, ctx, "b1_", sg, PLAN1, BANK1)
        psum = banks.psum
        did, after = sg.did, sg.after
        filled, emptied, vacant = banks.filled, banks.emptied, banks.vacant
        reader, writer = banks.reader, banks.writer

        def loaded(n):
            return f"w_in{n % 3}", 16 * (n // 3 + 1)

        last_use = [("qk", 3), ("qk", 7)] + [("nat", c * T + T - 1) for c in range(NCH)] + [("wo", 3), ("wo", 7)]

        block = ctx.enter_context(nc.Block())

        @block.sync
        def _(sp):
            sp.dma_start(cn[:, :], A["consts"][:, 0:CN["lvl"]]).then_inc(*did("const", 16))
            sp.dma_start(posi[:, :], A["positions"]).then_inc(*did("const", 16))
            for i in range(T):
                sp.dma_start(x[:, i, :], A["x"][i * P:(i + 1) * P, :]).then_inc(*did("x_in", 16))
            for l in range(L):
                if l:
                    sp.wait_ge(*emptied(l - 1, "route"))
                    sp.wait_ge(*after(l - 1, "routed", 1))
                sp.dma_start(prm[:, :], A["pc"][l]).then_inc(*did("prm", 16))
                sp.dma_start(prb[:, :], A["pb"][l]).then_inc(*did("prm", 16))
                win = A["w_in"][l].rearrange("(k p) n -> p k n", p=P)
                wout = A["w_out"][l].rearrange("(k p) n -> p k n", p=P)

                def load(n, src, width):
                    if n >= 3:
                        sp.wait_ge(*filled(l, *last_use[n - 3]))
                    elif l:
                        sp.wait_ge(sg.sem("moe_h_full"), 2 * NE * l)
                        sp.wait_ge(sg.sem("moe_y_full"), 8 * NE * l)
                    sp.dma_start(ring[n % 3][:, 0:KD * width].rearrange("p (k n) -> p k n", k=KD),
                                 src).then_inc(*did(f"w_in{n % 3}", 16))

                for c in range(2):
                    load(c, win[:, :, c * MW:(c + 1) * MW], MW)
                for c in range(NCH):
                    load(2 + c, win[:, :, NAT0 + c * NCW:NAT0 + (c + 1) * NCW], NCW)
                sp.dma_start(w_uq[:, :, :], A["a_w_uq"][l].rearrange("(k p) n -> p k n", p=P)).then_inc(*did("w_small", 16))
                sp.dma_start(w_ukv[:, :], A["a_w_ukv"][l]).then_inc(*did("w_small", 16))
                sp.dma_start(w_s[:, :, :], A["c_w_s"][l].rearrange("g t s -> t g s")).then_inc(*did("w_small", 16))
                sp.dma_start(w_r[:, :, :], A["w_r"][l].rearrange("(k p) n -> p k n", p=P)).then_inc(*did("w_small", 16))
                for c in range(2):
                    load(6 + c, wout[:, :, c * 512:(c + 1) * 512], 512)

                def w13(e, q):
                    w = ring[q][:, :].rearrange("p (c k n) -> p c k n", c=2, k=KD)
                    for c, name in enumerate(("w1", "w3")):
                        src = A[name].rearrange("m (k p) n -> m p k n", p=P)[bass.ds(e + l * NE, 1)]
                        sp.dma_start(w[:, c, :, :], src.rearrange("m p k n -> (m p) k n")).then_inc(*did(f"moe_w13_{q}", 16))

                def w2(e, q):
                    w = ring[2][:, q * 2048:(q + 1) * 2048].rearrange("p (f n) -> p f n", f=2)
                    src = A["w2"].rearrange("m (f p) n -> m p f n", p=P)[bass.ds(e + l * NE, 1)]
                    sp.dma_start(w, src.rearrange("m p f n -> (m p) f n")).then_inc(*did(f"moe_w2_{q}", 16))

                for n in range(5, 8):
                    sp.wait_ge(*filled(l, *last_use[n]))
                for q in range(2):
                    w13(q, q)
                for q in range(2):
                    w2(q, q)
                with sp.Fori(1, NE // 2) as pair:
                    e = 2 * pair
                    for q in range(2):
                        sp.wait_ge(sg.sem("moe_h_full"), 2 * (e + (l * NE + q - 1)))
                        w13(e + q, q)
                    for q in range(2):
                        sp.wait_ge(sg.sem("moe_y_full"), 8 * (e + (l * NE + q - 1)))
                        w2(e + q, q)

        @block.tensor
        def _(pe):
            def turn(l, stage, src):
                for k in range(KD):
                    pe.wait_ge(*vacant(l, stage, k))
                    bank, full = writer(l, stage, k)
                    for i in range(T):
                        ins = pe.transpose(bank[:, i * P:(i + 1) * P], src[:, i, k * P:(k + 1) * P], ident)
                    ins.then_inc(*full)

            pe.wait_ge(sg.sem("const"), 32)
            for l in range(L):
                pe.wait_ge(*after(l, "xn", T))
                turn(l, "xT", nat)
                for k in range(KD):
                    pe.wait_ge(*emptied(l, "xT", k))
                for c in range(8):
                    if c % 4 == 0:
                        pe.wait_ge(*after(l, *loaded(c // 4)))
                    w = ring[c // 4][:, 0:KD * MW].rearrange("p (k n) -> p k n", k=KD)
                    pe.wait_ge(*vacant(l, "qk", c))
                    bank, full = writer(l, "qk", c)
                    for k in range(KD):
                        ins = pe.matmul(bank[0:MD, :], w[:, k, (c % 4) * MD:(c % 4 + 1) * MD], actT[:, k, :],
                                        start=k == 0, stop=k == KD - 1)
                    ins.then_inc(*full)
                for c in range(NCH):
                    pe.wait_ge(*after(l, *loaded(2 + c)))
                    w = ring[(2 + c) % 3][:, 0:KD * NCW].rearrange("p (k n) -> p k n", k=KD)
                    for i in range(T):
                        pe.wait_ge(*vacant(l, "nat", c * T + i))
                        bank, full = writer(l, "nat", c * T + i)
                        for k in range(KD):
                            ins = pe.matmul(bank[:, 0:NCW], actT[:, k, i * P:(i + 1) * P], w[:, k, :],
                                            start=k == 0, stop=k == KD - 1)
                        ins.then_inc(*full)
                for n in range(NCH * T):
                    pe.wait_ge(*emptied(l, "nat", n))
                for g, off in enumerate((O_I, O_F)):
                    pe.wait_ge(*vacant(l, "grow", g))
                    bank, full = writer(l, "grow", g)
                    for i in range(T):
                        ins = pe.transpose(bank[0:MH, i * P:(i + 1) * P], proj[:, i, off:off + MH], ident)
                    ins.then_inc(*full)
                pe.wait_ge(*after(l, "gate_mx", 1))
                pe.wait_ge(*after(l, "gate_em", 1))
                pe.wait_ge(*vacant(l, "gcol"))
                bank, full = writer(l, "gcol")
                for g, r in enumerate((0, 4)):
                    for i in range(T):
                        ins = pe.transpose(bank[:, (g * T + i) * MH:(g * T + i + 1) * MH],
                                           rows[:, r, i * P:(i + 1) * P], ident[0:MH, 0:MH])
                ins.then_inc(*full)
                pe.wait_ge(*after(l, "cqn", 2 * T))
                for k in range(3):
                    pe.wait_ge(*vacant(l, "cT", k))
                    bank, full = writer(l, "cT", k)
                    for i in range(T):
                        off = O_CQ + k * P
                        ins = pe.transpose(bank[:, i * P:(i + 1) * P], proj[:, i, off:off + P], ident)
                    ins.then_inc(*full)
                pe.wait_ge(*after(l, "w_small", 64))
                for k in range(3):
                    pe.wait_ge(*emptied(l, "cT", k))
                for i in range(T):
                    for c in range(2):
                        pe.wait_ge(*vacant(l, "uq", 2 * i + c))
                        bank, full = writer(l, "uq", 2 * i + c)
                        for k in range(2):
                            ins = pe.matmul(bank[:, 0:288], cT[:, k, i * P:(i + 1) * P],
                                            w_uq[:, k, c * 288:(c + 1) * 288], start=k == 0, stop=k == 1)
                        ins.then_inc(*full)
                for i in range(T):
                    for c in range(2):
                        pe.wait_ge(*vacant(l, "ukv", 2 * i + c))
                        bank, full = writer(l, "ukv", 2 * i + c)
                        pe.matmul(bank[:, 0:384], cT[:, 2, i * P:(i + 1) * P],
                                  w_ukv[:, c * 384:(c + 1) * 384], start=True, stop=True).then_inc(*full)
                pe.wait_ge(*vacant(l, "wsT"))
                bank, full = writer(l, "wsT")
                for g in range(CG):
                    ins = pe.transpose(bank[:, g * P:(g + 1) * P], w_s[:, g, :], ident)
                ins.then_inc(*full)
                pe.wait_ge(*emptied(l, "wsT"))
                pe.wait_ge(*after(l, "cvn", 1))
                for g2 in range(2):
                    pe.wait_ge(*vacant(l, "csg", g2))
                    bank, full = writer(l, "csg", g2)
                    for g in range(2):
                        o = O_CV + (2 * g2 + g) * CD
                        ins = pe.matmul(bank[:, g * T * CD:(g + 1) * T * CD].rearrange("p (t d) -> p t d", t=T),
                                        w_sT[:, 2 * g2 + g, :], proj[:, :, o:o + CD], start=True, stop=True)
                    ins.then_inc(*full)
                pe.wait_ge(*after(l, "qk_silu", 8))
                pe.wait_ge(*after(l, "vaug", 1))
                def m_scores(h):
                    pe.wait_ge(*vacant(l, f"m{h}", 0))
                    bank, full = writer(l, f"m{h}", 0)
                    pe.matmul(bank[:, :], cn[0:MH, CN["sel"] + h * P:CN["sel"] + (h + 1) * P], rows[:, 3, :],
                              start=True, stop=True).then_inc(*full)
                    for j in range(T):
                        pe.wait_ge(*vacant(l, f"m{h}", 1 + j))
                        bank, full = writer(l, f"m{h}", 1 + j)
                        pe.matmul(bank[:, j * P:], qkc[:, 4 + h, j * P:(j + 1) * P], qkc[:, h, j * P:],
                                  start=True, stop=True).then_inc(*full)

                def m_out(h):
                    pe.wait_ge(*after(l, "m_w", T * (h + 1)))
                    pe.wait_ge(*vacant(l, f"m{h}", 5))
                    bank, full = writer(l, f"m{h}", 5)
                    for i in range(T):
                        for j in range(i + 1):
                            ins = pe.matmul(bank[:, i * (MD + 1):(i + 1) * (MD + 1)],
                                            work[:, h % 2, j, i * P:(i + 1) * P], vaug[:, j, h, :],
                                            start=j == 0, stop=j == i)
                    ins.then_inc(*full)

                for h in range(MH):
                    m_scores(h)
                    m_out(h)
                pe.wait_ge(*after(l, "qk_rope", 2))

                def heads(h):
                    for c, src in enumerate((qa, ka)):
                        pe.wait_ge(*vacant(l, *turned(h, c)))
                        bank, full = writer(l, *turned(h, c))
                        for i in range(T):
                            ins = pe.transpose(bank[0:AQ, i * P:(i + 1) * P], src[:, i, h, :], ident)
                        ins.then_inc(*full)

                def scores(n):
                    h, i = divmod(n, T)
                    for c in range(2):
                        pe.wait_ge(*emptied(l, *turned(h, c)))
                    pe.wait_ge(*vacant(l, *att(n, 0)))
                    bank, full = writer(l, *att(n, 0))
                    pe.matmul(bank[:, 0:(i + 1) * P], headT[:, 2 * (h % 2), i * P:(i + 1) * P],
                              headT[:, 2 * (h % 2) + 1, 0:(i + 1) * P], start=True, stop=True).then_inc(*full)

                def turn_probs(n):
                    i = n % T
                    pe.wait_ge(*emptied(l, *att(n, 0)))
                    pe.wait_ge(*vacant(l, *att(n, 1)))
                    bank, full = writer(l, *att(n, 1))
                    for j in range(i + 1):
                        ins = pe.transpose(bank[:, j * P:(j + 1) * P], prob[:, n % 2, j * P:(j + 1) * P], ident)
                    ins.then_inc(*full)

                def values(n):
                    h, i = divmod(n, T)
                    pe.wait_ge(*emptied(l, *att(n, 1)))
                    pe.wait_ge(*vacant(l, *att(n, 2)))
                    bank, full = writer(l, *att(n, 2))
                    for j in range(i + 1):
                        ins = pe.matmul(bank[:, 0:AV], probT[:, n % 2, j * P:(j + 1) * P], va[:, j, h, :],
                                        start=j == 0, stop=j == i)
                    ins.then_inc(*full)

                for h in range(AH):
                    heads(h)
                    for i in range(T):
                        n = h * T + i
                        scores(n)
                        turn_probs(n)
                        values(n)
                pe.wait_ge(*after(l, "y_norm", 1))
                turn(l, "yT", nat)
                for k in range(KD):
                    pe.wait_ge(*emptied(l, "yT", k))
                for c in range(2):
                    pe.wait_ge(*after(l, *loaded(6 + c)))
                    w = ring[(6 + c) % 3][:, :].rearrange("p (k n) -> p k n", k=KD)
                    for i in range(T):
                        pe.wait_ge(*vacant(l, "wo", c * T + i))
                        bank, full = writer(l, "wo", c * T + i)
                        for k in range(KD):
                            ins = pe.matmul(bank[:, :], actT[:, k, i * P:(i + 1) * P], w[:, k, :],
                                            start=k == 0, stop=k == KD - 1)
                        ins.then_inc(*full)
                pe.wait_ge(*after(l, "fn", T))
                turn(l, "fT", nat)
                for k in range(KD):
                    pe.wait_ge(*emptied(l, "fT", k))
                pe.wait_ge(*vacant(l, "route"))
                bank, full = writer(l, "route")
                for i in range(T):
                    for k in range(KD):
                        ins = pe.matmul(bank[:, i * RW:(i + 1) * RW], actT[:, k, i * P:(i + 1) * P], w_r[:, k, :],
                                        start=k == 0, stop=k == KD - 1)
                ins.then_inc(*full)
                for b in range(8):
                    pe.wait_ge(sg.sem(f"bank_free{b}"), (l + 1) * BANK1[b])
                with pe.Fori(0, NE // 2) as pair:
                    e = 2 * pair
                    for q in range(2):
                        pe.wait_ge(sg.sem(f"moe_w13_{q}"), 16 * (e + (l * NE + 2)))
                        w = ring[q][:, :].rearrange("p (c k n) -> p c k n", c=2, k=KD)
                        for f in range(2):
                            pe.wait_ge(sg.sem(f"moe_h_free{f}"), e + (l * NE + q + 1))
                            for c in range(2):
                                for k in range(KD):
                                    ins = pe.matmul(psum[2 * f + c][:, :], w[:, c, k, f * P:(f + 1) * P],
                                                    actT[:, k, :], start=k == 0, stop=k == KD - 1)
                            ins.then_inc(*did("moe_h_full"))
                    for q in range(2):
                        pe.wait_ge(sg.sem(f"moe_w2_{q}"), 8 * (e + (l * NE + 2)))
                        for f in range(2):
                            pe.wait_ge(sg.sem(f"moe_h_free{f}"), e + (l * NE + q + 2))
                        w = ring[2][:, q * 2048:(q + 1) * 2048].rearrange("p (f n) -> p f n", f=2)
                        for n in range(2 * T):
                            pe.wait_ge(sg.sem("moe_y_free"), 8 * e + (8 * (l * NE + q) + n + 1))
                            for f in range(2):
                                ins = pe.matmul(psum[4 + n % 4][:, :],
                                                hmoe[:, q, f, (n // 2) * P:(n // 2 + 1) * P],
                                                w[:, f, (n % 2) * 512:(n % 2 + 1) * 512],
                                                start=f == 0, stop=f == 1)
                            ins.then_inc(*did("moe_y_full"))

        R_X, R_C, R_V, R_Q, R_K, R_Y, R_F = 0, 4, 12, 28, 52, 76, 132

        @block.scalar
        def _(act):
            chain = [0]

            def link(ins):
                chain[0] += 1
                ins.then_inc(sg.sem("act_step"), 1)
                act.wait_ge(sg.sem("act_step"), chain[0])

            def squares(src, i, n, at=0):
                return act.activation(nat[:, i, at:at + src.shape[1]], src, ACT.Square, accum_out=ss[:, n:n + 1])

            def gains(l, stage, offset):
                for k in range(0, KD, 2):
                    act.wait_ge(*filled(l, stage, k))
                    bank, free = reader(l, stage, k)
                    act.activation(actT[:, k, :], bank[:, :], ACT.Identity,
                                   scale=prm[:, offset + k:offset + k + 1]).then_inc(*free)

            act.wait_ge(*after(0, "angles", 1))
            act.activation(trig[:, 0, :, :], ang[:, 3, :, :], ACT.Sin)
            act.activation(trig[:, 1, :, :], ang[:, 1, :, :], ACT.Sin).then_inc(*did("trig"))
            act.wait_ge(sg.sem("x_in"), 16 * T)
            for l in range(L):
                act.wait_ge(*after(l, "prm", 32))
                if l:
                    act.wait_ge(*after(l - 1, "x_moe", 1))
                for i in range(T):
                    ins = squares(x[:, i, :], i, R_X + i)
                ins.then_inc(*did("ss_x"))
                gains(l, "xT", PC["attn"])
                for c in range(8):
                    act.wait_ge(*after(l, "qk_conv", c + 1))
                    if c >= 2:
                        act.wait_ge(*after(l, "qk_silu", c - 1))
                    act.activation(ebuf[0:MD, c % 2, :], qkc[:, c, :], ACT.Tanh, scale=0.5).then_inc(*did("qk_tanh"))
                for n in range(NCH * T):
                    c, i = divmod(n, T)
                    act.wait_ge(*filled(l, "nat", n))
                    bank, free = reader(l, "nat", n)
                    act.activation(proj[:, i, c * NCW:(c + 1) * NCW], bank[:, 0:NCW], ACT.Copy).then_inc(*free)
                for n in range(NCH * T):
                    act.wait_ge(*emptied(l, "nat", n))
                act.wait_ge(*after(l, "gate_abs", 1))
                link(act.activation(rows[:, 4, :], rows[:, 4, :], ACT.Exp))
                act.activation(rows[:, 4, :], rows[:, 4, :], ACT.Ln, bias=1.0).then_inc(*did("gate_ln"))
                for i in range(T):
                    squares(proj[:, i, O_CQ:O_CQ + QR], i, R_C + 2 * i)
                    ins = squares(proj[:, i, O_CKV:O_CKV + KVR], i, R_C + 2 * i + 1, QR)
                ins.then_inc(*did("ss_c"))
                act.wait_ge(*after(l, "gate_mx", 1))
                act.activation(rows[:, 4, :], rows[:, 4, :], ACT.Exp).then_inc(*did("gate_em"))
                act.activation(proj[:, :, O_MO:O_MO + MW], proj[:, :, O_MO:O_MO + MW], ACT.Tanh,
                               scale=0.5).then_inc(*did("mo_tanh"))
                act.wait_ge(*after(l, "gelu_arg", 1))
                act.activation(work[:, 0, :, :], work[:, 0, :, :], ACT.Tanh,
                               scale=float(np.sqrt(2 / np.pi))).then_inc(*did("gelu_tanh"))
                for k in range(3):
                    act.wait_ge(*filled(l, "cT", k))
                    bank, free = reader(l, "cT", k)
                    act.activation(cT[:, k, :], bank[:, :], ACT.Identity,
                                   scale=prm[:, PC["qg"] + k:PC["qg"] + k + 1]).then_inc(*free)
                for n in range(2 * T):
                    i, c = divmod(n, 2)
                    act.wait_ge(*filled(l, "uq", n))
                    bank, free = reader(l, "uq", n)
                    act.activation(qa[:, i, 3 * c:3 * c + 3, :],
                                   bank[:, 0:288].rearrange("p (h d) -> p h d", h=3), ACT.Copy).then_inc(*free)
                for n in range(2 * T):
                    i, c = divmod(n, 2)
                    act.wait_ge(*filled(l, "ukv", n))
                    bank, free = reader(l, "ukv", n)
                    kv = bank[:, 0:384].rearrange("p (h d) -> p h d", h=3)
                    act.activation(ka[:, i, 3 * c:3 * c + 3, 0:NOPE], kv[:, :, 0:NOPE], ACT.Copy)
                    act.activation(va[:, i, 3 * c:3 * c + 3, :], kv[:, :, NOPE:], ACT.Copy).then_inc(*free)
                act.wait_ge(*filled(l, "wsT"))
                bank, free = reader(l, "wsT")
                act.activation(w_sT[:, :, :], bank[:, :].rearrange("p (g s) -> p g s", g=CG), ACT.Copy).then_inc(*did("wsT_raw"))
                act.wait_ge(*emptied(l, "gcol"))
                for h in range(MH):
                    act.wait_ge(*filled(l, f"m{h}", 0))
                    bank, free = reader(l, f"m{h}", 0)
                    for j in range(T):
                        n = h * T + j
                        if n >= 2:
                            act.wait_ge(*after(l, "m_w", n - 1))
                        ins = act.activation(ebuf[:, n % 2, j * P:], bank[:, j * P:], ACT.Exp,
                                             bias=cols[:, 0, j, h:h + 1])
                        if j < T - 1:
                            ins.then_inc(*did("m_e"))
                    ins.then_inc(*free)
                for h in range(AH):
                    if h == 0:
                        act.wait_ge(*after(l, "m_h", MH))
                    if h >= 2:
                        act.wait_ge(*filled(l, *att((h - 1) * T - 1, 0)))
                    act.wait_ge(*filled(l, *turned(h, 0)))
                    bank, free = reader(l, *turned(h, 0))
                    act.activation(headT[:, 2 * (h % 2), :], bank[0:AQ, :], ACT.Copy).then_inc(*free)
                    for i in range(T):
                        n = h * T + i
                        act.wait_ge(*after(l, "a_max", n + 1))
                        if n >= 2:
                            act.wait_ge(*filled(l, *att(n - 2, 1)))
                        bank, free = reader(l, *att(n, 0))
                        act.activation(prob[:, n % 2, 0:(i + 1) * P], bank[:, 0:(i + 1) * P], ACT.Exp,
                                       bias=asum[:, 0, n:n + 1], scale=AQ ** -0.5,
                                       accum_out=asum[:, 1, n:n + 1]).then_inc(*free)
                gains(l, "yT", PC["mix"])
                for n in range(2 * T):
                    act.wait_ge(*emptied(l, "wo", n))
                for i in range(T):
                    ins = squares(x[:, i, :], i, R_F + i)
                ins.then_inc(*did("ss_f"))
                gains(l, "fT", PC["ffn"])
                act.wait_ge(*after(l, "r_shift", 1))
                act.activation(rg[:, 4, :, :], rg[:, 4, :, :], ACT.Exp)
                act.activation(r1[:, 4, :, :], r1[:, 4, :, :], ACT.Exp).then_inc(*did("r_exp"))
                with act.Fori(0, NE // 2) as pair:
                    e = 2 * pair
                    for q in range(2):
                        for f in range(2):
                            act.wait_ge(sg.sem("moe_h_full"), 2 * e + (2 * (l * NE + q) + f + 1))
                            act.activation(th[:, f, :], psum[2 * f][:, :], ACT.Tanh, scale=0.5).then_inc(*did("moe_tanh"))

        @block.gpsimd
        def _(pool):
            chain = [0]

            def link(ins):
                chain[0] += 1
                ins.then_inc(sg.sem("pool_step"), 1)
                pool.wait_ge(sg.sem("pool_step"), chain[0])

            def rsqrt(at, n, scale, eps=EPS):
                link(pool.tensor_scalar(ms[:, at:at + n], ss[:, at:at + n], scale, eps, ALU.mult, ALU.add))
                return pool.tensor_tensor(rs[:, at:at + n], ms[:, at:at + n], half[:, 0:n], ALU.pow)

            pool.memset(zero[:, :], 0.0).then_inc(*did("zero"))
            link(pool.memset(half[:, :], -0.5))
            link(pool.memset(vaug[:, :, :, MD:MD + 1], 1.0))
            for l in range(L):
                pool.wait_ge(*after(l, "ss_x", 1))
                rsqrt(R_X, T, 1.0 / D).then_inc(*did("rs_x"))
                for n in range(NCH * T):
                    pool.wait_ge(*emptied(l, "nat", n))
                if l:
                    pool.wait_ge(*after(l - 1, "m_h", MH))
                pool.tensor_copy(vaug[:, :, :, 0:MD],
                                 proj[:, :, O_MV:O_MV + MW].rearrange("p t (h d) -> p t h d", h=MH)).then_inc(*did("vaug"))
                pool.wait_ge(*after(l, "ss_c", 1))
                c2 = ms[:, R_C:R_C + 8].rearrange("p (t c) -> p t c", c=2)
                s2 = ss[:, R_C:R_C + 8].rearrange("p (t c) -> p t c", c=2)
                pool.tensor_scalar(c2[:, :, 0], s2[:, :, 0], 1.0 / QR, EPS, ALU.mult, ALU.add)
                link(pool.tensor_scalar(c2[:, :, 1], s2[:, :, 1], 1.0 / KVR, EPS, ALU.mult, ALU.add))
                pool.tensor_tensor(rs[:, R_C:R_C + 8], ms[:, R_C:R_C + 8], half[:, 0:8], ALU.pow).then_inc(*did("rs_c"))
                uv = proj[:, :, O_CU:O_CU + 2 * CW]
                if l:
                    pool.wait_ge(*after(l - 1, "y_norm", 1))
                link(pool.tensor_tensor(work[:, 0, :, :], uv, uv, ALU.mult))
                link(pool.tensor_scalar(work[:, 0, :, :], work[:, 0, :, :], 0.044715, 1.0, ALU.mult, ALU.add))
                pool.tensor_tensor(work[:, 0, :, :], work[:, 0, :, :], uv, ALU.mult).then_inc(*did("gelu_arg"))
                pool.wait_ge(*after(l, "ss_v", 1))
                rsqrt(R_V, T * CG, 1.0 / (4 * CD)).then_inc(*did("rs_v"))
                kr = proj[:, :, O_KR:O_KR + ROPE].unsqueeze(2).to_broadcast([P, T, AH, ROPE])
                if l:
                    pool.wait_ge(*filled(l - 1, *turned(AH - 1, 1)))
                pool.tensor_copy(ka[:, :, :, NOPE:], kr).then_inc(*did("k_rope"))
                for name, at in (("q", R_Q), ("k", R_K)):
                    pool.wait_ge(*after(l, f"ss_{name}", 1))
                    rsqrt(at, T * AH, 1.0 / AQ).then_inc(*did(f"rs_{name}"))
                pool.wait_ge(*after(l, "ss_y", 1))
                for t0, n, d in ((R_Y, T * MH, MD), (R_Y + T * MH, T * (AH + CG), AV)):
                    link(pool.tensor_scalar(ms[:, t0:t0 + n], ss[:, t0:t0 + n], 1.0 / d, EPS, ALU.mult, ALU.add))
                pool.tensor_tensor(rs[:, R_Y:R_Y + 56], ms[:, R_Y:R_Y + 56], half[:, 0:56], ALU.pow).then_inc(*did("rs_y"))
                pool.wait_ge(*after(l, "ss_f", 1))
                rsqrt(R_F, T, 1.0 / D).then_inc(*did("rs_f"))

        @block.vector
        def _(dve):
            chain = [0]

            def link(ins):
                chain[0] += 1
                ins.then_inc(sg.sem("dve_step"), 1)
                dve.wait_ge(sg.sem("dve_step"), chain[0])

            def tt(out, a, b, op):
                return dve.tensor_tensor(out, a, b, op)

            def ts(out, a, s1, s2=None, op0=ALU.mult, op1=None):
                return dve.tensor_scalar(out, a, s1, s2, op0, op1) if op1 is not None else dve.tensor_scalar(out, a, s1, None, op0)

            def stt(out, a, s, b, op0, op1):
                return dve.scalar_tensor_tensor(out=out, in0=a, scalar=s, in1=b, op0=op0, op1=op1)

            def bc(ap, n):
                return ap.unsqueeze(len(ap.shape)).to_broadcast([*ap.shape, n])

            def gains(l, stage, offset):
                for k in range(1, KD, 2):
                    dve.wait_ge(*filled(l, stage, k))
                    bank, free = reader(l, stage, k)
                    ts(actT[:, k, :], bank[:, :], prm[:, offset + k:offset + k + 1]).then_inc(*free)

            def group_squares(dst, src, tmp):
                link(tt(tmp, src, src, ALU.mult))
                return dve.tensor_reduce(dst, tmp, AX.X, ALU.add)

            for q in range(2):
                dve.memset(mx[:, q:q + 1], 0.0).then_inc(*did(f"moe_h_free{q}"))
            dve.memset(mx[:, 2:3], 0.0).then_inc(*did("moe_y_free", 4))
            dve.wait_ge(*after(0, "const", 32))
            link(dve.tensor_copy(posf[:, :], posi[:, :]))
            for i in range(T):
                link(ts(ang[:, 0, i, :], freq, posf[:, i:i + 1]))
            magic = 12582912.0
            link(ts(ang[:, 2, :, :], ang[:, 0, :, :], float(1 / (2 * np.pi)), magic, ALU.mult, ALU.add))
            link(ts(ang[:, 2, :, :], ang[:, 2, :, :], magic, None, ALU.subtract))
            for k, c in enumerate((6.28125, 0.0019350051879882812, 3.0199159819e-07)):
                link(stt(ang[:, 1, :, :], ang[:, 2, :, :], -c, ang[:, 0 if k == 0 else 1, :, :], ALU.mult, ALU.add))
            pi = 3.1415925
            link(ts(ang[:, 3, :, :], ang[:, 1, :, :], float(np.pi / 2), None, ALU.add))
            link(ts(ang[:, 2, :, :], ang[:, 3, :, :], pi, None, ALU.is_gt))
            link(stt(ang[:, 3, :, :], ang[:, 2, :, :], float(-2 * np.pi), ang[:, 3, :, :], ALU.mult, ALU.add))
            link(ts(ang[:, 1, :, :], ang[:, 1, :, :], pi, -pi, ALU.min, ALU.max))
            ts(ang[:, 3, :, :], ang[:, 3, :, :], pi, -pi, ALU.min, ALU.max).then_inc(*did("angles"))
            dve.wait_ge(sg.sem("x_in"), 16 * T)
            for l in range(L):
                dve.wait_ge(*after(l, "prm", 32))
                dve.wait_ge(*after(l, "rs_x", 1))
                for i in range(T):
                    ts(nat[:, i, :], x[:, i, :], rs[:, R_X + i:R_X + i + 1]).then_inc(*did("xn"))
                gains(l, "xT", PC["attn"])

                def silu(c):
                    dve.wait_ge(*after(l, "qk_tanh", c + 1))
                    stt(qkc[:, c, :], ebuf[0:MD, c % 2, :], 1.0, qkc[:, c, :], ALU.add, ALU.mult).then_inc(*did("qk_silu"))

                for c in range(8):
                    dve.wait_ge(*filled(l, "qk", c))
                    bank, free = reader(l, "qk", c)
                    w = PC["cw"] + 4 * c
                    link(ts(qkc[:, c, :], bank[0:MD, :], prm[0:MD, w + 3:w + 4],
                            prm[0:MD, PC["cbias"] + c:PC["cbias"] + c + 1], ALU.mult, ALU.add))
                    for d in range(1, 4):
                        ins = stt(qkc[:, c, d:], bank[0:MD, 0:S - d], prm[0:MD, w + 3 - d:w + 4 - d],
                                  qkc[:, c, d:], ALU.mult, ALU.add)
                        if d < 3:
                            link(ins)
                    link(ins)
                    dve.engine_nop().then_inc(*free)
                    dve.engine_nop().then_inc(*did("qk_conv"))
                    if c:
                        silu(c - 1)
                silu(7)
                dve.wait_ge(*filled(l, "grow", 0))
                bank, free = reader(l, "grow", 0)
                ts(rows[:, 0, :], bank[0:MH, :], prm[0:MH, PC["bi"]:PC["bi"] + 1], None, ALU.add).then_inc(*free)
                dve.wait_ge(*filled(l, "grow", 1))
                bank, free = reader(l, "grow", 1)
                ts(rows[:, 1, :], bank[0:MH, :], prm[0:MH, PC["bf"]:PC["bf"] + 1], None, ALU.add).then_inc(*free)
                dve.wait_ge(*emptied(l, "grow", 1))
                stt(rows[:, 4, :], rows[:, 1, :], -1.0, rows[:, 1, :], ALU.mult, ALU.min).then_inc(*did("gate_abs"))
                dve.wait_ge(*after(l, "gate_ln", 1))
                dve.wait_ge(*after(0, "zero", 1))
                link(stt(rows[:, 1, :], rows[:, 1, :], 0.0, rows[:, 4, :], ALU.min, ALU.subtract))
                link(dve.tensor_tensor_scan(rows[:, 2, :], rows[:, 1, :], zero[:, :], 0.0, ALU.add, ALU.add))
                link(tt(rows[:, 0, :], rows[:, 0, :], rows[:, 2, :], ALU.subtract))
                link(dve.tensor_tensor_scan(rows[:, 3, :], rows[:, 0, :], rows[:, 0, :], 0.0, ALU.max, ALU.max))
                link(ts(rows[:, 3, :], rows[:, 3, :], -1.0))
                tt(rows[:, 4, :], rows[:, 3, :], rows[:, 2, :], ALU.subtract).then_inc(*did("gate_mx"))
                dve.wait_ge(*after(l, "rs_c", 1))
                for i in range(T):
                    for c, (o, n) in enumerate(((O_CQ, QR), (O_CKV, KVR))):
                        ts(proj[:, i, o:o + n], proj[:, i, o:o + n],
                           rs[:, R_C + 2 * i + c:R_C + 2 * i + c + 1]).then_inc(*did("cqn"))
                dve.wait_ge(*filled(l, "gcol"))
                bank, free = reader(l, "gcol")
                dve.tensor_copy(cols[:, :, :, :].rearrange("p a t h -> p (a t h)"), bank[:, 0:2 * T * MH]).then_inc(*free)
                uv = proj[:, :, O_CU:O_CU + 2 * CW]
                dve.wait_ge(*after(l, "gelu_tanh", 1))
                link(stt(uv, work[:, 0, :, :], 1.0, uv, ALU.add, ALU.mult))
                vg = proj[:, :, O_CV:O_CV + CW].rearrange("p t (g d) -> p t g d", g=CG)
                r4 = lambda at, g: rs[:, at:at + T * g].rearrange("p (t g) -> p t g", t=T)
                s4 = lambda at, g: ss[:, at:at + T * g].rearrange("p (t g) -> p t g", t=T)
                group_squares(s4(R_V, CG), vg, work[:, 1, :, 0:CW].rearrange("p t (g d) -> p t g d", g=CG)).then_inc(*did("ss_v"))
                link(ts(proj[:, :, O_CU:O_CU + CW], proj[:, :, O_CU:O_CU + CW], 0.5))
                dve.wait_ge(*after(l, "rs_v", 1))
                for t in range(T):
                    link(stt(vg[:, t], vg[:, t], 0.5, bc(r4(R_V, CG)[:, t], CD), ALU.mult, ALU.mult))
                tt(proj[:, :, O_CV:O_CV + CW], proj[:, :, O_CV:O_CV + CW],
                   prb[:, PB["cv"]:PB["cv"] + CW].unsqueeze(1).to_broadcast([P, T, CW]), ALU.mult).then_inc(*did("cvn"))
                dve.wait_ge(*after(l, "wsT_raw", 1))
                dve.wait_ge(*filled(l, "wsT"))
                _, free = reader(l, "wsT")
                tt(w_sT[:, :, :], w_sT[:, :, :], upper.unsqueeze(1).to_broadcast([P, CG, P]), ALU.mult).then_inc(*free)
                for n in range(2 * T):
                    dve.wait_ge(*emptied(l, "uq", n))
                    dve.wait_ge(*emptied(l, "ukv", n))
                dve.wait_ge(*after(l, "k_rope", 1))
                dve.wait_ge(*after(0, "trig", 1))
                tmp = work[:, :, :, :].rearrange("p a t s -> p (a t s)")[:, 0:T * AH * AQ].rearrange(
                    "p (t h d) -> p t h d", t=T, h=AH)
                for name, at, arr in (("q", R_Q, qa), ("k", R_K, ka)):
                    link(group_squares(s4(at, AH), arr[:, :, :, :], tmp))
                    dve.engine_nop().then_inc(*did(f"ss_{name}"))
                for name, at, arr in (("q", R_Q, qa), ("k", R_K, ka)):
                    dve.wait_ge(*after(l, f"rs_{name}", 1))
                    flat = arr[:, :, :, :].rearrange("p t h d -> p (t h) d")
                    link(tt(flat, flat, bc(rs[:, at:at + T * AH], AQ), ALU.mult))
                    g = prb[:, PB[name + "h"]:PB[name + "h"] + AQ].unsqueeze(1).to_broadcast([P, T * AH, AQ])
                    link(tt(flat, flat, g, ALU.mult))
                    x1, x2 = arr[:, :, :, NOPE:NOPE + 16], arr[:, :, :, NOPE + 16:]
                    c, s = (trig[:, n, :, :].unsqueeze(2).to_broadcast([P, T, AH, ROPE // 2]) for n in range(2))
                    for t in range(T):
                        tt(rp[:, 0, t], x1[:, t], c[:, t], ALU.mult)
                        tt(rp[:, 1, t], x2[:, t], s[:, t], ALU.mult)
                        tt(rp[:, 2, t], x1[:, t], s[:, t], ALU.mult)
                        link(tt(rp[:, 3, t], x2[:, t], c[:, t], ALU.mult))
                    link(tt(x1, rp[:, 0], rp[:, 1], ALU.subtract))
                    tt(x2, rp[:, 2], rp[:, 3], ALU.add).then_inc(*did("qk_rope"))
                for g2 in range(2):
                    dve.wait_ge(*filled(l, "csg", g2))
                    bank, free = reader(l, "csg", g2)
                    for g in range(2):
                        gg = 2 * g2 + g
                        ins = stt(nat[:, :, MW + AW + gg * CD:MW + AW + (gg + 1) * CD],
                                  bank[:, g * T * CD:(g + 1) * T * CD].rearrange("p (t d) -> p t d", t=T),
                                  prm[:, PC["cb"] + gg:PC["cb"] + gg + 1],
                                  proj[:, :, O_CU + gg * CD:O_CU + (gg + 1) * CD], ALU.add, ALU.mult)
                    ins.then_inc(*free)
                def m_outputs(h):
                    dve.wait_ge(*filled(l, f"m{h}", 5))
                    bank, free = reader(l, f"m{h}", 5)
                    ts(nd[:, :, :], bank[:, 0:T * (MD + 1)].rearrange("p (t d) -> p t d", t=T),
                       MD ** -0.5 / 4).then_inc(*free)
                    dve.wait_ge(*emptied(l, f"m{h}", 5))
                    link(ts(den[:, 0, :], nd[:, :, MD], -1.0))
                    link(tt(den[:, 0, :], den[:, 0, :], nd[:, :, MD], ALU.max))
                    link(tt(den[:, 0, :], den[:, 0, :], cols[:, 1, :, h], ALU.max))
                    link(ts(den[:, 0, :], den[:, 0, :], 2.0))
                    link(dve.reciprocal(den[:, 1, :], den[:, 0, :]))
                    link(tt(nd[:, :, 0:MD], nd[:, :, 0:MD], bc(den[:, 1, :], MD), ALU.mult))
                    stt(nat[:, :, h * MD:(h + 1) * MD], proj[:, :, O_MO + h * MD:O_MO + (h + 1) * MD], 1.0,
                        nd[:, :, 0:MD], ALU.add, ALU.mult).then_inc(*did("m_h"))

                dve.wait_ge(*after(l, "mo_tanh", 1))
                for h in range(MH):
                    for j in range(T):
                        n = h * T + j
                        if j < T - 1:
                            dve.wait_ge(*after(l, "m_e", h * (T - 1) + j + 1))
                        else:
                            dve.wait_ge(*emptied(l, f"m{h}", 0))
                        dve.wait_ge(*filled(l, f"m{h}", 1 + j))
                        bank, free = reader(l, f"m{h}", 1 + j)
                        stt(work[:, h % 2, j, j * P:], ebuf[:, n % 2, j * P:], 1.0, bank[:, j * P:],
                            ALU.min, ALU.mult).then_inc(*free)
                        dve.wait_ge(*emptied(l, f"m{h}", 1 + j))
                        tt(work[:, h % 2, j, j * P:(j + 1) * P], work[:, h % 2, j, j * P:(j + 1) * P],
                           upper, ALU.mult).then_inc(*did("m_w"))
                    m_outputs(h)
                for h in range(AH):
                    if h >= 2:
                        dve.wait_ge(*filled(l, *att((h - 1) * T - 1, 0)))
                    dve.wait_ge(*filled(l, *turned(h, 1)))
                    bank, free = reader(l, *turned(h, 1))
                    dve.tensor_copy(headT[:, 2 * (h % 2) + 1, :], bank[0:AQ, :]).then_inc(*free)
                    for i in range(T):
                        n = h * T + i
                        dve.wait_ge(*filled(l, *att(n, 0)))
                        bank, _ = reader(l, *att(n, 0))
                        link(tt(bank[:, i * P:(i + 1) * P], bank[:, i * P:(i + 1) * P], neg, ALU.add))
                        link(dve.tensor_reduce(asum[:, 2, n:n + 1], bank[:, 0:(i + 1) * P], AX.X, ALU.max))
                        ts(asum[:, 0, n:n + 1], asum[:, 2, n:n + 1], -AQ ** -0.5).then_inc(*did("a_max"))
                        if n >= 2:
                            dve.wait_ge(*filled(l, *att(n - 2, 2)))
                        dve.wait_ge(*filled(l, *att(n, 1)))
                        bank, free = reader(l, *att(n, 1))
                        dve.tensor_copy(probT[:, n % 2, 0:(i + 1) * P], bank[:, 0:(i + 1) * P]).then_inc(*free)
                        link(dve.reciprocal(asum[:, 2, n:n + 1], asum[:, 1, n:n + 1]))
                        dve.wait_ge(*filled(l, *att(n, 2)))
                        bank, free = reader(l, *att(n, 2))
                        ts(nat[:, i, MW + h * AV:MW + (h + 1) * AV], bank[:, 0:AV], asum[:, 2, n:n + 1]).then_inc(*free)
                dve.wait_ge(*emptied(l, *att(AH * T - 1, 2)))
                dve.wait_ge(*after(l, "m_h", MH))
                ym = nat[:, :, 0:MW].rearrange("p t (g d) -> p t g d", g=MH)
                ya = nat[:, :, MW:].rearrange("p t (g d) -> p t g d", g=AH + CG)
                sq = actT[:, :, :].rearrange("p k s -> p (k s)")
                link(group_squares(s4(R_Y, MH), ym, sq[:, 0:T * MW].rearrange("p (t g d) -> p t g d", t=T, g=MH)))
                link(group_squares(s4(R_Y + T * MH, AH + CG), ya,
                                   sq[:, T * MW:].rearrange("p (t g d) -> p t g d", t=T, g=AH + CG)))
                dve.engine_nop().then_inc(*did("ss_y"))
                dve.wait_ge(*after(l, "rs_y", 1))
                for t in range(T):
                    link(tt(ym[:, t], ym[:, t], bc(r4(R_Y, MH)[:, t], MD), ALU.mult))
                    ins = tt(ya[:, t], ya[:, t], bc(r4(R_Y + T * MH, AH + CG)[:, t], AV), ALU.mult)
                    if t < T - 1:
                        link(ins)
                ins.then_inc(*did("y_norm"))
                gains(l, "yT", PC["mix"])
                for n in range(2 * T):
                    c, i = divmod(n, T)
                    dve.wait_ge(*filled(l, "wo", n))
                    bank, free = reader(l, "wo", n)
                    tt(x[:, i, c * 512:(c + 1) * 512], x[:, i, c * 512:(c + 1) * 512], bank[:, :], ALU.add).then_inc(*free)
                dve.wait_ge(*after(l, "rs_f", 1))
                for i in range(T):
                    ts(nat[:, i, :], x[:, i, :], rs[:, R_F + i:R_F + i + 1]).then_inc(*did("fn"))
                gains(l, "fT", PC["ffn"])
                dve.wait_ge(*filled(l, "route"))
                bank, free = reader(l, "route")
                dve.tensor_copy(lg[:, :, :], bank[:, 0:T * RW].rearrange("p (t n) -> p t n", t=T)).then_inc(*free)
                dve.wait_ge(*emptied(l, "route"))
                row = lambda ap, n: ap.unsqueeze(1).to_broadcast([P, T, n])

                def first_max(src, rank, n, eq, hot, m):
                    link(dve.tensor_reduce(m[0], src, AX.X, ALU.max))
                    link(tt(eq, src, bc(m[0], n), ALU.is_equal))
                    link(tt(eq, eq, row(rank, n), ALU.mult))
                    link(dve.tensor_reduce(m[1], eq, AX.X, ALU.max))
                    link(tt(hot, eq, bc(m[1], n), ALU.is_equal))

                m = [rsm[:, n, :] for n in range(16)]
                gl, el = lg[:, :, 0:NG], lg[:, :, NG:]
                link(tt(rg[:, 0], gl, row(prb[:, PB["bg"]:PB["bg"] + NG], NG), ALU.add))
                first_max(rg[:, 0], w4, NG, rg[:, 1], rg[:, 2], m[0:2])
                link(dve.tensor_reduce(m[2], gl, AX.X, ALU.max))
                link(tt(rg[:, 4], gl, bc(m[2], NG), ALU.subtract))
                hot8 = lambda n: r1[:, n].rearrange("p t (g e) -> p t g e", g=NG)
                link(dve.tensor_copy(hot8(0), bc(rg[:, 2], EG)))
                link(ts(r1[:, 1], r1[:, 0], BIG, -BIG, ALU.mult, ALU.add))
                link(tt(r1[:, 2], el, row(prb[:, PB["be"]:PB["be"] + NE], NE), ALU.add))
                link(tt(r1[:, 2], r1[:, 2], r1[:, 0], ALU.mult))
                link(tt(r1[:, 2], r1[:, 2], r1[:, 1], ALU.add))
                first_max(r1[:, 2], w32, NE, r1[:, 4], r1[:, 3], m[3:5])
                link(stt(r1[:, 2], r1[:, 3], -2 * BIG, r1[:, 2], ALU.mult, ALU.add))
                first_max(r1[:, 2], w32, NE, r1[:, 4], r1[:, 5], m[5:7])
                link(tt(r1[:, 3], r1[:, 3], r1[:, 5], ALU.add))
                link(tt(r1[:, 4], el, r1[:, 0], ALU.mult))
                link(tt(r1[:, 4], r1[:, 4], r1[:, 1], ALU.add))
                link(dve.tensor_reduce(m[7], r1[:, 4], AX.X, ALU.max))
                tt(r1[:, 4], r1[:, 4], bc(m[7], NE), ALU.subtract).then_inc(*did("r_shift"))
                dve.wait_ge(*after(l, "r_exp", 1))
                link(dve.tensor_reduce(m[8], rg[:, 4], AX.X, ALU.add))
                link(tt(rg[:, 5], rg[:, 4], rg[:, 2], ALU.mult))
                link(dve.tensor_reduce(m[9], rg[:, 5], AX.X, ALU.add))
                link(tt(r1[:, 4], r1[:, 4], r1[:, 3], ALU.mult))
                link(dve.tensor_reduce(m[10], r1[:, 4], AX.X, ALU.add))
                link(tt(m[11], m[10], m[8], ALU.mult))
                link(dve.reciprocal(m[12], m[11]))
                link(stt(m[13], m[12], 0.5, m[9], ALU.mult, ALU.mult))
                tt(gate[:, :, :], r1[:, 4], bc(m[13], NE), ALU.mult).then_inc(*did("routed"))
                dve.wait_ge(*after(l, "routed", 1))
                with dve.Fori(0, NE // 2) as pair:
                    e = 2 * pair
                    for q in range(2):
                        for f in range(2):
                            n = 2 * (l * NE + q) + f + 1
                            dve.wait_ge(sg.sem("moe_tanh"), 2 * e + n)
                            stt(th[:, f, :], th[:, f, :], 1.0, psum[2 * f][:, :], ALU.add, ALU.mult).then_inc(*did("moe_silu"))
                            dve.wait_ge(sg.sem("moe_silu"), 2 * e + n)
                            tt(hmoe[:, q, f, :], th[:, f, :], psum[2 * f + 1][:, :], ALU.mult).then_inc(*did(f"moe_h_free{f}"))
                    for q in range(2):
                        dve.wait_ge(sg.sem("moe_y_free"), 8 * e + (8 * (l * NE + q) + 4))
                        for n in range(2 * T):
                            i, c = divmod(n, 2)
                            dve.wait_ge(sg.sem("moe_y_full"), 8 * e + (8 * (l * NE + q) + n + 1))
                            stt(x[:, i, c * 512:(c + 1) * 512], psum[4 + n % 4][:, :],
                                gate[:, i, bass.ds(e + q, 1)], x[:, i, c * 512:(c + 1) * 512],
                                ALU.mult, ALU.add).then_inc(*did("moe_y_free"))
                dve.wait_ge(sg.sem("moe_y_free"), 8 * NE * (l + 1) + 4)
                dve.engine_nop().then_inc(*did("x_moe"))

        per = {n: c // L for n, c in sg.counted.items() if not n.startswith("moe_")}
        assert per == PER1, f"PER1 = {per}"


def block_two(nc, A, x, out):
    ctx = ExitStack()
    with ctx:
        def sb(name, shape, dt=F32):
            return ctx.enter_context(nc.sbuf_tensor("b2_" + name, shape, dt))

        cn = sb("cn", [P, 4 * P])
        lvl = sb("lvl", [P, 2, LEVELS, P])
        prm = sb("prm", [P, PC2N])
        prb = sb("prb", [P, PB2N])
        w_g2 = sb("w_g2", [GR, GKW])
        actT = sb("actT", [P, KD, S])
        ring = [sb(f"ring{n}", [P, KD * 512]) for n in range(3)]
        qkv = sb("qkv", [P, 12, S])
        gqk = sb("gqk", [P, 4, S])
        nat = sb("nat", [P, T, NATW2])
        y = sb("y", [P, T, D])
        kn = sb("kn", [P, T, DH, P])
        vb = sb("vb", [P, T, DH, P])
        sqb = sb("sqb", [P, 2, S])
        qs = sb("qs", [P, 2, S])
        kdn = sb("kdn", [P, 2, T, P])
        gst = sb("gst", [P, GH, P])
        ones = sb("ones", [P, P])
        cst = sb("cst", [P, 4])
        sm = sb("sm", [P, 14, T, DH])
        rf = sb("rf", [P, 4, 16])
        ss = sb("ss", [P, 40])
        ms = sb("ms", [P, 40])
        rs = sb("rs", [P, 40])
        half = sb("half", [P, 40])
        mats = {n: sb(n, [P, DH, P])[:, :, :] for n in (
            "attT", "wT", "u", "vnew", "kb", "qt", "kdec", "st", "gaT")}
        spare = actT[:, :, :].rearrange("p (n k) s -> p n (k s)", n=8)
        for n, name in enumerate(("eg", "dn", "dt", "lm", "lt", "inv", "invT", "t1")):
            mats[name] = spare[:, n, :].rearrange("p (h s) -> p h s", h=DH)
        ltm = sqb[:, :, :].rearrange("p b (h s) -> p b h s", h=DH)
        free1 = ring[1][:, :]
        bc_, arg, ex, qt2 = (free1[:, n * 1024:(n + 1) * 1024].rearrange("p (c s) -> p c s", c=2) for n in range(4))
        ka2 = qkv[:, 8:12, :].rearrange("p a s -> p (a s)").rearrange("p (c t b j) -> p c t b j", c=2, t=T, b=2)
        grT = mats["u"][0:GR, :, :].rearrange("p h s -> p (h s)")
        ident, upper, low = cn[:, 0:P], cn[:, P:2 * P], cn[:, 3 * P:4 * P]

        sg = Signals(nc, ctx, "b2_", PER2)
        banks = Banks(nc, ctx, "b2_", sg, PLAN2, BANK2)
        did, after = sg.did, sg.after
        filled, emptied, vacant = banks.filled, banks.emptied, banks.vacant
        reader, writer = banks.reader, banks.writer

        def heads(bank):
            return bank[:, :].rearrange("p (h s) -> p h s", h=DH)

        def bc(ap, n):
            return ap.unsqueeze(len(ap.shape)).to_broadcast([*ap.shape, n])

        def every(ap, n=DH):
            return ap.unsqueeze(1).to_broadcast([P, n, ap.shape[-1]])

        last_use = [("T", 4 * c + 3) for c in range(4)] + [("nat", 4 * c + 3) for c in range(4)]
        last_use += [("wo", 2 * T - 1)] * 2
        block = ctx.enter_context(nc.Block())

        @block.sync
        def _(sp):
            sp.dma_start(cn[:, :], A["consts"][:, 0:4 * P]).then_inc(*did("const", 16))
            sp.dma_start(lvl[:, :, :, :], A["consts"][:, CN["lvl"]:CNN].rearrange(
                "p (a n m) -> p a n m", a=2, n=LEVELS)).then_inc(*did("const", 16))
            for l in range(L):
                wt = A["w_in2_t"][l].rearrange("(k p) n -> p k n", p=P)
                wn = A["w_in2_n"][l].rearrange("(k p) n -> p k n", p=P)
                wout = A["w_out2"][l].rearrange("(k p) n -> p k n", p=P)
                if l:
                    for i in range(T):
                        sp.wait_ge(*after(l - 1, "ln_done", i + 1))
                sp.dma_start(prm[:, :], A["pc2"][l]).then_inc(*did("prm", 16))
                sp.dma_start(prb[:, :], A["pb2"][l]).then_inc(*did("prm", 16))
                sp.dma_start(w_g2[:, :], A["w_g2"][l]).then_inc(*did("prm", 16))

                def load(n, src, width):
                    if n >= 3:
                        sp.wait_ge(*filled(l, *last_use[n - 3]))
                    sp.dma_start(ring[n % 3][:, 0:KD * width].rearrange("p (k n) -> p k n", k=KD),
                                 src).then_inc(*did(f"w_in{n % 3}", 16))

                for c in range(4):
                    load(c, wt[:, :, c * 512:(c + 1) * 512], 512)
                for c in range(4):
                    load(4 + c, wn[:, :, c * NCW2:(c + 1) * NCW2], NCW2)
                for c in range(2):
                    load(8 + c, wout[:, :, c * 512:(c + 1) * 512], 512)
            for i in range(T):
                sp.wait_ge(*after(L - 1, "ln_done", i + 1))
                sp.dma_start(out[i * P:(i + 1) * P, :], x[:, i, :]).then_inc(*did("stored", 16))
            sp.wait_ge(sg.sem("stored"), 16 * T)

        @block.tensor
        def _(pe):
            def turn(l, stage, src):
                for k in range(KD):
                    pe.wait_ge(*vacant(l, stage, k))
                    bank, full = writer(l, stage, k)
                    for i in range(T):
                        ins = pe.transpose(bank[:, i * P:(i + 1) * P], src[:, i, k * P:(k + 1) * P], ident)
                    ins.then_inc(*full)
                for k in range(KD):
                    pe.wait_ge(*emptied(l, stage, k))

            def four(l, stage, lhsT, rhs, n=0):
                pe.wait_ge(*vacant(l, stage, n))
                bank, full = writer(l, stage, n)
                for h in range(DH):
                    ins = pe.matmul(bank[:, h * P:(h + 1) * P], lhsT(h), rhs(h), start=True, stop=True)
                ins.then_inc(*full)

            pe.wait_ge(sg.sem("const"), 32)
            for l in range(L):
                if l:
                    for i in range(T):
                        pe.wait_ge(*after(l - 1, "ln_done", i + 1))
                turn(l, "xT", x)
                for c in range(16):
                    if c % 4 == 0:
                        n = c // 4
                        pe.wait_ge(*after(l, f"w_in{n % 3}", 16 * (n // 3 + 1)))
                    w = ring[n % 3][:, :].rearrange("p (k n) -> p k n", k=KD)
                    pe.wait_ge(*vacant(l, "T", c))
                    bank, full = writer(l, "T", c)
                    for k in range(KD):
                        ins = pe.matmul(bank[:, :], w[:, k, (c % 4) * P:(c % 4 + 1) * P], actT[:, k, :],
                                        start=k == 0, stop=k == KD - 1)
                    ins.then_inc(*full)
                for c in range(4):
                    n = 4 + c
                    pe.wait_ge(*after(l, f"w_in{n % 3}", 16 * (n // 3 + 1)))
                    w = ring[n % 3][:, 0:KD * NCW2].rearrange("p (k n) -> p k n", k=KD)
                    for i in range(T):
                        pe.wait_ge(*vacant(l, "nat", c * T + i))
                        bank, full = writer(l, "nat", c * T + i)
                        for k in range(KD):
                            ins = pe.matmul(bank[:, 0:NCW2], actT[:, k, i * P:(i + 1) * P], w[:, k, :],
                                            start=k == 0, stop=k == KD - 1)
                        ins.then_inc(*full)
                pe.wait_ge(*after(0, "ones", 1))
                for c in range(8):
                    pe.wait_ge(*after(l, "sq", c + 1))
                    pe.wait_ge(*vacant(l, "l2", c))
                    bank, full = writer(l, "l2", c)
                    pe.matmul(bank[:, :], ones[:, :], sqb[:, c % 2, :], start=True, stop=True).then_inc(*full)
                pe.wait_ge(*after(l, "silu", 12))
                pe.wait_ge(*after(l, "beta", 1))
                for t in range(T):
                    pe.wait_ge(*vacant(l, "vn", t))
                    bank, full = writer(l, "vn", t)
                    for h in range(DH):
                        ins = pe.transpose(bank[:, h * P:(h + 1) * P], qkv[:, 8 + h, t * P:(t + 1) * P], ident)
                    ins.then_inc(*full)
                pe.wait_ge(*after(l, "gcum_in", 1))
                pe.wait_ge(*vacant(l, "gc"))
                bank, full = writer(l, "gc")
                pe.matmul(bank[:, 0:T * DH], upper, sm[:, 2, :, :].rearrange("p t h -> p (t h)"),
                          start=True, stop=True).then_inc(*full)
                pe.wait_ge(*after(l, "l2n", 8))
                for t in range(T):
                    pe.wait_ge(*vacant(l, "kn", t))
                    bank, full = writer(l, "kn", t)
                    for h in range(DH):
                        ins = pe.transpose(bank[:, h * P:(h + 1) * P], qkv[:, 4 + h, t * P:(t + 1) * P], ident)
                    ins.then_inc(*full)
                m = mats
                for t in range(T):
                    tok = slice(t * P, (t + 1) * P)
                    pe.wait_ge(*after(l, "g_rep", t + 1))
                    four(l, f"gb{t}", lambda h: m["vnew"][:, h, :], lambda h: upper)
                    four(l, f"kk{t}", lambda h: qkv[:, 4 + h, tok], lambda h: qkv[:, 4 + h, tok])
                    four(l, f"qk{t}", lambda h: qkv[:, 4 + h, tok], lambda h: qkv[:, h, tok])
                    pe.wait_ge(*after(l, "lm", t + 1))
                    pe.wait_ge(*vacant(l, f"lt{t}"))
                    bank, full = writer(l, f"lt{t}")
                    for h in range(DH):
                        ins = pe.transpose(bank[:, h * P:(h + 1) * P], m["lm"][:, h, :], ident)
                    ins.then_inc(*full)
                    for n in range(1, LEVELS):
                        pe.wait_ge(*after(l, "inv", (LEVELS - 1) * t + n))
                        pe.wait_ge(*after(l, "ltm", (LEVELS - 1) * t + n))
                        pe.wait_ge(*vacant(l, f"lv{t}", 3 * (n - 1)))
                        bank, full = writer(l, f"lv{t}", 3 * (n - 1))
                        for h in range(DH):
                            ins = pe.matmul(bank[:, h * P:(h + 1) * P], ltm[:, n % 2, h, :], m["inv"][:, h, :],
                                            start=True, stop=True)
                        ins.then_inc(*full)
                        pe.wait_ge(*emptied(l, f"lv{t}", 3 * (n - 1)))
                        four(l, f"lv{t}", lambda h: m["t1"][:, h, :], lambda h: m["invT"][:, h, :], 3 * (n - 1) + 1)
                        if n < LEVELS - 1:
                            four(l, f"lv{t}", lambda h: m["invT"][:, h, :], lambda h: m["t1"][:, h, :], 3 * (n - 1) + 2)
                    pe.wait_ge(*after(l, "kb", t + 1))
                    pe.wait_ge(*emptied(l, f"lv{t}", 3 * (LEVELS - 2) + 1))
                    four(l, f"u{t}", lambda h: m["invT"][:, h, :], lambda h: vb[:, t, h, :])
                    four(l, f"wT{t}", lambda h: m["kb"][:, h, :], lambda h: m["invT"][:, h, :])
                    pe.wait_ge(*emptied(l, f"u{t}"))
                    pe.wait_ge(*emptied(l, f"wT{t}"))
                    if t:
                        pe.wait_ge(*after(l, "state", t))
                        four(l, f"ws{t}", lambda h: m["wT"][:, h, :], lambda h: m["st"][:, h, :])
                    pe.wait_ge(*after(l, "vnew", t + 1))
                    pe.wait_ge(*vacant(l, f"o{t}"))
                    bank, full = writer(l, f"o{t}")
                    for h in range(DH):
                        if t:
                            pe.matmul(bank[:, h * P:(h + 1) * P], m["qt"][:, h, :], m["st"][:, h, :],
                                      start=True, stop=False)
                        ins = pe.matmul(bank[:, h * P:(h + 1) * P], m["attT"][:, h, :], m["vnew"][:, h, :],
                                        start=not t, stop=True)
                    ins.then_inc(*full)
                    if t < T - 1:
                        four(l, f"sk{t}", lambda h: m["kdec"][:, h, :], lambda h: m["vnew"][:, h, :])
                pe.wait_ge(*vacant(l, "grT"))
                bank, full = writer(l, "grT")
                for i in range(T):
                    ins = pe.transpose(bank[0:GR, i * P:(i + 1) * P], nat[:, i, O2_GR:O2_GR + GR], ident)
                ins.then_inc(*full)
                pe.wait_ge(*emptied(l, "grT"))
                pe.wait_ge(*after(l, "prm", 48))
                for c in range(2):
                    pe.wait_ge(*vacant(l, "gl", c))
                    bank, full = writer(l, "gl", c)
                    pe.matmul(bank[:, :], w_g2[:, c * P:(c + 1) * P], grT[:, :], start=True, stop=True).then_inc(*full)
                pe.wait_ge(*after(l, "kd", 1))
                for c in range(2):
                    pe.wait_ge(*vacant(l, "kd", c))
                    bank, full = writer(l, "kd", c)
                    for t in range(T):
                        ins = pe.transpose(bank[:, t * P:(t + 1) * P], ex[:, c, t * P:(t + 1) * P], ident)
                    ins.then_inc(*full)
                for c in range(2):
                    pe.wait_ge(*emptied(l, "kd", c))
                pe.wait_ge(*after(l, "gla_in", 1))
                for t in range(T):
                    for q in range(2):
                        pe.wait_ge(*vacant(l, f"ga{t}", q))
                        bank, full = writer(l, f"ga{t}", q)
                        for c in range(2):
                            for b in range(2):
                                o = c * P + b * 64
                                ins = pe.matmul(bank[:, o:o + 64], ka2[q * GK:(q + 1) * GK, c, t, b, :],
                                                qt2[q * GK:(q + 1) * GK, c, t * P + b * 64:t * P + (b + 1) * 64],
                                                start=True, stop=True)
                        ins.then_inc(*full)
                    for q in range(2):
                        pe.wait_ge(*emptied(l, f"ga{t}", q))
                    if t:
                        pe.wait_ge(*after(l, "gstate", t))
                    pe.wait_ge(*vacant(l, f"go{t}"))
                    bank, full = writer(l, f"go{t}")
                    for h in range(GH):
                        c = h // 2
                        v = nat[:, t, O2_GV + h * GV:O2_GV + (h + 1) * GV]
                        ins = pe.matmul(bank[:, h * P:(h + 1) * P], m["gaT"][:, h, :], v, start=True, stop=not t)
                        if t:
                            ins = pe.matmul(bank[:, h * P:(h + 1) * P], qs[:, c, t * P:(t + 1) * P],
                                            gst[:, h, :], start=False, stop=True)
                    ins.then_inc(*full)
                    if t < T - 1:
                        pe.wait_ge(*vacant(l, f"gs{t}"))
                        bank, full = writer(l, f"gs{t}")
                        for h in range(GH):
                            v = nat[:, t, O2_GV + h * GV:O2_GV + (h + 1) * GV]
                            ins = pe.matmul(bank[:, h * P:(h + 1) * P], kdn[:, h // 2, t, :], v,
                                            start=True, stop=True)
                        ins.then_inc(*full)
                pe.wait_ge(*after(l, "y", 1))
                turn(l, "yT", y)
                for n in (8, 9):
                    pe.wait_ge(*after(l, f"w_in{n % 3}", 16 * (n // 3 + 1)))
                for n in range(2 * T):
                    i, c = divmod(n, 2)
                    w = ring[(8 + c) % 3][:, :].rearrange("p (k n) -> p k n", k=KD)
                    pe.wait_ge(*vacant(l, "wo", n))
                    bank, full = writer(l, "wo", n)
                    for k in range(KD):
                        ins = pe.matmul(bank[:, :], actT[:, k, i * P:(i + 1) * P], w[:, k, :],
                                        start=k == 0, stop=k == KD - 1)
                    ins.then_inc(*full)

        @block.scalar
        def _(act):
            m = mats

            def copy_out(l, stage, dst, i=0, scale=None):
                act.wait_ge(*filled(l, stage, i))
                bank, free = reader(l, stage, i)
                src = bank[:, 0:dst.free_size()]
                if len(dst.shape) == 3:
                    src = src.rearrange("p (a b) -> p a b", a=dst.shape[1])
                if scale is None:
                    act.activation(dst, src, ACT.Copy).then_inc(*free)
                else:
                    act.activation(dst, src, ACT.Identity, scale=scale).then_inc(*free)

            def inverse_norm(l, c):
                act.wait_ge(*filled(l, "l2", c))
                bank, free = reader(l, "l2", c)
                dst = y[:, c // 2, (c % 2) * 512:(c % 2 + 1) * 512]
                act.activation(dst, bank[:, :], ACT.Ln, bias=cst[:, 0:1]).then_inc(*free)
                act.wait_ge(*emptied(l, "l2", c))
                act.activation(dst, dst, ACT.Exp, scale=-0.5,
                               bias=cst[:, 1:2] if c < DH else cst[:, 2:3]).then_inc(*did("l2r"))

            act.wait_ge(*after(0, "cst", 1))
            for l in range(L):
                act.wait_ge(*after(l, "prm", 48))
                for k in range(0, KD, 2):
                    copy_out(l, "xT", actT[:, k, :], k)
                for c in range(12):
                    act.wait_ge(*after(l, "conv", c + 1))
                    if c >= 2:
                        act.wait_ge(*after(l, "silu", c - 1))
                    act.activation(sqb[:, c % 2, :], qkv[:, c, :], ACT.Tanh, scale=0.5).then_inc(*did("tanh"))
                for c in range(4):
                    copy_out(l, "T", gqk[:, c, :], 12 + c)
                for n in range(16):
                    c, i = divmod(n, T)
                    copy_out(l, "nat", nat[:, i, c * NCW2:(c + 1) * NCW2], n)
                for n in range(16):
                    act.wait_ge(*emptied(l, "nat", n))
                act.activation(sm[:, 0, :, :], nat[:, :, O2_B:O2_B + DH], ACT.Tanh, scale=0.5).then_inc(*did("beta_tanh"))
                act.wait_ge(*after(l, "silu", 12))
                for c in range(8):
                    if c >= 2:
                        act.wait_ge(*filled(l, "l2", c - 2))
                    act.activation(sqb[:, c % 2, :], qkv[:, c, :], ACT.Square).then_inc(*did("sq"))
                    if c:
                        inverse_norm(l, c - 1)
                inverse_norm(l, 7)
                act.wait_ge(*after(l, "g_abs", 1))
                act.activation(sm[:, 5, :, :], sm[:, 4, :, :], ACT.Exp).then_inc(*did("g_e"))
                act.wait_ge(*after(l, "g_e", 1))
                act.activation(sm[:, 6, :, :], sm[:, 5, :, :], ACT.Ln, bias=1.0)
                act.activation(rf[:, 3, 0:DH], prb[:, PB2["alog"]:PB2["alog"] + DH], ACT.Exp).then_inc(*did("g_ln"))
                act.wait_ge(*after(l, "gcol", 1))
                act.activation(sm[:, 9, :, :], sm[:, 7, :, :], ACT.Exp).then_inc(*did("g_exp"))
                for t in range(T):
                    copy_out(l, "kn", kn[:, t, :, :], t)
                for t in range(T):
                    if t:
                        act.wait_ge(*filled(l, f"o{t - 1}"))
                        act.wait_ge(*after(l, "tile", t))
                    act.wait_ge(*filled(l, f"gb{t}"))
                    bank, free = reader(l, f"gb{t}")
                    act.activation(m["eg"][:, :, :], heads(bank), ACT.Exp).then_inc(*did("eg"))
                    act.wait_ge(*after(l, "d_arg", t + 1))
                    act.activation(m["dn"], m["dn"], ACT.Exp, scale=-1.0)
                    act.activation(m["dt"], m["dt"], ACT.Exp).then_inc(*did("decay"))
                    copy_out(l, f"lt{t}", m["lt"])
                    for n in range(1, LEVELS):
                        copy_out(l, f"lv{t}", m["t1"], 3 * (n - 1))
                    copy_out(l, f"u{t}", m["u"])
                    copy_out(l, f"wT{t}", m["wT"])
                    copy_out(l, f"o{t}", y[:, t, 0:DW])
                act.wait_ge(*after(l, "gg_abs", 1))
                act.activation(arg[:, :, :], arg[:, :, :], ACT.Exp).then_inc(*did("gg_e"))
                act.wait_ge(*after(l, "gg_e", 1))
                act.activation(ex[:, :, :], arg[:, :, :], ACT.Ln, bias=1.0).then_inc(*did("gg_ln"))
                act.wait_ge(*after(l, "x_last", 1))
                act.activation(ex[:, :, :], arg[:, :, :], ACT.Exp, scale=-1.0).then_inc(*did("e_last"))
                act.wait_ge(*after(l, "e_last", 1))
                act.activation(arg[:, :, :], bc_[:, :, :], ACT.Exp).then_inc(*did("e_start"))
                act.wait_ge(*after(l, "x_own", 1))
                act.activation(qt2[:, :, :], arg[:, :, :], ACT.Exp).then_inc(*did("e_own"))
                act.wait_ge(*after(l, "e_own", 1))
                act.activation(arg[:, :, :], arg[:, :, :], ACT.Exp, scale=-1.0).then_inc(*did("e_ownk"))
                act.wait_ge(*after(l, "x_cross", 1))
                act.activation(ka2[:, :, :, 1, 0:64].rearrange("p c t j -> p (c t) j"),
                               ka2[:, :, :, 1, 0:64].rearrange("p c t j -> p (c t) j"), ACT.Exp,
                               scale=-1.0).then_inc(*did("e_cross"))
                for c in range(2):
                    copy_out(l, "kd", kdn[:, c, :, :], c)
                for t in range(T):
                    copy_out(l, f"go{t}", y[:, t, DW:])
                for n, o in enumerate((O2_Z, O2_GZ)):
                    for t in range(T):
                        ins = act.activation(actT[:, 4 * n + t, :], nat[:, t, o:o + 512], ACT.Tanh, scale=0.5)
                ins.then_inc(*did("z_tanh"))
                for k in range(0, KD, 2):
                    name = "dng" if k < DH else "glag"
                    copy_out(l, "yT", actT[:, k, :], k, scale=prm[:, PC2[name]:PC2[name] + 1])
                for i in range(T):
                    act.wait_ge(*after(l, "ln_mean", i + 1))
                    act.activation(y[:, i, :], x[:, i, :], ACT.Square, accum_out=ss[:, 32 + i:33 + i]).then_inc(*did("ln_sq"))

        @block.gpsimd
        def _(pool):
            chain = [0]

            def link(ins):
                chain[0] += 1
                ins.then_inc(sg.sem("pool_step"), 1)
                pool.wait_ge(sg.sem("pool_step"), chain[0])

            pool.memset(ones[:, :], 1.0)
            link(pool.memset(half[:, :], -0.5))
            pool.memset(cst[:, 0:1], 4 * EPS)
            pool.memset(cst[:, 2:3], 0.0)
            link(pool.memset(cst[:, 1:2], float(-0.5 * np.log(DK))))
            pool.memset(cst[:, 3:4], 0.0).then_inc(*did("cst"))
            pool.memset(ms[:, 0:1], 0.0).then_inc(*did("ones"))
            pool.wait_ge(sg.sem("const"), 32)
            for l in range(L):
                for t in range(T):
                    for n in range(1, LEVELS):
                        s = (LEVELS - 1) * t + n
                        if n == 1:
                            pool.wait_ge(*emptied(l, f"lt{t}"))
                            for c in range(8):
                                if t == 0:
                                    pool.wait_ge(*filled(l, "l2", c))
                        if n >= 3:
                            pool.wait_ge(*filled(l, f"lv{t}", 3 * (n - 3)))
                        elif t:
                            pool.wait_ge(*filled(l, f"lv{t - 1}", 3 * (LEVELS - 2)))
                        pool.tensor_tensor(ltm[:, n % 2, :, :], mats["lt"], every(lvl[:, 1, n, :]),
                                           ALU.mult).then_inc(*did("ltm"))
                pool.wait_ge(*after(l, "ss_y", 1))
                link(pool.tensor_scalar(ms[:, 0:32], ss[:, 0:32], 1.0 / P, EPS, ALU.mult, ALU.add))
                pool.tensor_tensor(rs[:, 0:32], ms[:, 0:32], half[:, 0:32], ALU.pow).then_inc(*did("rs_y"))
                for i in range(T):
                    pool.wait_ge(*after(l, "ln_sq", i + 1))
                    k = slice(32 + i, 33 + i)
                    link(pool.tensor_scalar(ms[:, k], ss[:, k], 1.0 / D, EPS, ALU.mult, ALU.add))
                    pool.tensor_tensor(rs[:, k], ms[:, k], half[:, 0:1], ALU.pow).then_inc(*did("ln_rs"))

        @block.vector
        def _(dve):
            chain = [0]
            m = mats

            def link(ins):
                chain[0] += 1
                ins.then_inc(sg.sem("dve_step"), 1)
                dve.wait_ge(sg.sem("dve_step"), chain[0])

            def tt(out, a, b, op):
                return dve.tensor_tensor(out, a, b, op)

            def ts(out, a, s1, s2=None, op0=ALU.mult, op1=None):
                return dve.tensor_scalar(out, a, s1, s2, op0, op1) if op1 is not None else dve.tensor_scalar(out, a, s1, None, op0)

            def stt(out, a, s, b, op0, op1):
                return dve.scalar_tensor_tensor(out=out, in0=a, scalar=s, in1=b, op0=op0, op1=op1)

            link(dve.memset(gst[:, :, :], 0.0))
            dve.wait_ge(*after(0, "const", 32))
            for l in range(L):
                dve.wait_ge(*after(l, "prm", 48))
                for k in range(1, KD, 2):
                    dve.wait_ge(*filled(l, "xT", k))
                    bank, free = reader(l, "xT", k)
                    dve.tensor_copy(actT[:, k, :], bank[:, :]).then_inc(*free)

                def silu(c):
                    dve.wait_ge(*after(l, "tanh", c + 1))
                    stt(qkv[:, c, :], sqb[:, c % 2, :], 1.0, qkv[:, c, :], ALU.add, ALU.mult).then_inc(*did("silu"))

                for c in range(12):
                    dve.wait_ge(*filled(l, "T", c))
                    bank, free = reader(l, "T", c)
                    w = PC2["cw"] + 4 * c
                    link(ts(qkv[:, c, :], bank[:, :], prm[:, w + 3:w + 4]))
                    for d in range(1, 4):
                        ins = stt(qkv[:, c, d:], bank[:, 0:S - d], prm[:, w + 3 - d:w + 4 - d], qkv[:, c, d:],
                                  ALU.mult, ALU.add)
                        if d < 3:
                            link(ins)
                    link(ins)
                    dve.engine_nop().then_inc(*free)
                    dve.engine_nop().then_inc(*did("conv"))
                    if c:
                        silu(c - 1)
                silu(11)
                dve.wait_ge(*after(l, "beta_tanh", 1))
                link(ts(sm[:, 1], sm[:, 0], 0.5, 0.5, ALU.mult, ALU.add))
                ts(sm[:, 11], sm[:, 1], 0.5).then_inc(*did("beta"))
                dtb = prb[:, PB2["dtb"]:PB2["dtb"] + DH].unsqueeze(1).to_broadcast([P, T, DH])
                link(tt(sm[:, 3], nat[:, :, O2_A:O2_A + DH], dtb, ALU.add))
                stt(sm[:, 4], sm[:, 3], -1.0, sm[:, 3], ALU.mult, ALU.min).then_inc(*did("g_abs"))
                for c in range(8):
                    dve.wait_ge(*after(l, "l2r", c + 1))
                    tt(qkv[:, c, :], qkv[:, c, :], y[:, c // 2, (c % 2) * 512:(c % 2 + 1) * 512], ALU.mult).then_inc(*did("l2n"))
                dve.wait_ge(*after(l, "g_ln", 1))
                link(stt(sm[:, 2], sm[:, 3], 0.0, sm[:, 6], ALU.max, ALU.add))
                stt(sm[:, 2], sm[:, 2], -1.0, rf[:, 3, 0:DH].unsqueeze(1).to_broadcast([P, T, DH]),
                    ALU.mult, ALU.mult).then_inc(*did("gcum_in"))
                dve.wait_ge(*after(l, "beta", 1))
                for t in range(T):
                    dve.wait_ge(*filled(l, "vn", t))
                    bank, free = reader(l, "vn", t)
                    tt(vb[:, t, :, :], heads(bank), bc(sm[:, 11, t, :], P), ALU.mult).then_inc(*free)
                dve.wait_ge(*filled(l, "gc"))
                bank, free = reader(l, "gc")
                flat = lambda n: sm[:, n, :, :].rearrange("p t h -> p (t h)")
                link(dve.tensor_copy(flat(7), bank[:, 0:T * DH]))
                ts(flat(8), bank[:, 0:T * DH], -1.0).then_inc(*free)
                dve.wait_ge(*emptied(l, "gc"))
                dve.engine_nop().then_inc(*did("gcol"))
                dve.wait_ge(*after(l, "g_exp", 1))
                link(tt(sm[:, 10], sm[:, 9], sm[:, 1], ALU.mult))
                dve.wait_ge(*after(l, "gcum_in", 1))
                for t in range(T):
                    dve.wait_ge(*emptied(l, "kn", t))
                for t in range(T):
                    tok = slice(t * P, (t + 1) * P)
                    if t:
                        dve.wait_ge(*filled(l, f"o{t - 1}"))
                        dve.wait_ge(*filled(l, f"sk{t - 1}"))
                    dve.tensor_copy(m["vnew"][:, :, :], bc(sm[:, 2, t, :], P)).then_inc(*did("g_rep"))
                    dve.wait_ge(*after(l, "eg", t + 1))
                    dve.wait_ge(*filled(l, f"gb{t}"))
                    bank, free = reader(l, f"gb{t}")
                    for h in range(DH):
                        ts(m["dn"][:, h, :], heads(bank)[:, h, :], sm[:, 8, t, h:h + 1], 0.0, ALU.add, ALU.max)
                    for h in range(DH):
                        ins = ts(m["dt"][:, h, :], heads(bank)[:, h, :], sm[:, 8, t, h:h + 1], 0.0, ALU.add, ALU.min)
                    ins.then_inc(*free)
                    dve.wait_ge(*emptied(l, f"gb{t}"))
                    dve.engine_nop().then_inc(*did("d_arg"))
                    dve.wait_ge(*after(l, "decay", t + 1))
                    dve.wait_ge(*filled(l, f"kk{t}"))
                    bank, free = reader(l, f"kk{t}")
                    tt(m["lm"], m["dn"], heads(bank), ALU.mult).then_inc(*free)
                    dve.wait_ge(*emptied(l, f"kk{t}"))
                    for h in range(DH):
                        ins = stt(m["lm"][:, h, :], m["lm"][:, h, :], sm[:, 1, t, h:h + 1], low, ALU.mult, ALU.mult)
                    ins.then_inc(*did("lm"))
                    dve.wait_ge(*filled(l, f"qk{t}"))
                    bank, free = reader(l, f"qk{t}")
                    tt(m["attT"], m["dt"], heads(bank), ALU.mult).then_inc(*free)
                    dve.wait_ge(*emptied(l, f"qk{t}"))
                    link(tt(m["attT"][:, :, :], m["attT"][:, :, :], every(upper), ALU.mult))
                    dve.wait_ge(*after(l, "lm", t + 1))
                    link(tt(m["inv"], m["lm"], every(lvl[:, 0, 0, :]), ALU.mult))
                    link(tt(m["inv"], every(ident), m["inv"], ALU.subtract))
                    dve.wait_ge(*emptied(l, f"lt{t}"))
                    link(tt(m["invT"], m["lt"], every(lvl[:, 1, 0, :]), ALU.mult))
                    tt(m["invT"], every(ident), m["invT"], ALU.subtract).then_inc(*did("inv"))
                    tt(m["kb"][:, :, :], kn[:, t, :, :], bc(sm[:, 10, t, :], P), ALU.mult).then_inc(*did("kb"))
                    link(tt(m["kdec"][:, :, :], kn[:, t, :, :], bc(m["dt"][:, :, P - 1], P), ALU.mult))
                    link(tt(m["qt"][:, :, :], qkv[:, 0:4, tok], m["eg"], ALU.mult))
                    for n in range(1, LEVELS):
                        if n < LEVELS - 1:
                            dve.wait_ge(*filled(l, f"lv{t}", 3 * (n - 1) + 2))
                        dve.wait_ge(*filled(l, f"lv{t}", 3 * (n - 1) + 1))
                        bank, free = reader(l, f"lv{t}", 3 * (n - 1) + 1)
                        tt(m["invT"], m["invT"], heads(bank), ALU.subtract).then_inc(*free)
                        if n < LEVELS - 1:
                            dve.wait_ge(*emptied(l, f"lv{t}", 3 * (n - 1) + 1))
                            dve.wait_ge(*filled(l, f"lv{t}", 3 * (n - 1) + 2))
                            bank, free = reader(l, f"lv{t}", 3 * (n - 1) + 2)
                            tt(m["inv"], m["inv"], heads(bank), ALU.subtract).then_inc(*free)
                            dve.wait_ge(*emptied(l, f"lv{t}", 3 * (n - 1) + 2))
                            dve.engine_nop().then_inc(*did("inv"))
                    dve.wait_ge(*emptied(l, f"u{t}"))
                    if t:
                        dve.wait_ge(*filled(l, f"ws{t}"))
                        bank, free = reader(l, f"ws{t}")
                        tt(m["vnew"][:, :, :], m["u"][:, :, :], heads(bank), ALU.subtract).then_inc(*free)
                        dve.wait_ge(*emptied(l, f"ws{t}"))
                        dve.engine_nop().then_inc(*did("vnew"))
                    else:
                        dve.tensor_copy(m["vnew"][:, :, :], m["u"][:, :, :]).then_inc(*did("vnew"))
                    dve.wait_ge(*filled(l, f"o{t}"))
                    if t < T - 1:
                        dve.wait_ge(*filled(l, f"sk{t}"))
                        bank, free = reader(l, f"sk{t}")
                        if t:
                            for h in range(DH):
                                ins = stt(m["st"][:, h, :], m["st"][:, h, :], m["eg"][:, h, P - 1:P],
                                          heads(bank)[:, h, :], ALU.mult, ALU.add)
                        else:
                            ins = dve.tensor_copy(m["st"][:, :, :], heads(bank))
                        ins.then_inc(*free)
                        dve.wait_ge(*emptied(l, f"sk{t}"))
                        dve.engine_nop().then_inc(*did("state"))
                    dve.engine_nop().then_inc(*did("tile"))
                dve.wait_ge(*filled(l, "grT"))
                bank, free = reader(l, "grT")
                dve.tensor_copy(grT[:, :], bank[0:GR, :]).then_inc(*free)
                for c in range(2):
                    dve.wait_ge(*filled(l, "gl", c))
                    bank, free = reader(l, "gl", c)
                    ts(qt2[:, c, :], bank[:, :], prm[:, PC2["gb"] + c:PC2["gb"] + c + 1], None, ALU.add).then_inc(*free)
                for c in range(2):
                    dve.wait_ge(*emptied(l, "gl", c))
                stt(arg[:, :, :], qt2[:, :, :], -1.0, qt2[:, :, :], ALU.mult, ALU.min).then_inc(*did("gg_abs"))
                dve.wait_ge(*after(l, "gg_ln", 1))
                link(stt(qt2[:, :, :], qt2[:, :, :], 0.0, ex[:, :, :], ALU.min, ALU.subtract))
                link(dve.memset(arg[:, :, :], 0.0))
                for c in range(2):
                    for t in range(T):
                        ins = dve.tensor_tensor_scan(bc_[:, c, t * P:(t + 1) * P], qt2[:, c, t * P:(t + 1) * P],
                                                     arg[:, c, t * P:(t + 1) * P], 0.0, ALU.add, ALU.add)
                        link(ins)
                link(ts(bc_[:, :, :], bc_[:, :, :], 1.0 / TAU))
                tiles = lambda ap, w: ap[:, :, :].rearrange("p c (t j) -> p (c t) j", j=w)
                gq = gqk[:, 0:2, :]
                gk = gqk[:, 2:4, :]
                tt(tiles(arg, P), tiles(bc_, P), bc(tiles(bc_, P)[:, :, P - 1], P), ALU.subtract).then_inc(*did("x_last"))
                dve.wait_ge(*after(l, "e_last", 1))
                tt(ex[:, :, :], ex[:, :, :], gk, ALU.mult).then_inc(*did("kd"))
                dve.wait_ge(*after(l, "e_start", 1))
                link(stt(qs[:, :, :], arg[:, :, :], GK ** -0.5, gq, ALU.mult, ALU.mult))
                link(dve.tensor_copy(rf[:, 0, 0:2 * T], tiles(arg, P)[:, :, P - 1]))
                tt(tiles(arg, 64), tiles(bc_, 64), bc(tiles(bc_, 64)[:, :, 31], 64), ALU.subtract).then_inc(*did("x_own"))
                dve.wait_ge(*after(l, "e_ownk", 1))
                link(stt(qt2[:, :, :], qt2[:, :, :], GK ** -0.5, gq, ALU.mult, ALU.mult))
                link(dve.memset(ka2[:, :, :, 0, 64:128].rearrange("p c t j -> p (c t) j"), 0.0))
                own = tiles(arg, P)
                gkt = gk.rearrange("p c (t j) -> p (c t) j", j=P)
                kaf = ka2.rearrange("p c t b j -> p (c t) b j")
                link(tt(kaf[:, :, 0, 0:64], own[:, :, 0:64], gkt[:, :, 0:64], ALU.mult))
                link(tt(kaf[:, :, 1, 64:128], own[:, :, 64:128], gkt[:, :, 64:128], ALU.mult))
                tt(kaf[:, :, 1, 0:64], tiles(bc_, P)[:, :, 0:64], bc(tiles(bc_, P)[:, :, 95], 64),
                   ALU.subtract).then_inc(*did("x_cross"))
                dve.wait_ge(*after(l, "e_cross", 1))
                tt(kaf[:, :, 1, 0:64], kaf[:, :, 1, 0:64], gkt[:, :, 0:64], ALU.mult).then_inc(*did("gla_in"))
                for t in range(T):
                    if t:
                        dve.wait_ge(*filled(l, f"go{t - 1}"))
                    for q in range(2):
                        dve.wait_ge(*filled(l, f"ga{t}", q))
                        bank, free = reader(l, f"ga{t}", q)
                        tt(m["gaT"].rearrange("p (c q) s -> p q c s", q=2)[:, q],
                           bank[:, 0:2 * P].rearrange("p (c s) -> p c s", c=2), every(upper, 2),
                           ALU.mult).then_inc(*free)
                    if t < T - 1:
                        dve.wait_ge(*filled(l, f"go{t}"))
                        dve.wait_ge(*filled(l, f"gs{t}"))
                        bank, free = reader(l, f"gs{t}")
                        for h in range(GH):
                            c, own_rows = h // 2, slice((h % 2) * GK, (h % 2 + 1) * GK)
                            src = bank[own_rows, h * P:(h + 1) * P]
                            if t:
                                ins = stt(gst[own_rows, h, :], gst[own_rows, h, :],
                                          rf[own_rows, 0, c * T + t:c * T + t + 1], src, ALU.mult, ALU.add)
                            else:
                                ins = dve.tensor_copy(gst[own_rows, h, :], src)
                        ins.then_inc(*free)
                        dve.wait_ge(*emptied(l, f"gs{t}"))
                        dve.engine_nop().then_inc(*did("gstate"))
                for t in range(T):
                    dve.wait_ge(*emptied(l, f"o{t}"))
                    dve.wait_ge(*emptied(l, f"go{t}"))
                dve.wait_ge(*after(l, "z_tanh", 1))
                for n, o in enumerate((O2_Z, O2_GZ)):
                    for t in range(T):
                        ins = stt(nat[:, t, o:o + 512], actT[:, 4 * n + t, :], 1.0, nat[:, t, o:o + 512],
                                  ALU.add, ALU.mult)
                link(ins)
                yh = y[:, :, :].rearrange("p t (g d) -> p (t g) d", d=P)
                sq = actT[:, :, :].rearrange("p k s -> p (k s)").rearrange("p (g d) -> p g d", d=P)
                link(tt(sq, yh, yh, ALU.mult))
                dve.tensor_reduce(ss[:, 0:32], sq, AX.X, ALU.add).then_inc(*did("ss_y"))
                dve.wait_ge(*after(l, "rs_y", 1))
                link(tt(yh, yh, bc(rs[:, 0:32], P), ALU.mult))
                link(stt(y[:, :, 0:512], y[:, :, 0:512], 0.5, nat[:, :, O2_Z:O2_Z + 512], ALU.mult, ALU.mult))
                stt(y[:, :, 512:], y[:, :, 512:], 0.5, nat[:, :, O2_GZ:O2_GZ + 512], ALU.mult, ALU.mult).then_inc(*did("y"))
                for k in range(1, KD, 2):
                    name = "dng" if k < DH else "glag"
                    dve.wait_ge(*filled(l, "yT", k))
                    bank, free = reader(l, "yT", k)
                    ts(actT[:, k, :], bank[:, :], prm[:, PC2[name]:PC2[name] + 1]).then_inc(*free)
                def norm(i):
                    dve.wait_ge(*after(l, "ln_rs", i + 1))
                    link(stt(x[:, i, :], x[:, i, :], rs[:, 32 + i:33 + i], prb[:, 0:D], ALU.mult, ALU.mult))
                    tt(x[:, i, :], x[:, i, :], prb[:, PB2["lnb"]:PB2["lnb"] + D], ALU.add).then_inc(*did("ln_done"))

                for i in range(T):
                    for c in range(2):
                        dve.wait_ge(*filled(l, "wo", 2 * i + c))
                        bank, free = reader(l, "wo", 2 * i + c)
                        stt(x[:, i, c * 512:(c + 1) * 512], x[:, i, c * 512:(c + 1) * 512], ALPHA, bank[:, :],
                            ALU.mult, ALU.add).then_inc(*free)
                    for c in range(2):
                        dve.wait_ge(*emptied(l, "wo", 2 * i + c))
                    link(dve.tensor_reduce(rf[:, 1, i:i + 1], x[:, i, :], AX.X, ALU.add))
                    link(ts(rf[:, 2, i:i + 1], rf[:, 1, i:i + 1], 1.0 / D))
                    ts(x[:, i, :], x[:, i, :], rf[:, 2, i:i + 1], None, ALU.subtract).then_inc(*did("ln_mean"))
                    if i:
                        norm(i - 1)
                norm(T - 1)

        once = ("const", "cst", "ones", "stored")
        per = {n: c // L for n, c in sg.counted.items() if n not in once}
        assert per == PER2, f"PER2 = {per}"


def build(nc, A, out):
    with nc.sbuf_tensor("x", [P, T, D], F32) as x:
        block_one(nc, A, x)
        block_two(nc, A, x, out)


def columns(parts, n):
    out = np.zeros((P, n), np.float32)
    at = 0
    for a in parts:
        out[:a.shape[0], at:at + a.shape[1]] = a
        at += a.shape[1]
    return out


def lay_out(v):
    v = {k: np.asarray(a) for k, a in v.items()}
    A = {"x": v["x"].reshape(S, D), "positions": np.ascontiguousarray(v["positions"].reshape(T, P).T),
         "consts": constants()}
    for n in ("w_in", "w_out", "a_w_uq", "a_w_ukv", "c_w_s"):
        A[n] = v[n]
    for n in ("w1", "w3", "w2"):
        A[n] = v[n].reshape(L * NE, *v[n].shape[2:])
    A["w_r"] = np.concatenate([v["w_group"], v["w_expert"]], axis=-1)
    pc, pb = [], []
    for l in range(L):
        kt = lambda a: a.reshape(-1, P).T
        conv = v["m_conv_w"][l].reshape(4, 8, MD).transpose(2, 1, 0).reshape(MD, 32)
        pc.append(columns([kt(v["attn_norm"][l]), kt(v["ffn_norm"][l]), kt(v["mix_out_norm"][l]),
                           kt(v["a_q_norm"][l]), kt(v["a_kv_norm"][l]), v["c_b_s"][l].T, conv,
                           v["m_conv_b"][l].reshape(8, MD).T, v["m_gate_bias"][l][:MH, None],
                           v["m_gate_bias"][l][MH:, None]], PCN))
        row = np.concatenate([v["a_q_head_norm"][l], v["a_k_head_norm"][l], v["c_v_norm"][l],
                              v["b_group"][l], v["b_expert"][l]])
        pb.append(np.broadcast_to(row, (P, PBN)))
    A["pc"], A["pb"] = np.stack(pc), np.ascontiguousarray(np.stack(pb))
    w = v["w_in_2"]
    o = np.cumsum([0, 3 * DW, DW, 2 * DH, 2 * GKW, 2 * GW + GR])
    A["w_in2_t"] = np.concatenate([w[:, :, o[0]:o[1]], w[:, :, o[3]:o[4]]], axis=-1)
    A["w_in2_n"] = np.concatenate([w[:, :, o[1]:o[3]], w[:, :, o[4]:o[5]]], axis=-1)
    A["w_out2"], A["w_g2"] = v["w_out_2"], v["gla_gate_w2_2"]
    A["pc2"] = np.stack([columns([v["conv_w_2"][l].reshape(4, 12, P).transpose(2, 1, 0).reshape(P, 48),
                                  v["dn_norm_g_2"][l][:, None], v["gla_norm_g_2"][l][:, None],
                                  v["gla_gate_b_2"][l].reshape(2, P).T], PC2N) for l in range(L)])
    A["pb2"] = np.stack([np.broadcast_to(np.concatenate([v[n][l] for n in (
        "ln_g_2", "ln_b_2", "dn_a_log_2", "dn_dt_bias_2")]), (P, PB2N)) for l in range(L)])
    return {k: np.ascontiguousarray(a) for k, a in A.items()}


def kernel(**inputs):
    import concourse.bacc as bacc
    from concourse.bass_utils import run_bass_kernel_spmd

    nc = bacc.Bacc("TRN2", target_bir_lowering=False, num_devices=1, dynamic_dma_scratch_size=2048)
    arrays = {f"in_{k}": a for k, a in lay_out(inputs).items()}
    A = {k[3:]: nc.dram_tensor(k, a.shape, mybir.dt.from_np(a.dtype), kind="ExternalInput").ap()
         for k, a in arrays.items()}
    out = nc.dram_tensor("out", (S, D), F32, kind="ExternalOutput").ap()
    build(nc, A, out)
    r = run_bass_kernel_spmd(nc, [arrays], core_ids=[0])
    return r.results[0]["out"].reshape(1, S, D)
```

```python
from contextlib import ExitStack

import numpy as np
import concourse.bass as bass
from concourse import mybir

ALU = mybir.AluOpType
ACT = mybir.ActivationFunctionType
AX = mybir.AxisListType
F32 = mybir.dt.float32
I32 = mybir.dt.int32

P = 128
S, D, L = 512, 1024, 2
T = S // P
KD = D // P
EPS = 1e-6
BIG = 1e30

MH, MD = 4, 96
MW = MH * MD
AH, NOPE, ROPE, AQ, AV = 6, 64, 32, 96, 64
AW = AH * AV
QR, KVR = 256, 128
CG, CD = 4, 64
CW = CG * CD
D_IN = 4 * MW + 2 * MH + QR + KVR + ROPE + 2 * CW
NAT0 = 2 * MW
NATW = D_IN - NAT0
NCH = 4
NCW = NATW // NCH
O_MV, O_MO, O_I, O_F = 0, MW, 2 * MW, 2 * MW + MH
O_CQ = O_F + MH
O_CKV = O_CQ + QR
O_KR = O_CKV + KVR
O_CU = O_KR + ROPE
O_CV = O_CU + CW
NG, EG = 4, 8
NE = NG * EG
FE = 256
RW = NG + NE
NPAIR = (2 * S // P + NE) // 2
NBLK = 2 * NPAIR
NOWHERE = 4095

DH, DK = 4, 128
DW = DH * DK
GH, GK, GV = 4, 64, 128
GW = GH * GV
GKW = GH * GK
GR = 16
TAU = 16.0
D_IN2 = 3 * DW + DW + 2 * DH + 2 * GKW + 2 * GW + GR
ALPHA = (2.0 * L) ** 0.25
LEVELS = 7
O2_Z, O2_B, O2_A = 0, DW, DW + DH
O2_GV = DW + 2 * DH
O2_GZ = O2_GV + GW
O2_GR = O2_GZ + GW
NATW2 = O2_GR + GR
NCW2 = NATW2 // 4

PC = {}
PB = {}
PC2 = {}
PB2 = {}


def pack_offsets(table, items):
    at = 0
    for name, n in items:
        table[name] = at
        at += n
    return at


PCN = pack_offsets(PC, [("attn", KD), ("ffn", KD), ("mix", KD), ("qg", 2), ("kvg", 1), ("cb", CG),
                        ("cw", 8 * 4), ("cbias", 8), ("bi", 1), ("bf", 1)])
PBN = pack_offsets(PB, [("qh", AQ), ("kh", AQ), ("cv", CW), ("bg", NG), ("be", NE)])
PC2N = pack_offsets(PC2, [("cw", 12 * 4), ("dng", 1), ("glag", 1), ("gb", 2)])
PB2N = pack_offsets(PB2, [("lng", D), ("lnb", D), ("alog", DH), ("dtb", DH)])

CN = {}
CNN = pack_offsets(CN, [("ident", P), ("upper", P), ("neg", P), ("low", P), ("w4", NG), ("w32", NE),
                        ("freq", ROPE // 2), ("sel", MH * P), ("supper", P), ("blk", NBLK), ("tok", T), ("lvl", LEVELS * P), ("lvlt", LEVELS * P)])


def constants():
    c = np.zeros((P, CNN), np.float32)
    i, j = np.arange(P)[:, None], np.arange(P)[None, :]
    c[:, CN["ident"]:CN["ident"] + P] = i == j
    c[:, CN["upper"]:CN["upper"] + P] = i <= j
    c[:, CN["neg"]:CN["neg"] + P] = np.where(j <= i, 0.0, -BIG)
    c[:, CN["low"]:CN["low"] + P] = j < i
    c[:, CN["w4"]:CN["w4"] + NG] = NG - np.arange(NG)
    c[:, CN["w32"]:CN["w32"] + NE] = NE - np.arange(NE)
    half = np.arange(0, ROPE, 2, dtype=np.float32) / np.float32(ROPE)
    c[:, CN["freq"]:CN["freq"] + ROPE // 2] = np.float32(1.0) / (np.float32(10000.0) ** half)
    for h in range(MH):
        c[h, CN["sel"] + h * P:CN["sel"] + (h + 1) * P] = 1.0
    c[:, CN["supper"]:CN["supper"] + P] = i < j
    c[:, CN["blk"]:CN["blk"] + NBLK] = np.arange(NBLK)
    c[:, CN["tok"]:CN["tok"] + T] = np.arange(T)[None, :] * P + i
    for n in range(LEVELS):
        b = 1 << n
        m = ((i // (2 * b)) == (j // (2 * b))) & ((i // b) % 2 == 1) & ((j // b) % 2 == 0)
        c[:, CN["lvl"] + n * P:CN["lvl"] + (n + 1) * P] = m
        c[:, CN["lvlt"] + n * P:CN["lvlt"] + (n + 1) * P] = m.T
    return c


def bank_plan(uses):
    first, at = {}, 0
    for name, n in uses:
        first[name] = at
        at += n
    per = [len(range(b, at, 8)) for b in range(8)]
    return first, per


def attention_order():
    order = [("q", 0), ("k", 0)]
    pairs = AH * T
    for m in range(pairs + 2):
        order += [(0, m)] * (m < pairs)
        if m % T == 2 and m // T + 1 < AH:
            order += [("q", m // T + 1), ("k", m // T + 1)]
        order += [(1, m - 1)] * (1 <= m <= pairs) + [(2, m - 2)] * (m >= 2)
    return {use: n for n, use in enumerate(order)}


ATTENTION = attention_order()


def att(n, step):
    return "heads", ATTENTION[step, n]


def turned(h, c):
    return "heads", ATTENTION["qk"[c], h]


PLAN1, BANK1 = bank_plan([
    ("xT", KD), ("qk", 8), ("nat", NCH * T), ("grow", 2), ("gcol", 1), ("cT", 3), ("uq", 2 * T),
    ("ukv", 2 * T), ("wsT", 1), ("csg", 2)]
    + [("m0", 1 + T)] + [u for k in range(MH) for u in ((f"m{k + 1}", 1 + T), (f"mo{k}", 1))[k == MH - 1:]]
    + [("heads", AH * (2 + 3 * T))]
    + [("yT", KD), ("wo", 2 * T), ("fT", KD), ("route", 1), ("places", 1)])

TILES2 = []
for t_ in range(T):
    TILES2 += [(f"{n}{t_}", 1) for n in ("gb", "kk", "qk", "lt")]
    TILES2 += [(f"lv{t_}", 3 * (LEVELS - 1) - 1), (f"u{t_}", 1), (f"wT{t_}", 1)]
    TILES2 += [(f"ws{t_}", 1)] * (t_ > 0) + [(f"o{t_}", 1)] + [(f"sk{t_}", 1)] * (t_ < T - 1)
GLA2 = []
for t_ in range(T):
    GLA2 += [(f"ga{t_}", 2), (f"go{t_}", 1)] + [(f"gs{t_}", 1)] * (t_ < T - 1)

PLAN2, BANK2 = bank_plan(
    [("xT", KD), ("T", 16), ("nat", 16), ("l2", 8), ("vn", T), ("gc", 1), ("kn", T)] + TILES2
    + [("grT", 1), ("gl", 2), ("kd", 2)] + GLA2 + [("yT", KD), ("wo", 2 * T)])

PER2 = {
    "prm": 48, "w_in0": 64, "w_in1": 48, "w_in2": 48, "tanh": 12, "beta_tanh": 1, "sq": 8, "l2r": 8, "g_e": 1,
    "g_ln": 1, "g_exp": 1, "eg": 4, "decay": 4, "gg_e": 1, "gg_ln": 1, "e_last": 1, "e_start": 1, "e_own": 1,
    "e_ownk": 1, "e_cross": 1, "z_tanh": 4, "ss_y": 1, "ln_sq": 4, "ltm": 24, "rs_y": 2, "ln_rs": 4, "conv": 12,
    "silu": 12, "beta": 1, "g_abs": 1, "l2n": 8, "gcum_in": 1, "gcol": 1, "g_rep": 4, "d_arg": 4, "lm": 4,
    "inv": 24, "kb": 4, "vnew": 4, "state": 3, "tile": 4, "gg_abs": 1, "x_last": 1, "kd": 1, "x_own": 1,
    "x_cross": 1, "gla_in": 1, "gstate": 3, "ss_gy": 1, "y": 2, "ln_mean": 4, "ln_done": 4,
}
PER1 = {
    "const": 16, "x_in": 32, "prm": 32, "w_in0": 48, "w_in1": 48, "w_in2": 32, "w_small": 64, "xn_out": 64,
    "table_clear": 16, "table_in": 16, "y_in0": 32, "y_in1": 32, "trig": 0, "ss_x": 4, "qk_tanh": 8, "gate_ln": 1,
    "ss_c": 1, "gate_em": 1, "mo_tanh": 1, "gelu_tanh": 1, "wsT_raw": 1, "qk_sq": 2, "m_e": 12, "k_scaled": 1,
    "ss_f": 4, "r_exp": 1, "ones": 0, "nowhere": 0, "rs_x": 4, "vaug": 1, "rs_c": 1, "gelu_arg": 1, "rs_v": 1,
    "k_rope": 1, "rs_q": 1, "rs_k": 1, "mc_norm": 1, "rs_y": 1, "rs_f": 4, "slots_put": 128, "angles": 0, "xn": 4,
    "qk_conv": 8, "qk_silu": 8, "gate_abs": 1, "gate_mx": 1, "cqn": 8, "ss_v": 1, "cvn": 1, "m_w": 16, "ss_q": 1,
    "m_h": 4, "ss_k": 1, "qk_rope": 2, "a_max": 24, "ss_y": 3, "y_norm": 1, "fn": 4, "choices": 1, "r_shift": 1,
    "block_experts": 1, "slots": 1, "y_added": 4,
}


class Signals:

    def __init__(self, nc, ctx, prefix, per):
        self.nc, self.ctx, self.prefix, self.per = nc, ctx, prefix, per
        self.sems = {}
        self.counted = {}

    def sem(self, name):
        if name not in self.sems:
            self.sems[name] = self.ctx.enter_context(self.nc.semaphore(self.prefix + name))
        return self.sems[name]

    def did(self, name, n=1):
        self.counted[name] = self.counted.get(name, 0) + n
        return self.sem(name), n

    def after(self, layer, name, n):
        return self.sem(name), layer * self.per.get(name, 0) + n


class Banks:

    def __init__(self, nc, ctx, prefix, sg, plan, per):
        self.psum = [ctx.enter_context(nc.psum_tensor(f"{prefix}bank{b}", [P, 512], F32)) for b in range(8)]
        self.sg, self.plan, self.per = sg, plan, per

    def turn(self, layer, stage, i):
        n = self.plan[stage] + i
        return n % 8, layer * self.per[n % 8] + n // 8

    def filled(self, layer, stage, i=0):
        b, before = self.turn(layer, stage, i)
        return self.sg.sem(f"bank_full{b}"), before + 1

    def emptied(self, layer, stage, i=0):
        b, before = self.turn(layer, stage, i)
        return self.sg.sem(f"bank_free{b}"), before + 1

    def vacant(self, layer, stage, i=0):
        b, before = self.turn(layer, stage, i)
        return self.sg.sem(f"bank_free{b}"), before

    def writer(self, layer, stage, i=0):
        b, _ = self.turn(layer, stage, i)
        return self.psum[b], (self.sg.sem(f"bank_full{b}"), 1)

    def reader(self, layer, stage, i=0):
        b, _ = self.turn(layer, stage, i)
        return self.psum[b], (self.sg.sem(f"bank_free{b}"), 1)


def block_one(nc, A, x, sems):
    ctx = ExitStack()
    with ctx:
        def sb(name, shape, dt=F32):
            return ctx.enter_context(nc.sbuf_tensor("b1_" + name, shape, dt))

        cn = sb("cn", [P, CN["lvl"]])
        prm = sb("prm", [P, PCN])
        prb = sb("prb", [P, PBN])
        actT = sb("actT", [P, KD, S])
        nat = sb("nat", [P, T, D])
        proj = sb("proj", [P, T, NATW])
        ring = [sb(f"ring{n}", [P, KD * 512]) for n in range(3)]
        qkc = sb("qkc", [MD, 8, S])
        work = sb("work", [P, 2, T, S])
        ebuf = sb("ebuf", [P, 2, S])
        vaug = sb("vaug", [P, T, MH, MD + 1])
        qa = sb("qa", [P, T, AH, AQ])
        ka = sb("ka", [P, T, AH, AQ])
        va = sb("va", [P, T, AH, AV])
        w_uq = sb("w_uq", [P, 2, AH * AQ])
        w_ukv = sb("w_ukv", [P, AH * (NOPE + AV)])
        w_s = sb("w_s", [P, CG, P])
        w_sT = w_s
        w_r = sb("w_r", [P, KD, RW])
        rg = sb("rg", [P, 8, T, NG])
        asum = sb("asum", [P, 4, AH * T])
        ss = sb("ss", [P, 136])
        ms = sb("ms", [P, 136])
        rs = sb("rs", [P, 136])
        half = sb("half", [P, 64])
        cols = sb("cols", [P, 2, T, MH])
        nd = sb("nd", [P, T, MD + 1])
        den = sb("den", [P, 2, T])
        trig = sb("trig", [P, 2, T, ROPE // 2])
        ang = sb("ang", [P, 4, T, ROPE // 2])
        posi = sb("posi", [P, T], I32)
        posf = sb("posf", [P, T])
        mx = sb("mx", [P, 8])
        lg = sb("lg", [P, T, RW])
        r1 = sb("r1", [P, 6, T, NE])
        rsm = sb("rsm", [P, 16, T])
        gate = sb("gate", [P, T, NE])
        ones = sb("ones", [P, P])
        places = sb("places", [P, 4, NE])
        slot = sb("slot", [P, T, 2], I32)
        slotf = sb("slotf", [P, T, 2])
        info = sb("info", [P, T, 2, 4], I32)
        nowhere = sb("nowhere", [P, NBLK, 4], I32)
        table = sb("table", [P, NBLK, 4], I32)
        blkf = sb("blkf", [P, NBLK])
        blke = sb("blke", [P, NBLK], I32)
        tok_ix = sb("tok_ix", [P, 2], I32)
        out_ix = sb("out_ix", [P, 2], I32)
        out_gate = sb("out_gate", [P, 2])
        xn_rows = nc.dram_tensor("xn_rows", (S, D), F32, kind="Internal").ap()
        slot_rows = nc.dram_tensor("slot_rows", (NBLK * P, 4), I32, kind="Internal").ap()
        y_rows = nc.dram_tensor("y_rows", (2 * S, D), F32, kind="Internal").ap()

        headT = work[0:AQ, 0, :, :]
        prob = work[:, 1, 0:2, :]
        probT = work[:, 1, 2:4, :]
        cT = actT[:, 0:3, :]
        headsq = actT[:, :, :].rearrange("p k s -> p (k s)")[:, 0:T * AH * AQ].rearrange(
            "p (t h d) -> p t h d", t=T, h=AH)
        rows = actT[0:MH, 3:8, :]
        rp = actT[:, :, :].rearrange("p k s -> p (k s)")[:, 0:4 * T * AH * ROPE // 2].rearrange(
            "p (n t h d) -> p n t h d", n=4, t=T, h=AH)
        nat_flat = nat[:, :, :].rearrange("p t d -> p (t d)")
        xg = nat_flat[:, 0:2 * D].rearrange("p (q d) -> p q d", q=2)
        xgT = nat_flat[:, 2 * D:4 * D].rearrange("p (q k s) -> p q k s", q=2, k=KD)
        proj_flat = proj[:, :, :].rearrange("p t n -> p (t n)")
        yo = proj_flat[:, 0:2 * D].rearrange("p (q d) -> p q d", q=2)
        cmp = proj_flat[:, 2 * D:2 * D + NBLK * NE].rearrange("p (b e) -> p b e", b=NBLK)
        th = ebuf[:, 0, :].rearrange("p (q f) -> p q f", q=2)
        hid = ebuf[:, 1, :].rearrange("p (q f) -> p q f", q=2)
        hidT = va[:, :, :, :].rearrange("p t h d -> p (t h d)")[:, 0:4 * P].rearrange("p (q f s) -> p q f s", q=2, f=2)
        yb = work[:, :, :, :].rearrange("p q t s -> p q (t s)")
        ident = cn[:, CN["ident"]:CN["ident"] + P]
        upper = cn[:, CN["upper"]:CN["upper"] + P]
        neg = cn[:, CN["neg"]:CN["neg"] + P]
        w4 = cn[:, CN["w4"]:CN["w4"] + NG]
        w32 = cn[:, CN["w32"]:CN["w32"] + NE]
        freq = cn[:, CN["freq"]:CN["freq"] + ROPE // 2]

        supper = cn[:, CN["supper"]:CN["supper"] + P]

        sg = Signals(nc, sems, "b1_", PER1)
        banks = Banks(nc, ctx, "b1_", sg, PLAN1, BANK1)
        psum = banks.psum
        did, after = sg.did, sg.after
        filled, emptied, vacant = banks.filled, banks.emptied, banks.vacant
        reader, writer = banks.reader, banks.writer

        def loaded(n):
            return f"w_in{n % 3}", 16 * (n // 3 + 1)

        last_use = [("qk", 3), ("qk", 7)] + [("nat", c * T + T - 1) for c in range(NCH)] + [("wo", 6), ("wo", 7)]

        block = ctx.enter_context(nc.Block())

        @block.sync
        def _(sp):
            sp.dma_start(cn[:, :], A["consts"][:, 0:CN["lvl"]]).then_inc(*did("const", 16))
            sp.dma_start(posi[:, :], A["positions"]).then_inc(*did("const", 16))
            for i in range(T):
                sp.dma_start(x[:, i, :], A["x"][i * P:(i + 1) * P, :]).then_inc(*did("x_in", 16))
            for l in range(L):
                if l:
                    sp.wait_ge(*emptied(l - 1, "route"))
                    sp.wait_ge(*after(l - 1, "block_experts", 1))
                    sp.wait_ge(sg.sem("moe_xgT"), 2 * NPAIR * l)
                sp.dma_start(prm[:, :], A["pc"][l]).then_inc(*did("prm", 16))
                sp.dma_start(prb[:, :], A["pb"][l]).then_inc(*did("prm", 16))
                win = A["w_in"][l].rearrange("(k p) n -> p k n", p=P)
                wout = A["w_out"][l].rearrange("(k p) n -> p k n", p=P)

                def load(n, src, width):
                    if n >= 3:
                        sp.wait_ge(*filled(l, *last_use[n - 3]))
                    elif l:
                        sp.wait_ge(sg.sem("moe_y"), 2 * NPAIR * l)
                    sp.dma_start(ring[n % 3][:, 0:KD * width].rearrange("p (k n) -> p k n", k=KD),
                                 src).then_inc(*did(f"w_in{n % 3}", 16))

                for c in range(2):
                    load(c, win[:, :, c * MW:(c + 1) * MW], MW)
                for c in range(NCH):
                    load(2 + c, win[:, :, NAT0 + c * NCW:NAT0 + (c + 1) * NCW], NCW)
                sp.dma_start(w_uq[:, :, :], A["a_w_uq"][l].rearrange("(k p) n -> p k n", p=P)).then_inc(*did("w_small", 16))
                sp.dma_start(w_ukv[:, :], A["a_w_ukv"][l]).then_inc(*did("w_small", 16))
                sp.dma_start(w_s[:, :, :], A["c_w_s"][l].rearrange("g t s -> t g s")).then_inc(*did("w_small", 16))
                sp.dma_start(w_r[:, :, :], A["w_r"][l].rearrange("(k p) n -> p k n", p=P)).then_inc(*did("w_small", 16))
                for c in range(2):
                    load(6 + c, wout[:, :, c * 512:(c + 1) * 512], 512)
                for i in range(T):
                    sp.wait_ge(*after(l, "fn", i + 1))
                    sp.dma_start(xn_rows[i * P:(i + 1) * P, :], nat[:, i, :]).then_inc(*did("xn_out", 16))
                sp.wait_ge(*after(0, "nowhere", 1))
                table_rows = slot_rows.rearrange("(b p) c -> p b c", p=P)
                sp.dma_start(table_rows, nowhere[:, :, :]).then_inc(*did("table_clear", 16))
                for n in range(5, 8):
                    sp.wait_ge(*filled(l, *last_use[n]))

                def w13(row, q):
                    w = ring[q][:, :].rearrange("p (k c n) -> p k c n", c=2, k=KD)
                    for c, name in enumerate(("w1", "w3")):
                        src = A[name].rearrange("m (k p) n -> m p k n", p=P)[bass.ds(row, 1)]
                        sp.dma_start(w[:, :, c, :], src.rearrange("m p k n -> (m p) k n")).then_inc(
                            sg.sem(f"moe_w13_{q}"), 16)

                def w2(row, q):
                    w = ring[2][:, q * 2048:(q + 1) * 2048].rearrange("p (f n) -> p f n", f=2)
                    src = A["w2"].rearrange("m (f p) n -> m p f n", p=P)[bass.ds(row, 1)]
                    sp.dma_start(w, src.rearrange("m p f n -> (m p) f n")).then_inc(sg.sem(f"moe_w2_{q}"), 16)

                def expert_row(b):
                    return sp.value_load(blke[0:1, b:b + 1] if isinstance(b, int) else blke[0:1, bass.ds(b, 1)],
                                         min_val=0, max_val=NE - 1) + l * NE

                sp.wait_ge(*after(l, "block_experts", 1))
                rows_0 = [expert_row(q) for q in range(2)]
                for q in range(2):
                    w13(rows_0[q], q)
                sp.wait_ge(*after(l, "slots_put", 16 * 2 * T))
                sp.dma_start(table[:, :, :], table_rows).then_inc(*did("table_in", 16))
                for q in range(2):
                    w2(rows_0[q], q)
                with sp.Fori(1, NPAIR) as pair:
                    rows_q = [expert_row(2 * pair + q) for q in range(2)]
                    for q in range(2):
                        sp.wait_ge(sg.sem("moe_h"), 2 * pair + (2 * l * NPAIR + q - 1))
                        w13(rows_q[q], q)
                    for q in range(2):
                        sp.wait_ge(sg.sem("moe_y"), 2 * pair + (2 * l * NPAIR + q - 1))
                        w2(rows_q[q], q)
                for q in range(2):
                    sp.wait_ge(sg.sem(f"moe_scattered{q}"), 16 * NPAIR * (l + 1))
                for i in range(T):
                    if i >= 2:
                        sp.wait_ge(*after(l, "y_added", i - 1))
                    sp.dma_start(yb[:, i % 2, :], y_rows.rearrange("(t p k) d -> t p (k d)", p=P, k=2)[i]).then_inc(
                        *did(f"y_in{i % 2}", 16))

        @block.tensor
        def _(pe):
            def turn(l, stage, src, ready=None):
                for k in range(KD):
                    if ready:
                        pe.wait_ge(*ready(k))
                    pe.wait_ge(*vacant(l, stage, k))
                    bank, full = writer(l, stage, k)
                    for i in range(T):
                        ins = pe.transpose(bank[:, i * P:(i + 1) * P], src[:, i, k * P:(k + 1) * P], ident)
                    ins.then_inc(*full)

            pe.wait_ge(sg.sem("const"), 32)
            for l in range(L):
                pe.wait_ge(*after(l, "xn", T))
                turn(l, "xT", nat)
                for k in range(KD):
                    pe.wait_ge(*emptied(l, "xT", k))
                for c in range(8):
                    if c % 4 == 0:
                        pe.wait_ge(*after(l, *loaded(c // 4)))
                    w = ring[c // 4][:, 0:KD * MW].rearrange("p (k n) -> p k n", k=KD)
                    pe.wait_ge(*vacant(l, "qk", c))
                    bank, full = writer(l, "qk", c)
                    for k in range(KD):
                        ins = pe.matmul(bank[0:MD, :], w[:, k, (c % 4) * MD:(c % 4 + 1) * MD], actT[:, k, :],
                                        start=k == 0, stop=k == KD - 1)
                    ins.then_inc(*full)
                for c in range(NCH):
                    pe.wait_ge(*after(l, *loaded(2 + c)))
                    w = ring[(2 + c) % 3][:, 0:KD * NCW].rearrange("p (k n) -> p k n", k=KD)
                    for i in range(T):
                        pe.wait_ge(*vacant(l, "nat", c * T + i))
                        bank, full = writer(l, "nat", c * T + i)
                        for k in range(KD):
                            ins = pe.matmul(bank[:, 0:NCW], actT[:, k, i * P:(i + 1) * P], w[:, k, :],
                                            start=k == 0, stop=k == KD - 1)
                        ins.then_inc(*full)
                for n in range(NCH * T):
                    pe.wait_ge(*emptied(l, "nat", n))
                for g, off in enumerate((O_I, O_F)):
                    pe.wait_ge(*vacant(l, "grow", g))
                    bank, full = writer(l, "grow", g)
                    for i in range(T):
                        ins = pe.transpose(bank[0:MH, i * P:(i + 1) * P], proj[:, i, off:off + MH], ident)
                    ins.then_inc(*full)
                pe.wait_ge(*after(l, "gate_mx", 1))
                pe.wait_ge(*after(l, "gate_em", 1))
                pe.wait_ge(*vacant(l, "gcol"))
                bank, full = writer(l, "gcol")
                for g, r in enumerate((0, 4)):
                    for i in range(T):
                        ins = pe.transpose(bank[:, (g * T + i) * MH:(g * T + i + 1) * MH],
                                           rows[:, r, i * P:(i + 1) * P], ident[0:MH, 0:MH])
                ins.then_inc(*full)
                pe.wait_ge(*after(l, "cqn", 2 * T))
                for k in range(3):
                    pe.wait_ge(*vacant(l, "cT", k))
                    bank, full = writer(l, "cT", k)
                    for i in range(T):
                        off = O_CQ + k * P
                        ins = pe.transpose(bank[:, i * P:(i + 1) * P], proj[:, i, off:off + P], ident)
                    ins.then_inc(*full)
                pe.wait_ge(*after(l, "w_small", 64))
                for k in range(3):
                    pe.wait_ge(*emptied(l, "cT", k))
                for i in range(T):
                    for c in range(2):
                        pe.wait_ge(*vacant(l, "uq", 2 * i + c))
                        bank, full = writer(l, "uq", 2 * i + c)
                        for k in range(2):
                            ins = pe.matmul(bank[:, 0:288], cT[:, k, i * P:(i + 1) * P],
                                            w_uq[:, k, c * 288:(c + 1) * 288], start=k == 0, stop=k == 1)
                        ins.then_inc(*full)
                for i in range(T):
                    for c in range(2):
                        pe.wait_ge(*vacant(l, "ukv", 2 * i + c))
                        bank, full = writer(l, "ukv", 2 * i + c)
                        pe.matmul(bank[:, 0:384], cT[:, 2, i * P:(i + 1) * P],
                                  w_ukv[:, c * 384:(c + 1) * 384], start=True, stop=True).then_inc(*full)
                pe.wait_ge(*vacant(l, "wsT"))
                bank, full = writer(l, "wsT")
                for g in range(CG):
                    ins = pe.transpose(bank[:, g * P:(g + 1) * P], w_s[:, g, :], ident)
                ins.then_inc(*full)
                pe.wait_ge(*emptied(l, "wsT"))
                pe.wait_ge(*after(l, "cvn", 1))
                for g2 in range(2):
                    pe.wait_ge(*vacant(l, "csg", g2))
                    bank, full = writer(l, "csg", g2)
                    for g in range(2):
                        o = O_CV + (2 * g2 + g) * CD
                        ins = pe.matmul(bank[:, g * T * CD:(g + 1) * T * CD].rearrange("p (t d) -> p t d", t=T),
                                        w_sT[:, 2 * g2 + g, :], proj[:, :, o:o + CD], start=True, stop=True)
                    ins.then_inc(*full)
                pe.wait_ge(*after(l, "qk_silu", 8))
                pe.wait_ge(*after(l, "vaug", 1))
                def m_scores(h):
                    pe.wait_ge(*vacant(l, f"m{h}", 0))
                    bank, full = writer(l, f"m{h}", 0)
                    pe.matmul(bank[:, :], cn[0:MH, CN["sel"] + h * P:CN["sel"] + (h + 1) * P], rows[:, 3, :],
                              start=True, stop=True).then_inc(*full)
                    for j in range(T):
                        pe.wait_ge(*vacant(l, f"m{h}", 1 + j))
                        bank, full = writer(l, f"m{h}", 1 + j)
                        pe.matmul(bank[:, j * P:], qkc[:, 4 + h, j * P:(j + 1) * P], qkc[:, h, j * P:],
                                  start=True, stop=True).then_inc(*full)

                def m_out(h):
                    pe.wait_ge(*after(l, "m_w", T * (h + 1)))
                    pe.wait_ge(*vacant(l, f"mo{h}"))
                    bank, full = writer(l, f"mo{h}")
                    for i in range(T):
                        for j in range(i + 1):
                            ins = pe.matmul(bank[:, i * (MD + 1):(i + 1) * (MD + 1)],
                                            work[:, h % 2, j, i * P:(i + 1) * P], vaug[:, j, h, :],
                                            start=j == 0, stop=j == i)
                    ins.then_inc(*full)

                m_scores(0)
                for h in range(MH):
                    if h + 1 < MH:
                        m_scores(h + 1)
                    m_out(h)
                pe.wait_ge(*after(l, "qk_rope", 2))

                def heads(h):
                    for c, src in enumerate((qa, ka)):
                        pe.wait_ge(*vacant(l, *turned(h, c)))
                        bank, full = writer(l, *turned(h, c))
                        for i in range(T):
                            ins = pe.transpose(bank[0:AQ, i * P:(i + 1) * P], src[:, i, h, :], ident)
                        ins.then_inc(*full)

                def scores(n):
                    h, i = divmod(n, T)
                    for c in range(2):
                        pe.wait_ge(*emptied(l, *turned(h, c)))
                    pe.wait_ge(*vacant(l, *att(n, 0)))
                    bank, full = writer(l, *att(n, 0))
                    pe.matmul(bank[:, 0:(i + 1) * P], headT[:, 2 * (h % 2), i * P:(i + 1) * P],
                              headT[:, 2 * (h % 2) + 1, 0:(i + 1) * P], start=True, stop=True).then_inc(*full)

                def turn_probs(n):
                    i = n % T
                    pe.wait_ge(*emptied(l, *att(n, 0)))
                    pe.wait_ge(*vacant(l, *att(n, 1)))
                    bank, full = writer(l, *att(n, 1))
                    for j in range(i + 1):
                        ins = pe.transpose(bank[:, j * P:(j + 1) * P], prob[:, n % 2, j * P:(j + 1) * P], ident)
                    ins.then_inc(*full)

                def values(n):
                    h, i = divmod(n, T)
                    pe.wait_ge(*emptied(l, *att(n, 1)))
                    pe.wait_ge(*vacant(l, *att(n, 2)))
                    bank, full = writer(l, *att(n, 2))
                    for j in range(i + 1):
                        ins = pe.matmul(bank[:, 0:AV], probT[:, n % 2, j * P:(j + 1) * P], va[:, j, h, :],
                                        start=j == 0, stop=j == i)
                    ins.then_inc(*full)

                heads(0)
                for m in range(AH * T + 2):
                    if m < AH * T:
                        scores(m)
                    if m % T == 2 and m // T + 1 < AH:
                        heads(m // T + 1)
                    if 1 <= m <= AH * T:
                        turn_probs(m - 1)
                    if m >= 2:
                        values(m - 2)
                turn(l, "yT", nat, lambda k: after(l, "y_norm" if MW <= k * P < MW + AW else "mc_norm", 1))
                for k in range(KD):
                    pe.wait_ge(*emptied(l, "yT", k))
                for c in range(2):
                    pe.wait_ge(*after(l, *loaded(6 + c)))
                for n in range(2 * T):
                    i, c = divmod(n, 2)
                    w = ring[(6 + c) % 3][:, :].rearrange("p (k n) -> p k n", k=KD)
                    pe.wait_ge(*vacant(l, "wo", n))
                    bank, full = writer(l, "wo", n)
                    for k in range(KD):
                        ins = pe.matmul(bank[:, :], actT[:, k, i * P:(i + 1) * P], w[:, k, :],
                                        start=k == 0, stop=k == KD - 1)
                    ins.then_inc(*full)
                pe.wait_ge(*after(l, "fn", T))
                turn(l, "fT", nat)
                for k in range(KD):
                    pe.wait_ge(*emptied(l, "fT", k))
                pe.wait_ge(*vacant(l, "route"))
                bank, full = writer(l, "route")
                for i in range(T):
                    for k in range(KD):
                        ins = pe.matmul(bank[:, i * RW:(i + 1) * RW], actT[:, k, i * P:(i + 1) * P], w_r[:, k, :],
                                        start=k == 0, stop=k == KD - 1)
                ins.then_inc(*full)
                pe.wait_ge(*after(l, "choices", 1))
                pe.wait_ge(*after(0, "ones", 1))
                pe.wait_ge(*vacant(l, "places"))
                bank, full = writer(l, "places")
                for i in range(T + 1):
                    for j in range(min(i + 1, T)):
                        ins = pe.matmul(bank[:, i * NE:(i + 1) * NE], supper if j == i else ones[:, :],
                                        r1[:, 2, j, :], start=j == 0, stop=j == min(i, T - 1))
                ins.then_inc(*full)
                for b in range(8):
                    pe.wait_ge(sg.sem(f"bank_free{b}"), (l + 1) * BANK1[b])
                with pe.Fori(0, NPAIR) as pair:
                    n2 = 2 * l * NPAIR + 1
                    def turn_hidden(q):
                        for f in range(2):
                            ins = pe.transpose(psum[6 + q][:, f * P:(f + 1) * P], hid[:, q, f * P:(f + 1) * P], ident)
                        ins.then_inc(sg.sem("moe_hid_turned"), 1)

                    for q in range(2):
                        pe.wait_ge(sg.sem(f"moe_gathered{q}"), 16 * pair + 16 * (l * NPAIR + 1))
                        if q == 0:
                            pe.wait_ge(sg.sem("moe_y_out"), 2 * pair + n2)
                        for k in range(KD):
                            ins = pe.transpose(psum[6 * q + k // 4][:, (k % 4) * P:(k % 4 + 1) * P],
                                               xg[:, q, k * P:(k + 1) * P], ident)
                            if k == 3:
                                ins.then_inc(sg.sem("moe_half"), 1)
                        ins.then_inc(sg.sem("moe_turned"), 1)
                    for q in range(2):
                        pe.wait_ge(sg.sem(f"moe_w13_{q}"), 32 * pair + 32 * (l * NPAIR + 1))
                        pe.wait_ge(sg.sem("moe_xgT"), 2 * pair + (n2 + q))
                        for k in range(KD):
                            if q == 1 and k == KD // 2:
                                pe.wait_ge(sg.sem("moe_hid"), 2 * pair + n2)
                                turn_hidden(0)
                            ins = pe.matmul(psum[4 + q][:, :], xgT[:, q, k, :], ring[q][:, k * 512:(k + 1) * 512],
                                            start=k == 0, stop=k == KD - 1)
                        ins.then_inc(sg.sem("moe_h"), 1)
                    for q in range(2):
                        pe.wait_ge(sg.sem(f"moe_w2_{q}"), 16 * pair + 16 * (l * NPAIR + 1))
                        pe.wait_ge(sg.sem("moe_hidT"), 2 * pair + (n2 + q))
                        if q == 1:
                            pe.wait_ge(sg.sem("moe_y_out"), 2 * pair + (n2 + 1))
                        w = ring[2][:, q * 2048:(q + 1) * 2048].rearrange("p (f n) -> p f n", f=2)
                        for c in range(2):
                            if q == 0 and c == 1:
                                pe.wait_ge(sg.sem("moe_hid"), 2 * pair + (n2 + 1))
                                turn_hidden(1)
                            for f in range(2):
                                ins = pe.matmul(psum[2 * q + c][:, :], hidT[:, q, f, :],
                                                w[:, f, c * 512:(c + 1) * 512], start=f == 0, stop=f == 1)
                        ins.then_inc(sg.sem("moe_y"), 1)

        R_X, R_C, R_V, R_Q, R_K, R_Y, R_F = 0, 4, 12, 28, 52, 76, 132

        @block.scalar
        def _(act):
            chain = [0]

            def link(ins):
                chain[0] += 1
                ins.then_inc(sg.sem("act_step"), 1)
                act.wait_ge(sg.sem("act_step"), chain[0])

            def squares(src, i, n, at=0):
                return act.activation(nat[:, i, at:at + src.shape[1]], src, ACT.Square, accum_out=ss[:, n:n + 1])

            def gains(l, stage, offset):
                for k in range(0, KD, 2):
                    act.wait_ge(*filled(l, stage, k))
                    bank, free = reader(l, stage, k)
                    act.activation(actT[:, k, :], bank[:, :], ACT.Identity,
                                   scale=prm[:, offset + k:offset + k + 1]).then_inc(*free)

            act.memzero(mx[:, 4:5]).then_inc(sg.sem("moe_y_out"), 2)
            act.wait_ge(*after(0, "angles", 1))
            act.activation(trig[:, 0, :, :], ang[:, 3, :, :], ACT.Sin)
            act.activation(trig[:, 1, :, :], ang[:, 1, :, :], ACT.Sin).then_inc(*did("trig"))
            act.wait_ge(sg.sem("x_in"), 16 * T)
            for l in range(L):
                act.wait_ge(*after(l, "prm", 32))
                for i in range(T):
                    if l:
                        act.wait_ge(*after(l - 1, "y_added", i + 1))
                    squares(x[:, i, :], i, R_X + i).then_inc(*did("ss_x"))
                gains(l, "xT", PC["attn"])
                for c in range(8):
                    act.wait_ge(*after(l, "qk_conv", c + 1))
                    if c >= 2:
                        act.wait_ge(*after(l, "qk_silu", c - 1))
                    act.activation(ebuf[0:MD, c % 2, :], qkc[:, c, :], ACT.Tanh, scale=0.5).then_inc(*did("qk_tanh"))
                for n in range(NCH * T):
                    c, i = divmod(n, T)
                    act.wait_ge(*filled(l, "nat", n))
                    bank, free = reader(l, "nat", n)
                    act.activation(proj[:, i, c * NCW:(c + 1) * NCW], bank[:, 0:NCW], ACT.Copy).then_inc(*free)
                for n in range(NCH * T):
                    act.wait_ge(*emptied(l, "nat", n))
                act.wait_ge(*after(l, "gate_abs", 1))
                link(act.activation(rows[:, 4, :], rows[:, 4, :], ACT.Exp))
                act.activation(rows[:, 4, :], rows[:, 4, :], ACT.Ln, bias=1.0).then_inc(*did("gate_ln"))
                for i in range(T):
                    squares(proj[:, i, O_CQ:O_CQ + QR], i, R_C + 2 * i)
                    ins = squares(proj[:, i, O_CKV:O_CKV + KVR], i, R_C + 2 * i + 1, QR)
                ins.then_inc(*did("ss_c"))
                act.wait_ge(*after(l, "gate_mx", 1))
                act.activation(rows[:, 4, :], rows[:, 4, :], ACT.Exp).then_inc(*did("gate_em"))
                act.activation(proj[:, :, O_MO:O_MO + MW], proj[:, :, O_MO:O_MO + MW], ACT.Tanh,
                               scale=0.5).then_inc(*did("mo_tanh"))
                act.wait_ge(*after(l, "gelu_arg", 1))
                act.activation(work[:, 0, :, :], work[:, 0, :, :], ACT.Tanh,
                               scale=float(np.sqrt(2 / np.pi))).then_inc(*did("gelu_tanh"))
                for k in range(3):
                    act.wait_ge(*filled(l, "cT", k))
                    bank, free = reader(l, "cT", k)
                    act.activation(cT[:, k, :], bank[:, :], ACT.Identity,
                                   scale=prm[:, PC["qg"] + k:PC["qg"] + k + 1]).then_inc(*free)
                for n in range(2 * T):
                    i, c = divmod(n, 2)
                    act.wait_ge(*filled(l, "uq", n))
                    bank, free = reader(l, "uq", n)
                    act.activation(qa[:, i, 3 * c:3 * c + 3, :],
                                   bank[:, 0:288].rearrange("p (h d) -> p h d", h=3), ACT.Copy).then_inc(*free)
                for n in range(2 * T):
                    i, c = divmod(n, 2)
                    act.wait_ge(*filled(l, "ukv", n))
                    bank, free = reader(l, "ukv", n)
                    kv = bank[:, 0:384].rearrange("p (h d) -> p h d", h=3)
                    act.activation(ka[:, i, 3 * c:3 * c + 3, 0:NOPE], kv[:, :, 0:NOPE], ACT.Copy)
                    act.activation(va[:, i, 3 * c:3 * c + 3, :], kv[:, :, NOPE:], ACT.Copy).then_inc(*free)
                act.wait_ge(*filled(l, "wsT"))
                bank, free = reader(l, "wsT")
                act.activation(w_sT[:, :, :], bank[:, :].rearrange("p (g s) -> p g s", g=CG), ACT.Copy).then_inc(*did("wsT_raw"))
                for n in range(2 * T):
                    act.wait_ge(*emptied(l, "ukv", n))
                act.wait_ge(*after(l, "k_rope", 1))
                act.activation(headsq, qa[:, :, :, :], ACT.Square).then_inc(*did("qk_sq"))
                act.wait_ge(*emptied(l, "gcol"))
                for h in range(MH):
                    act.wait_ge(*filled(l, f"m{h}", 0))
                    bank, free = reader(l, f"m{h}", 0)
                    for j in range(T):
                        n = h * T + j
                        if n >= 2:
                            act.wait_ge(*after(l, "m_w", n - 1))
                        ins = act.activation(ebuf[:, n % 2, j * P:], bank[:, j * P:], ACT.Exp,
                                             bias=cols[:, 0, j, h:h + 1])
                        if j < T - 1:
                            ins.then_inc(*did("m_e"))
                    ins.then_inc(*free)
                    if h == 0:
                        act.wait_ge(*after(l, "ss_q", 1))
                        act.activation(headsq, ka[:, :, :, :], ACT.Square).then_inc(*did("qk_sq"))
                    if h == MH - 2:
                        act.wait_ge(*after(l, "rs_k", 1))
                        for i in range(T):
                            for a in range(AH):
                                at = R_K + i * AH + a
                                ins = act.activation(ka[:, i, a, :], ka[:, i, a, :], ACT.Identity,
                                                     scale=rs[:, at:at + 1])
                        ins.then_inc(*did("k_scaled"))

                def turned_q(h):
                    if h >= 2:
                        act.wait_ge(*filled(l, *att((h - 1) * T - 1, 0)))
                    act.wait_ge(*filled(l, *turned(h, 0)))
                    bank, free = reader(l, *turned(h, 0))
                    act.activation(headT[:, 2 * (h % 2), :], bank[0:AQ, :], ACT.Copy).then_inc(*free)

                turned_q(0)
                for n in range(AH * T):
                    i = n % T
                    act.wait_ge(*after(l, "a_max", n + 1))
                    if n >= 2:
                        act.wait_ge(*filled(l, *att(n - 2, 1)))
                    bank, free = reader(l, *att(n, 0))
                    act.activation(prob[:, n % 2, 0:(i + 1) * P], bank[:, 0:(i + 1) * P], ACT.Exp,
                                   bias=asum[:, 0, n:n + 1], scale=AQ ** -0.5,
                                   accum_out=asum[:, 1, n:n + 1]).then_inc(*free)
                    if i == 2 and n // T + 1 < AH:
                        turned_q(n // T + 1)
                gains(l, "yT", PC["mix"])
                for i in range(T):
                    for c in range(2):
                        act.wait_ge(*emptied(l, "wo", 2 * i + c))
                    squares(x[:, i, :], i, R_F + i).then_inc(*did("ss_f"))
                gains(l, "fT", PC["ffn"])
                act.wait_ge(*after(l, "r_shift", 1))
                act.activation(rg[:, 4, :, :], rg[:, 4, :, :], ACT.Exp)
                act.activation(r1[:, 4, :, :], r1[:, 4, :, :], ACT.Exp).then_inc(*did("r_exp"))
                with act.Fori(0, NPAIR) as pair:
                    n2 = 2 * l * NPAIR + 1
                    for q in range(2):
                        act.wait_ge(sg.sem("moe_h"), 2 * pair + (n2 + q))
                        act.activation(th[:, q, :], psum[4 + q][:, 0:FE], ACT.Tanh, scale=0.5).then_inc(
                            sg.sem("moe_tanh"), 1)
                        act.wait_ge(sg.sem("moe_hid_turned"), 2 * pair + (n2 + q))
                        act.activation(hidT[:, q, :, :], psum[6 + q][:, 0:FE].rearrange("p (f s) -> p f s", f=2),
                                       ACT.Copy).then_inc(sg.sem("moe_hidT"), 1)
                    for q in range(2):
                        act.wait_ge(sg.sem("moe_out_ix"), 2 * pair + (n2 + q))
                        act.wait_ge(sg.sem("moe_y"), 2 * pair + (n2 + q))
                        for c in range(2):
                            ins = act.activation(yo[:, q, c * 512:(c + 1) * 512], psum[2 * q + c][:, :],
                                                 ACT.Identity, scale=out_gate[:, q:q + 1])
                        ins.then_inc(sg.sem("moe_y_out"), 1)

        @block.gpsimd
        def _(pool):
            chain = [0]

            def link(ins):
                chain[0] += 1
                ins.then_inc(sg.sem("pool_step"), 1)
                pool.wait_ge(sg.sem("pool_step"), chain[0])

            def rsqrt(at, n, scale, eps=EPS):
                link(pool.tensor_scalar(ms[:, at:at + n], ss[:, at:at + n], scale, eps, ALU.mult, ALU.add))
                return pool.tensor_tensor(rs[:, at:at + n], ms[:, at:at + n], half[:, 0:n], ALU.pow)

            pool.memset(ones[:, :], 1.0).then_inc(*did("ones"))
            pool.memset(nowhere[:, :, :], NOWHERE).then_inc(*did("nowhere"))
            link(pool.memset(half[:, :], -0.5))
            link(pool.memset(vaug[:, :, :, MD:MD + 1], 1.0))
            for l in range(L):
                for i in range(T):
                    pool.wait_ge(*after(l, "ss_x", i + 1))
                    rsqrt(R_X + i, 1, 1.0 / D).then_inc(*did("rs_x"))
                for n in range(NCH * T):
                    pool.wait_ge(*emptied(l, "nat", n))
                if l:
                    pool.wait_ge(*after(l - 1, "m_h", MH))
                pool.tensor_copy(vaug[:, :, :, 0:MD],
                                 proj[:, :, O_MV:O_MV + MW].rearrange("p t (h d) -> p t h d", h=MH)).then_inc(*did("vaug"))
                pool.wait_ge(*after(l, "ss_c", 1))
                c2 = ms[:, R_C:R_C + 8].rearrange("p (t c) -> p t c", c=2)
                s2 = ss[:, R_C:R_C + 8].rearrange("p (t c) -> p t c", c=2)
                pool.tensor_scalar(c2[:, :, 0], s2[:, :, 0], 1.0 / QR, EPS, ALU.mult, ALU.add)
                link(pool.tensor_scalar(c2[:, :, 1], s2[:, :, 1], 1.0 / KVR, EPS, ALU.mult, ALU.add))
                pool.tensor_tensor(rs[:, R_C:R_C + 8], ms[:, R_C:R_C + 8], half[:, 0:8], ALU.pow).then_inc(*did("rs_c"))
                uv = proj[:, :, O_CU:O_CU + 2 * CW]
                if l:
                    pool.wait_ge(*after(l - 1, "y_norm", 1))
                link(pool.tensor_tensor(work[:, 0, :, :], uv, uv, ALU.mult))
                link(pool.tensor_scalar(work[:, 0, :, :], work[:, 0, :, :], 0.044715, 1.0, ALU.mult, ALU.add))
                pool.tensor_tensor(work[:, 0, :, :], work[:, 0, :, :], uv, ALU.mult).then_inc(*did("gelu_arg"))
                pool.wait_ge(*after(l, "ss_v", 1))
                rsqrt(R_V, T * CG, 1.0 / (4 * CD)).then_inc(*did("rs_v"))
                kr = proj[:, :, O_KR:O_KR + ROPE].unsqueeze(2).to_broadcast([P, T, AH, ROPE])
                if l:
                    pool.wait_ge(*filled(l - 1, *turned(AH - 1, 1)))
                pool.tensor_copy(ka[:, :, :, NOPE:], kr).then_inc(*did("k_rope"))
                for name, at in (("q", R_Q), ("k", R_K)):
                    pool.wait_ge(*after(l, f"ss_{name}", 1))
                    rsqrt(at, T * AH, 1.0 / AQ).then_inc(*did(f"rs_{name}"))
                def norms(at, n_heads, g0, g1, d):
                    s_n, m_n, r_n = (a[:, at:at + T * n_heads].rearrange("p (t g) -> p t g", t=T)[:, :, g0:g1]
                                     for a in (ss, ms, rs))
                    link(pool.tensor_scalar(m_n, s_n, 1.0 / d, EPS, ALU.mult, ALU.add))
                    h_n = half[:, 0:T * (g1 - g0)].rearrange("p (t g) -> p t g", t=T)
                    return pool.tensor_tensor(r_n, m_n, h_n, ALU.pow)

                pool.wait_ge(*after(l, "ss_y", 2))
                link(norms(R_Y, MH, 0, MH, MD))
                link(norms(R_Y + T * MH, AH + CG, AH, AH + CG, CD))
                for t in range(T):
                    for y_t, at in ((nat[:, t, 0:MW].rearrange("p (g d) -> p g d", g=MH), R_Y + t * MH),
                                    (nat[:, t, MW + AW:].rearrange("p (g d) -> p g d", g=CG),
                                     R_Y + T * MH + t * (AH + CG) + AH)):
                        g, d = y_t.shape[1], y_t.shape[2]
                        ins = pool.tensor_tensor(y_t, y_t, rs[:, at:at + g].unsqueeze(2).to_broadcast([P, g, d]),
                                                 ALU.mult)
                ins.then_inc(*did("mc_norm"))
                pool.wait_ge(*after(l, "ss_y", 3))
                norms(R_Y + T * MH, AH + CG, 0, AH, AV).then_inc(*did("rs_y"))
                for i in range(T):
                    pool.wait_ge(*after(l, "ss_f", i + 1))
                    rsqrt(R_F + i, 1, 1.0 / D).then_inc(*did("rs_f"))
                pool.wait_ge(*after(l, "slots", 1))
                pool.wait_ge(*after(l, "table_clear", 16))
                for i in range(T):
                    for k in range(2):
                        pool.indirect_dma_start(
                            out=slot_rows, out_offset=bass.IndirectOffsetOnAxis(ap=slot[:, i, k:k + 1], axis=0),
                            in_=info[:, i, k, :], in_offset=None, bounds_check=NBLK * P - 1,
                            oob_is_err=False).then_inc(*did("slots_put", 16))
                pool.wait_ge(*after(l, "table_in", 16))
                pool.wait_ge(*after(l, "xn_out", 16 * T))
                pool.wait_ge(*filled(l, "route"))

                def gather(b, q, g):
                    pool.tensor_copy(tok_ix[:, q:q + 1], table[:, bass.ds(b, 1), 0]).then_inc(
                        sg.sem("moe_tok_ix"), 1)
                    pool.wait_ge(sg.sem("moe_tok_ix"), g)
                    pool.sem_inc(sg.sem("moe_issued"), 1)
                    pool.indirect_dma_start(
                        out=xg[:, q, :], out_offset=None, in_=xn_rows,
                        in_offset=bass.IndirectOffsetOnAxis(ap=tok_ix[:, q:q + 1], axis=0),
                        bounds_check=S - 1, oob_is_err=False).then_inc(sg.sem(f"moe_gathered{q}"), 16)

                def scatter(q):
                    pool.indirect_dma_start(
                        out=y_rows, out_offset=bass.IndirectOffsetOnAxis(ap=out_ix[:, q:q + 1], axis=0),
                        in_=yo[:, q, :], in_offset=None, bounds_check=2 * S - 1,
                        oob_is_err=False).then_inc(sg.sem(f"moe_scattered{q}"), 16)

                def outputs(b, q):
                    pool.tensor_copy(out_ix[:, q:q + 1], table[:, bass.ds(b, 1), 1])
                    pool.tensor_copy(out_gate[:, q:q + 1],
                                     table[:, bass.ds(b, 1), 2].bitcast(F32)).then_inc(
                        sg.sem("moe_out_ix"), 1)

                n2 = 2 * l * NPAIR + 1
                for q in range(2):
                    gather(q, q, n2 + q)
                for q in range(2):
                    outputs(q, q)
                with pool.Fori(1, NPAIR) as pair:
                    block_of = [pool.snap(2 * pair + q) for q in range(2)]
                    for q in range(2):
                        pool.wait_ge(sg.sem("moe_turned"), 2 * pair + (n2 - 2 + q))
                        gather(block_of[q], q, 2 * pair + (n2 + q))
                    for q in range(2):
                        pool.wait_ge(sg.sem("moe_y_out"), 2 * pair + (n2 + q))
                        pool.sem_inc(sg.sem("moe_issued"), 1)
                        scatter(q)
                    for q in range(2):
                        pool.wait_ge(sg.sem(f"moe_scattered{q}"), 16 * pair + 16 * l * NPAIR)
                        outputs(block_of[q], q)
                for q in range(2):
                    pool.wait_ge(sg.sem("moe_y_out"), 2 * NPAIR * (l + 1) + 1 + q)
                    scatter(q)

        @block.vector
        def _(dve):
            chain = [0]

            def link(ins):
                chain[0] += 1
                ins.then_inc(sg.sem("dve_step"), 1)
                dve.wait_ge(sg.sem("dve_step"), chain[0])

            def tt(out, a, b, op):
                return dve.tensor_tensor(out, a, b, op)

            def ts(out, a, s1, s2=None, op0=ALU.mult, op1=None):
                return dve.tensor_scalar(out, a, s1, s2, op0, op1) if op1 is not None else dve.tensor_scalar(out, a, s1, None, op0)

            def stt(out, a, s, b, op0, op1):
                return dve.scalar_tensor_tensor(out=out, in0=a, scalar=s, in1=b, op0=op0, op1=op1)

            def bc(ap, n):
                return ap.unsqueeze(len(ap.shape)).to_broadcast([*ap.shape, n])

            def gains(l, stage, offset):
                for k in range(1, KD, 2):
                    dve.wait_ge(*filled(l, stage, k))
                    bank, free = reader(l, stage, k)
                    ts(actT[:, k, :], bank[:, :], prm[:, offset + k:offset + k + 1]).then_inc(*free)

            def group_squares(dst, src, tmp):
                link(tt(tmp, src, src, ALU.mult))
                return dve.tensor_reduce(dst, tmp, AX.X, ALU.add)

            dve.wait_ge(*after(0, "const", 32))
            tokens = cn[:, CN["tok"]:CN["tok"] + T]
            link(dve.memset(info[:, :, :, :], 0))
            for k in range(2):
                link(dve.tensor_copy(info[:, :, k, 0], tokens))
                link(ts(slotf[:, :, k], tokens, 2.0, float(k), ALU.mult, ALU.add))
            link(dve.tensor_copy(info[:, :, :, 1], slotf[:, :, :]))
            link(dve.tensor_copy(posf[:, :], posi[:, :]))
            for i in range(T):
                link(ts(ang[:, 0, i, :], freq, posf[:, i:i + 1]))
            magic = 12582912.0
            link(ts(ang[:, 2, :, :], ang[:, 0, :, :], float(1 / (2 * np.pi)), magic, ALU.mult, ALU.add))
            link(ts(ang[:, 2, :, :], ang[:, 2, :, :], magic, None, ALU.subtract))
            for k, c in enumerate((6.28125, 0.0019350051879882812, 3.0199159819e-07)):
                link(stt(ang[:, 1, :, :], ang[:, 2, :, :], -c, ang[:, 0 if k == 0 else 1, :, :], ALU.mult, ALU.add))
            pi = 3.1415925
            link(ts(ang[:, 3, :, :], ang[:, 1, :, :], float(np.pi / 2), None, ALU.add))
            link(ts(ang[:, 2, :, :], ang[:, 3, :, :], pi, None, ALU.is_gt))
            link(stt(ang[:, 3, :, :], ang[:, 2, :, :], float(-2 * np.pi), ang[:, 3, :, :], ALU.mult, ALU.add))
            link(ts(ang[:, 1, :, :], ang[:, 1, :, :], pi, -pi, ALU.min, ALU.max))
            ts(ang[:, 3, :, :], ang[:, 3, :, :], pi, -pi, ALU.min, ALU.max).then_inc(*did("angles"))
            dve.wait_ge(sg.sem("x_in"), 16 * T)
            for l in range(L):
                dve.wait_ge(*after(l, "prm", 32))
                for i in range(T):
                    dve.wait_ge(*after(l, "rs_x", i + 1))
                    ts(nat[:, i, :], x[:, i, :], rs[:, R_X + i:R_X + i + 1]).then_inc(*did("xn"))
                gains(l, "xT", PC["attn"])

                def silu(c):
                    dve.wait_ge(*after(l, "qk_tanh", c + 1))
                    stt(qkc[:, c, :], ebuf[0:MD, c % 2, :], 1.0, qkc[:, c, :], ALU.add, ALU.mult).then_inc(*did("qk_silu"))

                for c in range(8):
                    dve.wait_ge(*filled(l, "qk", c))
                    bank, free = reader(l, "qk", c)
                    w = PC["cw"] + 4 * c
                    link(ts(qkc[:, c, :], bank[0:MD, :], prm[0:MD, w + 3:w + 4],
                            prm[0:MD, PC["cbias"] + c:PC["cbias"] + c + 1], ALU.mult, ALU.add))
                    for d in range(1, 4):
                        ins = stt(qkc[:, c, d:], bank[0:MD, 0:S - d], prm[0:MD, w + 3 - d:w + 4 - d],
                                  qkc[:, c, d:], ALU.mult, ALU.add)
                        if d < 3:
                            link(ins)
                    link(ins)
                    dve.engine_nop().then_inc(*free)
                    dve.engine_nop().then_inc(*did("qk_conv"))
                    if c:
                        silu(c - 1)
                silu(7)
                dve.wait_ge(*filled(l, "grow", 0))
                bank, free = reader(l, "grow", 0)
                ts(rows[:, 0, :], bank[0:MH, :], prm[0:MH, PC["bi"]:PC["bi"] + 1], None, ALU.add).then_inc(*free)
                dve.wait_ge(*filled(l, "grow", 1))
                bank, free = reader(l, "grow", 1)
                ts(rows[:, 1, :], bank[0:MH, :], prm[0:MH, PC["bf"]:PC["bf"] + 1], None, ALU.add).then_inc(*free)
                dve.wait_ge(*emptied(l, "grow", 1))
                stt(rows[:, 4, :], rows[:, 1, :], -1.0, rows[:, 1, :], ALU.mult, ALU.min).then_inc(*did("gate_abs"))
                dve.wait_ge(*after(l, "gate_ln", 1))
                link(stt(rows[:, 1, :], rows[:, 1, :], 0.0, rows[:, 4, :], ALU.min, ALU.subtract))
                link(dve.tensor_tensor_scan(rows[:, 2, :], rows[:, 1, :], rows[:, 1, :], 0.0, ALU.add, ALU.min))
                link(tt(rows[:, 0, :], rows[:, 0, :], rows[:, 2, :], ALU.subtract))
                link(dve.tensor_tensor_scan(rows[:, 3, :], rows[:, 0, :], rows[:, 0, :], 0.0, ALU.max, ALU.max))
                link(ts(rows[:, 3, :], rows[:, 3, :], -1.0))
                tt(rows[:, 4, :], rows[:, 3, :], rows[:, 2, :], ALU.subtract).then_inc(*did("gate_mx"))
                dve.wait_ge(*after(l, "rs_c", 1))
                for i in range(T):
                    for c, (o, n) in enumerate(((O_CQ, QR), (O_CKV, KVR))):
                        ts(proj[:, i, o:o + n], proj[:, i, o:o + n],
                           rs[:, R_C + 2 * i + c:R_C + 2 * i + c + 1]).then_inc(*did("cqn"))
                dve.wait_ge(*filled(l, "gcol"))
                bank, free = reader(l, "gcol")
                dve.tensor_copy(cols[:, :, :, :].rearrange("p a t h -> p (a t h)"), bank[:, 0:2 * T * MH]).then_inc(*free)
                uv = proj[:, :, O_CU:O_CU + 2 * CW]
                dve.wait_ge(*after(l, "gelu_tanh", 1))
                link(stt(uv, work[:, 0, :, :], 1.0, uv, ALU.add, ALU.mult))
                vg = proj[:, :, O_CV:O_CV + CW].rearrange("p t (g d) -> p t g d", g=CG)
                r4 = lambda at, g: rs[:, at:at + T * g].rearrange("p (t g) -> p t g", t=T)
                s4 = lambda at, g: ss[:, at:at + T * g].rearrange("p (t g) -> p t g", t=T)
                group_squares(s4(R_V, CG), vg, work[:, 1, :, 0:CW].rearrange("p t (g d) -> p t g d", g=CG)).then_inc(*did("ss_v"))
                link(ts(proj[:, :, O_CU:O_CU + CW], proj[:, :, O_CU:O_CU + CW], 0.5))
                dve.wait_ge(*after(l, "rs_v", 1))
                for t in range(T):
                    link(stt(vg[:, t], vg[:, t], 0.5, bc(r4(R_V, CG)[:, t], CD), ALU.mult, ALU.mult))
                tt(proj[:, :, O_CV:O_CV + CW], proj[:, :, O_CV:O_CV + CW],
                   prb[:, PB["cv"]:PB["cv"] + CW].unsqueeze(1).to_broadcast([P, T, CW]), ALU.mult).then_inc(*did("cvn"))
                dve.wait_ge(*after(l, "wsT_raw", 1))
                dve.wait_ge(*filled(l, "wsT"))
                _, free = reader(l, "wsT")
                tt(w_sT[:, :, :], w_sT[:, :, :], upper.unsqueeze(1).to_broadcast([P, CG, P]), ALU.mult).then_inc(*free)
                for n in range(2 * T):
                    dve.wait_ge(*emptied(l, "uq", n))
                    dve.wait_ge(*emptied(l, "ukv", n))
                dve.wait_ge(*after(l, "k_rope", 1))
                dve.wait_ge(*after(0, "trig", 1))
                def head_sums(name, at, n):
                    dve.wait_ge(*after(l, "qk_sq", n))
                    dve.tensor_reduce(s4(at, AH), headsq, AX.X, ALU.add).then_inc(*did(f"ss_{name}"))

                def head_norm(name, at, arr):
                    flat = arr[:, :, :, :].rearrange("p t h d -> p (t h) d")
                    if name == "q":
                        dve.wait_ge(*after(l, f"rs_{name}", 1))
                        link(tt(flat, flat, bc(rs[:, at:at + T * AH], AQ), ALU.mult))
                    else:
                        dve.wait_ge(*after(l, "k_scaled", 1))
                    g = prb[:, PB[name + "h"]:PB[name + "h"] + AQ].unsqueeze(1).to_broadcast([P, T * AH, AQ])
                    link(tt(flat, flat, g, ALU.mult))
                    x1, x2 = arr[:, :, :, NOPE:NOPE + 16], arr[:, :, :, NOPE + 16:]
                    c, s = (trig[:, n, :, :].unsqueeze(2).to_broadcast([P, T, AH, ROPE // 2]) for n in range(2))
                    for t in range(T):
                        tt(rp[:, 0, t], x1[:, t], c[:, t], ALU.mult)
                        tt(rp[:, 1, t], x2[:, t], s[:, t], ALU.mult)
                        tt(rp[:, 2, t], x1[:, t], s[:, t], ALU.mult)
                        link(tt(rp[:, 3, t], x2[:, t], c[:, t], ALU.mult))
                    link(tt(x1, rp[:, 0], rp[:, 1], ALU.subtract))
                    tt(x2, rp[:, 2], rp[:, 3], ALU.add).then_inc(*did("qk_rope"))

                for g2 in range(2):
                    dve.wait_ge(*filled(l, "csg", g2))
                    bank, free = reader(l, "csg", g2)
                    for g in range(2):
                        gg = 2 * g2 + g
                        ins = stt(nat[:, :, MW + AW + gg * CD:MW + AW + (gg + 1) * CD],
                                  bank[:, g * T * CD:(g + 1) * T * CD].rearrange("p (t d) -> p t d", t=T),
                                  prm[:, PC["cb"] + gg:PC["cb"] + gg + 1],
                                  proj[:, :, O_CU + gg * CD:O_CU + (gg + 1) * CD], ALU.add, ALU.mult)
                    ins.then_inc(*free)
                def m_outputs(h):
                    dve.wait_ge(*filled(l, f"mo{h}"))
                    bank, free = reader(l, f"mo{h}")
                    ts(nd[:, :, :], bank[:, 0:T * (MD + 1)].rearrange("p (t d) -> p t d", t=T),
                       MD ** -0.5 / 4).then_inc(*free)
                    dve.wait_ge(*emptied(l, f"mo{h}"))
                    link(ts(den[:, 0, :], nd[:, :, MD], -1.0))
                    link(tt(den[:, 0, :], den[:, 0, :], nd[:, :, MD], ALU.max))
                    link(tt(den[:, 0, :], den[:, 0, :], cols[:, 1, :, h], ALU.max))
                    link(ts(den[:, 0, :], den[:, 0, :], 2.0))
                    link(dve.reciprocal(den[:, 1, :], den[:, 0, :]))
                    link(tt(nd[:, :, 0:MD], nd[:, :, 0:MD], bc(den[:, 1, :], MD), ALU.mult))
                    stt(nat[:, :, h * MD:(h + 1) * MD], proj[:, :, O_MO + h * MD:O_MO + (h + 1) * MD], 1.0,
                        nd[:, :, 0:MD], ALU.add, ALU.mult).then_inc(*did("m_h"))

                dve.wait_ge(*after(l, "mo_tanh", 1))
                for h in range(MH):
                    for j in range(T):
                        n = h * T + j
                        if j < T - 1:
                            dve.wait_ge(*after(l, "m_e", h * (T - 1) + j + 1))
                        else:
                            dve.wait_ge(*emptied(l, f"m{h}", 0))
                        dve.wait_ge(*filled(l, f"m{h}", 1 + j))
                        bank, free = reader(l, f"m{h}", 1 + j)
                        stt(work[:, h % 2, j, j * P:], ebuf[:, n % 2, j * P:], 1.0, bank[:, j * P:],
                            ALU.min, ALU.mult).then_inc(*free)
                        dve.wait_ge(*emptied(l, f"m{h}", 1 + j))
                        tt(work[:, h % 2, j, j * P:(j + 1) * P], work[:, h % 2, j, j * P:(j + 1) * P],
                           upper, ALU.mult).then_inc(*did("m_w"))
                    if h == 0:
                        head_sums("q", R_Q, 1)
                    elif h == 1:
                        head_sums("k", R_K, 2)
                    elif h == 2:
                        head_norm("q", R_Q, qa)
                    else:
                        head_norm("k", R_K, ka)
                    if h < MH - 1:
                        m_outputs(h)
                def turned_k(h):
                    if h >= 2:
                        dve.wait_ge(*filled(l, *att((h - 1) * T - 1, 0)))
                    dve.wait_ge(*filled(l, *turned(h, 1)))
                    bank, free = reader(l, *turned(h, 1))
                    dve.tensor_copy(headT[:, 2 * (h % 2) + 1, :], bank[0:AQ, :]).then_inc(*free)

                def row_max(n):
                    i = n % T
                    dve.wait_ge(*filled(l, *att(n, 0)))
                    bank, _ = reader(l, *att(n, 0))
                    link(tt(bank[:, i * P:(i + 1) * P], bank[:, i * P:(i + 1) * P], neg, ALU.add))
                    link(dve.tensor_reduce(asum[:, 2, n:n + 1], bank[:, 0:(i + 1) * P], AX.X, ALU.max))
                    ts(asum[:, 0, n:n + 1], asum[:, 2, n:n + 1], -AQ ** -0.5).then_inc(*did("a_max"))

                def turned_probs(n):
                    i = n % T
                    if n >= 2:
                        dve.wait_ge(*filled(l, *att(n - 2, 2)))
                    dve.wait_ge(*filled(l, *att(n, 1)))
                    bank, free = reader(l, *att(n, 1))
                    dve.tensor_copy(probT[:, n % 2, 0:(i + 1) * P], bank[:, 0:(i + 1) * P]).then_inc(*free)
                    link(dve.reciprocal(asum[:, 3, n:n + 1], asum[:, 1, n:n + 1]))

                def attended(n):
                    h, i = divmod(n, T)
                    dve.wait_ge(*filled(l, *att(n, 2)))
                    bank, free = reader(l, *att(n, 2))
                    ts(nat[:, i, MW + h * AV:MW + (h + 1) * AV], bank[:, 0:AV], asum[:, 3, n:n + 1]).then_inc(*free)

                ym, ya, yc = (nat[:, :, o:o + g * d].rearrange("p t (g d) -> p t g d", g=g)
                              for o, g, d in ((0, MH, MD), (MW, AH, AV), (MW + AW, CG, CD)))
                sq = actT[:, :, :].rearrange("p k s -> p (k s)")
                sqm, sqc, sqa = (sq[:, T * o:T * (o + g * d)].rearrange("p (t g d) -> p t g d", t=T, g=g)
                                 for o, g, d in ((0, MH, MD), (MW, CG, CD), (MW + CW, AH, AV)))

                turned_k(0)
                for m in range(AH * T + 2):
                    if m < AH * T:
                        row_max(m)
                    if m == 0:
                        m_outputs(MH - 1)
                    if m % T == 2 and m // T + 1 < AH:
                        turned_k(m // T + 1)
                    if 1 <= m <= AH * T:
                        turned_probs(m - 1)
                    if m >= 2:
                        attended(m - 2)
                    if m == 1:
                        dve.wait_ge(*after(l, "m_h", MH))
                        group_squares(s4(R_Y, MH), ym, sqm).then_inc(*did("ss_y"))
                    elif m == 2:
                        group_squares(s4(R_Y + T * MH, AH + CG)[:, :, AH:], yc, sqc).then_inc(*did("ss_y"))
                    elif m % T == 1:
                        h = m // T - 1
                        dve.wait_ge(*emptied(l, *att(m - 2, 2)))
                        link(group_squares(s4(R_Y + T * MH, AH + CG)[:, :, h:h + 1], ya[:, :, h:h + 1],
                                           sqa[:, :, h:h + 1]))
                dve.wait_ge(*emptied(l, *att(AH * T - 1, 2)))
                dve.wait_ge(*after(l, "m_h", MH))
                dve.engine_nop().then_inc(*did("ss_y"))
                dve.wait_ge(*after(l, "rs_y", 1))
                for t in range(T):
                    ins = tt(ya[:, t], ya[:, t], bc(r4(R_Y + T * MH, AH + CG)[:, t, 0:AH], AV), ALU.mult)
                ins.then_inc(*did("y_norm"))
                gains(l, "yT", PC["mix"])
                def normed(i):
                    dve.wait_ge(*after(l, "rs_f", i + 1))
                    ts(nat[:, i, :], x[:, i, :], rs[:, R_F + i:R_F + i + 1]).then_inc(*did("fn"))

                for n in range(2 * T):
                    i, c = divmod(n, 2)
                    dve.wait_ge(*filled(l, "wo", n))
                    bank, free = reader(l, "wo", n)
                    tt(x[:, i, c * 512:(c + 1) * 512], x[:, i, c * 512:(c + 1) * 512], bank[:, :], ALU.add).then_inc(*free)
                    if c and i:
                        normed(i - 1)
                normed(T - 1)
                gains(l, "fT", PC["ffn"])
                dve.wait_ge(*filled(l, "route"))
                bank, free = reader(l, "route")
                dve.tensor_copy(lg[:, :, :], bank[:, 0:T * RW].rearrange("p (t n) -> p t n", t=T)).then_inc(*free)
                dve.wait_ge(*emptied(l, "route"))
                row = lambda ap, n: ap.unsqueeze(1).to_broadcast([P, T, n])

                def first_max(src, rank, n, eq, hot, m):
                    link(dve.tensor_reduce(m[0], src, AX.X, ALU.max))
                    link(tt(eq, src, bc(m[0], n), ALU.is_equal))
                    link(tt(eq, eq, row(rank, n), ALU.mult))
                    link(dve.tensor_reduce(m[1], eq, AX.X, ALU.max))
                    link(tt(hot, eq, bc(m[1], n), ALU.is_equal))

                m = [rsm[:, n, :] for n in range(16)]
                gl, el = lg[:, :, 0:NG], lg[:, :, NG:]
                link(tt(rg[:, 0], gl, row(prb[:, PB["bg"]:PB["bg"] + NG], NG), ALU.add))
                first_max(rg[:, 0], w4, NG, rg[:, 1], rg[:, 2], m[0:2])
                link(dve.tensor_reduce(m[2], gl, AX.X, ALU.max))
                link(tt(rg[:, 4], gl, bc(m[2], NG), ALU.subtract))
                hot8 = lambda n: r1[:, n].rearrange("p t (g e) -> p t g e", g=NG)
                link(dve.tensor_copy(hot8(0), bc(rg[:, 2], EG)))
                link(ts(r1[:, 1], r1[:, 0], BIG, -BIG, ALU.mult, ALU.add))
                link(tt(r1[:, 2], el, row(prb[:, PB["be"]:PB["be"] + NE], NE), ALU.add))
                link(tt(r1[:, 2], r1[:, 2], r1[:, 0], ALU.mult))
                link(tt(r1[:, 2], r1[:, 2], r1[:, 1], ALU.add))
                first_max(r1[:, 2], w32, NE, r1[:, 4], r1[:, 3], m[3:5])
                link(stt(r1[:, 2], r1[:, 3], -2 * BIG, r1[:, 2], ALU.mult, ALU.add))
                first_max(r1[:, 2], w32, NE, r1[:, 4], r1[:, 5], m[5:7])
                tt(r1[:, 2], r1[:, 3], r1[:, 5], ALU.add).then_inc(*did("choices"))
                link(tt(r1[:, 4], el, r1[:, 0], ALU.mult))
                link(tt(r1[:, 4], r1[:, 4], r1[:, 1], ALU.add))
                link(dve.tensor_reduce(m[7], r1[:, 4], AX.X, ALU.max))
                tt(r1[:, 4], r1[:, 4], bc(m[7], NE), ALU.subtract).then_inc(*did("r_shift"))
                dve.wait_ge(*after(l, "r_exp", 1))
                link(dve.tensor_reduce(m[8], rg[:, 4], AX.X, ALU.add))
                link(tt(rg[:, 5], rg[:, 4], rg[:, 2], ALU.mult))
                link(dve.tensor_reduce(m[9], rg[:, 5], AX.X, ALU.add))
                dve.wait_ge(*after(l, "choices", 1))
                link(tt(r1[:, 4], r1[:, 4], r1[:, 2], ALU.mult))
                link(dve.tensor_reduce(m[10], r1[:, 4], AX.X, ALU.add))
                link(tt(m[11], m[10], m[8], ALU.mult))
                link(dve.reciprocal(m[12], m[11]))
                link(stt(m[13], m[12], 0.5, m[9], ALU.mult, ALU.mult))
                link(tt(gate[:, :, :], r1[:, 4], bc(m[13], NE), ALU.mult))
                dve.wait_ge(*filled(l, "places"))
                bank, free = reader(l, "places")
                total = bank[:, T * NE:(T + 1) * NE]
                link(ts(places[:, 0, :], total, 0.0, None, ALU.is_gt))
                for n in range(1, S // P):
                    link(stt(places[:, 0, :], total, float(n * P), places[:, 0, :], ALU.is_gt, ALU.add))
                link(dve.memset(places[:, 3, :], 0.0))
                link(dve.tensor_tensor_scan(places[:, 1, :], places[:, 0, :], places[:, 3, :], 0.0, ALU.add, ALU.add))
                link(tt(cmp, places[:, 1, :].unsqueeze(1).to_broadcast([P, NBLK, NE]),
                        bc(cn[:, CN["blk"]:CN["blk"] + NBLK], NE), ALU.is_le))
                link(dve.tensor_reduce(blkf[:, :], cmp, AX.X, ALU.add))
                dve.tensor_scalar(blke[:, :], blkf[:, :], float(NE - 1), None, ALU.min).then_inc(*did("block_experts"))
                link(tt(places[:, 2, :], places[:, 1, :], places[:, 0, :], ALU.subtract))
                link(ts(places[:, 2, :], places[:, 2, :], float(P)))
                tt(r1[:, 2], bank[:, 0:T * NE].rearrange("p (t e) -> p t e", t=T), row(places[:, 2, :], NE),
                   ALU.add).then_inc(*free)
                dve.wait_ge(*emptied(l, "places"))
                for k, hot in enumerate((3, 5)):
                    link(tt(r1[:, 4], r1[:, 2], r1[:, hot], ALU.mult))
                    link(dve.tensor_reduce(slotf[:, :, k], r1[:, 4], AX.X, ALU.add))
                    link(tt(r1[:, 4], gate[:, :, :], r1[:, hot], ALU.mult))
                    link(dve.tensor_reduce(info[:, :, k, 2].bitcast(F32), r1[:, 4], AX.X, ALU.add))
                dve.tensor_copy(slot[:, :, :], slotf[:, :, :]).then_inc(*did("slots"))
                with dve.Fori(0, NPAIR) as pair:
                    n2 = 2 * l * NPAIR + 1
                    for q in range(2):
                        for k, turned_k4 in ((0, "moe_half"), (4, "moe_turned")):
                            dve.wait_ge(sg.sem(turned_k4), 2 * pair + (n2 + q))
                            ins = tt(xgT[:, q, k:k + 4, :], psum[6 * q + k // 4][:, :].rearrange("p (k s) -> p k s", k=4),
                                     bc(prm[:, PC["ffn"] + k:PC["ffn"] + k + 4], P), ALU.mult)
                        ins.then_inc(sg.sem("moe_xgT"), 1)
                    for q in range(2):
                        dve.wait_ge(sg.sem("moe_tanh"), 2 * pair + (n2 + q))
                        stt(th[:, q, :], th[:, q, :], 1.0, psum[4 + q][:, 0:FE], ALU.add, ALU.mult).then_inc(
                            sg.sem("moe_silu"), 1)
                        dve.wait_ge(sg.sem("moe_silu"), 2 * pair + (n2 + q))
                        tt(hid[:, q, :], th[:, q, :], psum[4 + q][:, FE:2 * FE], ALU.mult).then_inc(
                            sg.sem("moe_hid"), 1)
                for i in range(T):
                    dve.wait_ge(*after(l, f"y_in{i % 2}", 16 * (i // 2 + 1)))
                    link(tt(x[:, i, :], x[:, i, :], yb[:, i % 2, 0:D], ALU.add))
                    tt(x[:, i, :], x[:, i, :], yb[:, i % 2, D:2 * D], ALU.add).then_inc(*did("y_added"))

        per = {n: c // L for n, c in sg.counted.items() if not n.startswith("moe_")}
        assert per == PER1, f"PER1 = {per}"
    return list(sg.sems.values())


def block_two(nc, A, x, out):
    ctx = ExitStack()
    with ctx:
        def sb(name, shape, dt=F32):
            return ctx.enter_context(nc.sbuf_tensor("b2_" + name, shape, dt))

        cn = sb("cn", [P, 4 * P])
        lvl = sb("lvl", [P, 2, LEVELS, P])
        prm = sb("prm", [P, PC2N])
        prb = sb("prb", [P, PB2N])
        w_g2 = sb("w_g2", [GR, GKW])
        actT = sb("actT", [P, KD, S])
        ring = [sb(f"ring{n}", [P, KD * 512]) for n in range(3)]
        qkv = sb("qkv", [P, 12, S])
        gqk = sb("gqk", [P, 4, S])
        nat = sb("nat", [P, T, NATW2])
        y = sb("y", [P, T, D])
        kn = sb("kn", [P, T, DH, P])
        vb = sb("vb", [P, T, DH, P])
        sqb = sb("sqb", [P, 2, S])
        qs = sb("qs", [P, 2, S])
        kdn = sb("kdn", [P, 2, T, P])
        gst = sb("gst", [P, GH, P])
        ones = sb("ones", [P, P])
        cst = sb("cst", [P, 4])
        sm = sb("sm", [P, 14, T, DH])
        rf = sb("rf", [P, 4, 16])
        ss = sb("ss", [P, 40])
        ms = sb("ms", [P, 40])
        rs = sb("rs", [P, 40])
        half = sb("half", [P, 40])
        mats = {n: sb(n, [P, DH, P])[:, :, :] for n in (
            "attT", "wT", "u", "vnew", "kb", "qt", "kdec", "st", "gaT")}
        spare = actT[:, :, :].rearrange("p (n k) s -> p n (k s)", n=8)
        for n, name in enumerate(("eg", "dn", "dt", "lm", "lt", "inv", "invT", "t1")):
            mats[name] = spare[:, n, :].rearrange("p (h s) -> p h s", h=DH)
        sq2 = actT[:, 4:8, :].rearrange("p t (g d) -> p t g d", d=P)
        by_head = lambda a: a[:, 0:T * 2 * DH].rearrange("p (t g) -> p t g", t=T)
        ltm = sqb[:, :, :].rearrange("p b (h s) -> p b h s", h=DH)
        free1 = ring[1][:, :]
        bc_, arg, ex, qt2 = (free1[:, n * 1024:(n + 1) * 1024].rearrange("p (c s) -> p c s", c=2) for n in range(4))
        ka2 = qkv[:, 8:12, :].rearrange("p a s -> p (a s)").rearrange("p (c t b j) -> p c t b j", c=2, t=T, b=2)
        grT = mats["u"][0:GR, :, :].rearrange("p h s -> p (h s)")
        ident, upper, low = cn[:, 0:P], cn[:, P:2 * P], cn[:, 3 * P:4 * P]

        sg = Signals(nc, ctx, "b2_", PER2)
        banks = Banks(nc, ctx, "b2_", sg, PLAN2, BANK2)
        did, after = sg.did, sg.after
        filled, emptied, vacant = banks.filled, banks.emptied, banks.vacant
        reader, writer = banks.reader, banks.writer

        def heads(bank):
            return bank[:, :].rearrange("p (h s) -> p h s", h=DH)

        def bc(ap, n):
            return ap.unsqueeze(len(ap.shape)).to_broadcast([*ap.shape, n])

        def every(ap, n=DH):
            return ap.unsqueeze(1).to_broadcast([P, n, ap.shape[-1]])

        last_use = [("T", 4 * c + 3) for c in range(4)] + [("nat", 4 * c + 3) for c in range(4)]
        last_use += [("wo", 2 * T - 1)] * 2
        block = ctx.enter_context(nc.Block())

        @block.sync
        def _(sp):
            sp.dma_start(cn[:, :], A["consts"][:, 0:4 * P]).then_inc(*did("const", 16))
            sp.dma_start(lvl[:, :, :, :], A["consts"][:, CN["lvl"]:CNN].rearrange(
                "p (a n m) -> p a n m", a=2, n=LEVELS)).then_inc(*did("const", 16))
            for l in range(L):
                wt = A["w_in2_t"][l].rearrange("(k p) n -> p k n", p=P)
                wn = A["w_in2_n"][l].rearrange("(k p) n -> p k n", p=P)
                wout = A["w_out2"][l].rearrange("(k p) n -> p k n", p=P)
                if l:
                    for i in range(T):
                        sp.wait_ge(*after(l - 1, "ln_done", i + 1))
                sp.dma_start(prm[:, :], A["pc2"][l]).then_inc(*did("prm", 16))
                sp.dma_start(prb[:, :], A["pb2"][l]).then_inc(*did("prm", 16))
                sp.dma_start(w_g2[:, :], A["w_g2"][l]).then_inc(*did("prm", 16))

                def load(n, src, width):
                    if n >= 3:
                        sp.wait_ge(*filled(l, *last_use[n - 3]))
                    sp.dma_start(ring[n % 3][:, 0:KD * width].rearrange("p (k n) -> p k n", k=KD),
                                 src).then_inc(*did(f"w_in{n % 3}", 16))

                for c in range(4):
                    load(c, wt[:, :, c * 512:(c + 1) * 512], 512)
                for c in range(4):
                    load(4 + c, wn[:, :, c * NCW2:(c + 1) * NCW2], NCW2)
                for c in range(2):
                    load(8 + c, wout[:, :, c * 512:(c + 1) * 512], 512)
            for i in range(T):
                sp.wait_ge(*after(L - 1, "ln_done", i + 1))
                sp.dma_start(out[i * P:(i + 1) * P, :], x[:, i, :]).then_inc(*did("stored", 16))
            sp.wait_ge(sg.sem("stored"), 16 * T)

        @block.tensor
        def _(pe):
            def turn(l, stage, src, ready=None):
                for k in range(KD):
                    if ready:
                        pe.wait_ge(*ready(k))
                    pe.wait_ge(*vacant(l, stage, k))
                    bank, full = writer(l, stage, k)
                    for i in range(T):
                        ins = pe.transpose(bank[:, i * P:(i + 1) * P], src[:, i, k * P:(k + 1) * P], ident)
                    ins.then_inc(*full)
                for k in range(KD):
                    pe.wait_ge(*emptied(l, stage, k))

            def four(l, stage, lhsT, rhs, n=0):
                pe.wait_ge(*vacant(l, stage, n))
                bank, full = writer(l, stage, n)
                for h in range(DH):
                    ins = pe.matmul(bank[:, h * P:(h + 1) * P], lhsT(h), rhs(h), start=True, stop=True)
                ins.then_inc(*full)

            pe.wait_ge(sg.sem("const"), 32)
            for l in range(L):
                if l:
                    for i in range(T):
                        pe.wait_ge(*after(l - 1, "ln_done", i + 1))
                turn(l, "xT", x)
                for c in range(16):
                    if c % 4 == 0:
                        n = c // 4
                        pe.wait_ge(*after(l, f"w_in{n % 3}", 16 * (n // 3 + 1)))
                    w = ring[n % 3][:, :].rearrange("p (k n) -> p k n", k=KD)
                    pe.wait_ge(*vacant(l, "T", c))
                    bank, full = writer(l, "T", c)
                    for k in range(KD):
                        ins = pe.matmul(bank[:, :], w[:, k, (c % 4) * P:(c % 4 + 1) * P], actT[:, k, :],
                                        start=k == 0, stop=k == KD - 1)
                    ins.then_inc(*full)
                for c in range(4):
                    n = 4 + c
                    pe.wait_ge(*after(l, f"w_in{n % 3}", 16 * (n // 3 + 1)))
                    w = ring[n % 3][:, 0:KD * NCW2].rearrange("p (k n) -> p k n", k=KD)
                    for i in range(T):
                        pe.wait_ge(*vacant(l, "nat", c * T + i))
                        bank, full = writer(l, "nat", c * T + i)
                        for k in range(KD):
                            ins = pe.matmul(bank[:, 0:NCW2], actT[:, k, i * P:(i + 1) * P], w[:, k, :],
                                            start=k == 0, stop=k == KD - 1)
                        ins.then_inc(*full)
                pe.wait_ge(*after(0, "ones", 1))
                for c in range(8):
                    pe.wait_ge(*after(l, "sq", c + 1))
                    pe.wait_ge(*vacant(l, "l2", c))
                    bank, full = writer(l, "l2", c)
                    pe.matmul(bank[:, :], ones[:, :], sqb[:, c % 2, :], start=True, stop=True).then_inc(*full)
                pe.wait_ge(*after(l, "silu", 12))
                pe.wait_ge(*after(l, "beta", 1))
                for t in range(T):
                    pe.wait_ge(*vacant(l, "vn", t))
                    bank, full = writer(l, "vn", t)
                    for h in range(DH):
                        ins = pe.transpose(bank[:, h * P:(h + 1) * P], qkv[:, 8 + h, t * P:(t + 1) * P], ident)
                    ins.then_inc(*full)
                pe.wait_ge(*after(l, "gcum_in", 1))
                pe.wait_ge(*vacant(l, "gc"))
                bank, full = writer(l, "gc")
                pe.matmul(bank[:, 0:T * DH], upper, sm[:, 2, :, :].rearrange("p t h -> p (t h)"),
                          start=True, stop=True).then_inc(*full)
                pe.wait_ge(*after(l, "l2n", 8))
                for t in range(T):
                    pe.wait_ge(*vacant(l, "kn", t))
                    bank, full = writer(l, "kn", t)
                    for h in range(DH):
                        ins = pe.transpose(bank[:, h * P:(h + 1) * P], qkv[:, 4 + h, t * P:(t + 1) * P], ident)
                    ins.then_inc(*full)
                m = mats
                for t in range(T):
                    tok = slice(t * P, (t + 1) * P)
                    pe.wait_ge(*after(l, "g_rep", t + 1))
                    four(l, f"gb{t}", lambda h: m["vnew"][:, h, :], lambda h: upper)
                    four(l, f"kk{t}", lambda h: qkv[:, 4 + h, tok], lambda h: qkv[:, 4 + h, tok])
                    four(l, f"qk{t}", lambda h: qkv[:, 4 + h, tok], lambda h: qkv[:, h, tok])
                    pe.wait_ge(*after(l, "lm", t + 1))
                    pe.wait_ge(*vacant(l, f"lt{t}"))
                    bank, full = writer(l, f"lt{t}")
                    for h in range(DH):
                        ins = pe.transpose(bank[:, h * P:(h + 1) * P], m["lm"][:, h, :], ident)
                    ins.then_inc(*full)
                    for n in range(1, LEVELS):
                        pe.wait_ge(*after(l, "inv", (LEVELS - 1) * t + n))
                        pe.wait_ge(*after(l, "ltm", (LEVELS - 1) * t + n))
                        pe.wait_ge(*vacant(l, f"lv{t}", 3 * (n - 1)))
                        bank, full = writer(l, f"lv{t}", 3 * (n - 1))
                        for h in range(DH):
                            ins = pe.matmul(bank[:, h * P:(h + 1) * P], ltm[:, n % 2, h, :], m["inv"][:, h, :],
                                            start=True, stop=True)
                        ins.then_inc(*full)
                        pe.wait_ge(*emptied(l, f"lv{t}", 3 * (n - 1)))
                        four(l, f"lv{t}", lambda h: m["t1"][:, h, :], lambda h: m["invT"][:, h, :], 3 * (n - 1) + 1)
                        if n < LEVELS - 1:
                            four(l, f"lv{t}", lambda h: m["invT"][:, h, :], lambda h: m["t1"][:, h, :], 3 * (n - 1) + 2)
                    pe.wait_ge(*after(l, "kb", t + 1))
                    pe.wait_ge(*emptied(l, f"lv{t}", 3 * (LEVELS - 2) + 1))
                    four(l, f"u{t}", lambda h: m["invT"][:, h, :], lambda h: vb[:, t, h, :])
                    four(l, f"wT{t}", lambda h: m["kb"][:, h, :], lambda h: m["invT"][:, h, :])
                    pe.wait_ge(*emptied(l, f"u{t}"))
                    pe.wait_ge(*emptied(l, f"wT{t}"))
                    if t:
                        pe.wait_ge(*after(l, "state", t))
                        four(l, f"ws{t}", lambda h: m["wT"][:, h, :], lambda h: m["st"][:, h, :])
                    pe.wait_ge(*after(l, "vnew", t + 1))
                    pe.wait_ge(*vacant(l, f"o{t}"))
                    bank, full = writer(l, f"o{t}")
                    for h in range(DH):
                        if t:
                            pe.matmul(bank[:, h * P:(h + 1) * P], m["qt"][:, h, :], m["st"][:, h, :],
                                      start=True, stop=False)
                        ins = pe.matmul(bank[:, h * P:(h + 1) * P], m["attT"][:, h, :], m["vnew"][:, h, :],
                                        start=not t, stop=True)
                    ins.then_inc(*full)
                    if t < T - 1:
                        four(l, f"sk{t}", lambda h: m["kdec"][:, h, :], lambda h: m["vnew"][:, h, :])
                pe.wait_ge(*vacant(l, "grT"))
                bank, full = writer(l, "grT")
                for i in range(T):
                    ins = pe.transpose(bank[0:GR, i * P:(i + 1) * P], nat[:, i, O2_GR:O2_GR + GR], ident)
                ins.then_inc(*full)
                pe.wait_ge(*emptied(l, "grT"))
                pe.wait_ge(*after(l, "prm", 48))
                for c in range(2):
                    pe.wait_ge(*vacant(l, "gl", c))
                    bank, full = writer(l, "gl", c)
                    pe.matmul(bank[:, :], w_g2[:, c * P:(c + 1) * P], grT[:, :], start=True, stop=True).then_inc(*full)
                pe.wait_ge(*after(l, "kd", 1))
                for c in range(2):
                    pe.wait_ge(*vacant(l, "kd", c))
                    bank, full = writer(l, "kd", c)
                    for t in range(T):
                        ins = pe.transpose(bank[:, t * P:(t + 1) * P], ex[:, c, t * P:(t + 1) * P], ident)
                    ins.then_inc(*full)
                for c in range(2):
                    pe.wait_ge(*emptied(l, "kd", c))
                pe.wait_ge(*after(l, "gla_in", 1))
                for t in range(T):
                    for q in range(2):
                        pe.wait_ge(*vacant(l, f"ga{t}", q))
                        bank, full = writer(l, f"ga{t}", q)
                        for c in range(2):
                            for b in range(2):
                                o = c * P + b * 64
                                ins = pe.matmul(bank[:, o:o + 64], ka2[q * GK:(q + 1) * GK, c, t, b, :],
                                                qt2[q * GK:(q + 1) * GK, c, t * P + b * 64:t * P + (b + 1) * 64],
                                                start=True, stop=True)
                        ins.then_inc(*full)
                    for q in range(2):
                        pe.wait_ge(*emptied(l, f"ga{t}", q))
                    if t:
                        pe.wait_ge(*after(l, "gstate", t))
                    pe.wait_ge(*vacant(l, f"go{t}"))
                    bank, full = writer(l, f"go{t}")
                    for h in range(GH):
                        c = h // 2
                        v = nat[:, t, O2_GV + h * GV:O2_GV + (h + 1) * GV]
                        ins = pe.matmul(bank[:, h * P:(h + 1) * P], m["gaT"][:, h, :], v, start=True, stop=not t)
                        if t:
                            ins = pe.matmul(bank[:, h * P:(h + 1) * P], qs[:, c, t * P:(t + 1) * P],
                                            gst[:, h, :], start=False, stop=True)
                    ins.then_inc(*full)
                    if t < T - 1:
                        pe.wait_ge(*vacant(l, f"gs{t}"))
                        bank, full = writer(l, f"gs{t}")
                        for h in range(GH):
                            v = nat[:, t, O2_GV + h * GV:O2_GV + (h + 1) * GV]
                            ins = pe.matmul(bank[:, h * P:(h + 1) * P], kdn[:, h // 2, t, :], v,
                                            start=True, stop=True)
                        ins.then_inc(*full)
                turn(l, "yT", y, lambda k: after(l, "y", 1 + k // DH))
                for n in (8, 9):
                    pe.wait_ge(*after(l, f"w_in{n % 3}", 16 * (n // 3 + 1)))
                for n in range(2 * T):
                    i, c = divmod(n, 2)
                    w = ring[(8 + c) % 3][:, :].rearrange("p (k n) -> p k n", k=KD)
                    pe.wait_ge(*vacant(l, "wo", n))
                    bank, full = writer(l, "wo", n)
                    for k in range(KD):
                        ins = pe.matmul(bank[:, :], actT[:, k, i * P:(i + 1) * P], w[:, k, :],
                                        start=k == 0, stop=k == KD - 1)
                    ins.then_inc(*full)

        @block.scalar
        def _(act):
            m = mats

            def copy_out(l, stage, dst, i=0, scale=None):
                act.wait_ge(*filled(l, stage, i))
                bank, free = reader(l, stage, i)
                src = bank[:, 0:dst.free_size()]
                if len(dst.shape) == 3:
                    src = src.rearrange("p (a b) -> p a b", a=dst.shape[1])
                if scale is None:
                    act.activation(dst, src, ACT.Copy).then_inc(*free)
                else:
                    act.activation(dst, src, ACT.Identity, scale=scale).then_inc(*free)

            norm_of = lambda c: y[:, c // 2, (c % 2) * 512:(c % 2 + 1) * 512]

            def log_norm(l, c):
                act.wait_ge(*filled(l, "l2", c))
                bank, free = reader(l, "l2", c)
                act.activation(norm_of(c), bank[:, :], ACT.Ln, bias=cst[:, 0:1]).then_inc(*free)

            def inverse_norm(l, c):
                act.wait_ge(*emptied(l, "l2", c))
                act.activation(norm_of(c), norm_of(c), ACT.Exp, scale=-0.5,
                               bias=cst[:, 1:2] if c < DH else cst[:, 2:3]).then_inc(*did("l2r"))

            act.wait_ge(*after(0, "cst", 1))
            for l in range(L):
                act.wait_ge(*after(l, "prm", 48))
                for k in range(0, KD, 2):
                    copy_out(l, "xT", actT[:, k, :], k)
                for c in range(12):
                    act.wait_ge(*after(l, "conv", c + 1))
                    if c >= 2:
                        act.wait_ge(*after(l, "silu", c - 1))
                    act.activation(sqb[:, c % 2, :], qkv[:, c, :], ACT.Tanh, scale=0.5).then_inc(*did("tanh"))
                for c in range(4):
                    copy_out(l, "T", gqk[:, c, :], 12 + c)
                for n in range(16):
                    c, i = divmod(n, T)
                    copy_out(l, "nat", nat[:, i, c * NCW2:(c + 1) * NCW2], n)
                for n in range(16):
                    act.wait_ge(*emptied(l, "nat", n))
                act.activation(sm[:, 0, :, :], nat[:, :, O2_B:O2_B + DH], ACT.Tanh, scale=0.5).then_inc(*did("beta_tanh"))
                act.wait_ge(*after(l, "silu", 12))
                for c in range(8):
                    if c >= 2:
                        act.wait_ge(*filled(l, "l2", c - 2))
                    act.activation(sqb[:, c % 2, :], qkv[:, c, :], ACT.Square).then_inc(*did("sq"))
                    if c:
                        log_norm(l, c - 1)
                log_norm(l, 7)
                for c in range(8):
                    inverse_norm(l, c)
                act.wait_ge(*after(l, "g_abs", 1))
                act.activation(sm[:, 5, :, :], sm[:, 4, :, :], ACT.Exp).then_inc(*did("g_e"))
                act.wait_ge(*after(l, "g_e", 1))
                act.activation(sm[:, 6, :, :], sm[:, 5, :, :], ACT.Ln, bias=1.0)
                act.activation(rf[:, 3, 0:DH], prb[:, PB2["alog"]:PB2["alog"] + DH], ACT.Exp).then_inc(*did("g_ln"))
                act.wait_ge(*after(l, "gcol", 1))
                act.activation(sm[:, 9, :, :], sm[:, 7, :, :], ACT.Exp).then_inc(*did("g_exp"))
                for t in range(T):
                    copy_out(l, "kn", kn[:, t, :, :], t)
                for t in range(T):
                    if t:
                        act.wait_ge(*filled(l, f"o{t - 1}"))
                        act.wait_ge(*after(l, "tile", t))
                    act.wait_ge(*filled(l, f"gb{t}"))
                    bank, free = reader(l, f"gb{t}")
                    act.activation(m["eg"][:, :, :], heads(bank), ACT.Exp).then_inc(*did("eg"))
                    act.wait_ge(*after(l, "d_arg", t + 1))
                    act.activation(m["dn"], m["dn"], ACT.Exp, scale=-1.0)
                    act.activation(m["dt"], m["dt"], ACT.Exp).then_inc(*did("decay"))
                    copy_out(l, f"lt{t}", m["lt"])
                    for n in range(1, LEVELS):
                        copy_out(l, f"lv{t}", m["t1"], 3 * (n - 1))
                    copy_out(l, f"u{t}", m["u"])
                    copy_out(l, f"wT{t}", m["wT"])
                    copy_out(l, f"o{t}", y[:, t, 0:DW])
                act.wait_ge(*after(l, "gg_abs", 1))
                act.activation(arg[:, :, :], arg[:, :, :], ACT.Exp).then_inc(*did("gg_e"))
                act.wait_ge(*after(l, "gg_e", 1))
                act.activation(ex[:, :, :], arg[:, :, :], ACT.Ln, bias=1.0).then_inc(*did("gg_ln"))
                act.wait_ge(*after(l, "x_last", 1))
                act.activation(ex[:, :, :], arg[:, :, :], ACT.Exp, scale=-1.0).then_inc(*did("e_last"))
                act.wait_ge(*after(l, "e_last", 1))
                act.activation(arg[:, :, :], bc_[:, :, :], ACT.Exp).then_inc(*did("e_start"))
                act.wait_ge(*after(l, "x_own", 1))
                act.activation(qt2[:, :, :], arg[:, :, :], ACT.Exp).then_inc(*did("e_own"))
                act.wait_ge(*after(l, "e_own", 1))
                act.activation(arg[:, :, :], arg[:, :, :], ACT.Exp, scale=-1.0).then_inc(*did("e_ownk"))
                act.wait_ge(*after(l, "x_cross", 1))
                act.activation(ka2[:, :, :, 1, 0:64].rearrange("p c t j -> p (c t) j"),
                               ka2[:, :, :, 1, 0:64].rearrange("p c t j -> p (c t) j"), ACT.Exp,
                               scale=-1.0).then_inc(*did("e_cross"))
                for c in range(2):
                    copy_out(l, "kd", kdn[:, c, :, :], c)
                act.wait_ge(*after(l, "tile", T))
                for t in range(T):
                    for n, o in enumerate((O2_Z, O2_GZ)):
                        ins = act.activation(actT[:, 4 * n + t, :], nat[:, t, o:o + 512], ACT.Tanh, scale=0.5)
                    ins.then_inc(*did("z_tanh"))
                act.wait_ge(*emptied(l, f"o{T - 1}"))
                for t in range(T):
                    copy_out(l, f"go{t}", y[:, t, DW:])
                    if t in (1, 2):
                        for i in (2 * t - 2, 2 * t - 1):
                            for h in range(DH):
                                ins = act.activation(kn[:, i, h, :], y[:, i, h * P:(h + 1) * P], ACT.Square,
                                                     accum_out=ss[:, 8 * i + h:8 * i + h + 1])
                ins.then_inc(*did("ss_y"))
                for k in range(0, KD, 2):
                    name = "dng" if k < DH else "glag"
                    copy_out(l, "yT", actT[:, k, :], k, scale=prm[:, PC2[name]:PC2[name] + 1])
                for i in range(T):
                    act.wait_ge(*after(l, "ln_mean", i + 1))
                    act.activation(y[:, i, :], x[:, i, :], ACT.Square, accum_out=ss[:, 32 + i:33 + i]).then_inc(*did("ln_sq"))

        @block.gpsimd
        def _(pool):
            chain = [0]

            def link(ins):
                chain[0] += 1
                ins.then_inc(sg.sem("pool_step"), 1)
                pool.wait_ge(sg.sem("pool_step"), chain[0])

            pool.memset(ones[:, :], 1.0)
            link(pool.memset(half[:, :], -0.5))
            pool.memset(cst[:, 0:1], 4 * EPS)
            pool.memset(cst[:, 2:3], 0.0)
            link(pool.memset(cst[:, 1:2], float(-0.5 * np.log(DK))))
            pool.memset(cst[:, 3:4], 0.0).then_inc(*did("cst"))
            pool.memset(ms[:, 0:1], 0.0).then_inc(*did("ones"))
            pool.wait_ge(sg.sem("const"), 32)
            for l in range(L):
                for t in range(T):
                    for n in range(1, LEVELS):
                        s = (LEVELS - 1) * t + n
                        if n == 1:
                            pool.wait_ge(*emptied(l, f"lt{t}"))
                            for c in range(8):
                                if t == 0:
                                    pool.wait_ge(*filled(l, "l2", c))
                        if n >= 3:
                            pool.wait_ge(*filled(l, f"lv{t}", 3 * (n - 3)))
                        elif t:
                            pool.wait_ge(*filled(l, f"lv{t - 1}", 3 * (LEVELS - 2)))
                        pool.tensor_tensor(ltm[:, n % 2, :, :], mats["lt"], every(lvl[:, 1, n, :]),
                                           ALU.mult).then_inc(*did("ltm"))
                for n in range(2):
                    pool.wait_ge(*after(l, "ss_y" if n == 0 else "ss_gy", 1))
                    s_n, m_n, r_n = (by_head(a)[:, :, n * DH:(n + 1) * DH] for a in (ss, ms, rs))
                    link(pool.tensor_scalar(m_n, s_n, 1.0 / P, EPS, ALU.mult, ALU.add))
                    pool.tensor_tensor(r_n, m_n, half[:, 0:T * DH].rearrange("p (t g) -> p t g", t=T),
                                       ALU.pow).then_inc(*did("rs_y"))
                for i in range(T):
                    pool.wait_ge(*after(l, "ln_sq", i + 1))
                    k = slice(32 + i, 33 + i)
                    link(pool.tensor_scalar(ms[:, k], ss[:, k], 1.0 / D, EPS, ALU.mult, ALU.add))
                    pool.tensor_tensor(rs[:, k], ms[:, k], half[:, 0:1], ALU.pow).then_inc(*did("ln_rs"))

        @block.vector
        def _(dve):
            chain = [0]
            m = mats

            def link(ins):
                chain[0] += 1
                ins.then_inc(sg.sem("dve_step"), 1)
                dve.wait_ge(sg.sem("dve_step"), chain[0])

            def tt(out, a, b, op):
                return dve.tensor_tensor(out, a, b, op)

            def ts(out, a, s1, s2=None, op0=ALU.mult, op1=None):
                return dve.tensor_scalar(out, a, s1, s2, op0, op1) if op1 is not None else dve.tensor_scalar(out, a, s1, None, op0)

            def stt(out, a, s, b, op0, op1):
                return dve.scalar_tensor_tensor(out=out, in0=a, scalar=s, in1=b, op0=op0, op1=op1)

            link(dve.memset(gst[:, :, :], 0.0))
            dve.wait_ge(*after(0, "const", 32))
            for l in range(L):
                dve.wait_ge(*after(l, "prm", 48))
                for k in range(1, KD, 2):
                    dve.wait_ge(*filled(l, "xT", k))
                    bank, free = reader(l, "xT", k)
                    dve.tensor_copy(actT[:, k, :], bank[:, :]).then_inc(*free)

                def silu(c):
                    dve.wait_ge(*after(l, "tanh", c + 1))
                    stt(qkv[:, c, :], sqb[:, c % 2, :], 1.0, qkv[:, c, :], ALU.add, ALU.mult).then_inc(*did("silu"))

                for c in range(12):
                    dve.wait_ge(*filled(l, "T", c))
                    bank, free = reader(l, "T", c)
                    w = PC2["cw"] + 4 * c
                    link(ts(qkv[:, c, :], bank[:, :], prm[:, w + 3:w + 4]))
                    for d in range(1, 4):
                        ins = stt(qkv[:, c, d:], bank[:, 0:S - d], prm[:, w + 3 - d:w + 4 - d], qkv[:, c, d:],
                                  ALU.mult, ALU.add)
                        if d < 3:
                            link(ins)
                    link(ins)
                    dve.engine_nop().then_inc(*free)
                    dve.engine_nop().then_inc(*did("conv"))
                    if c:
                        silu(c - 1)
                silu(11)
                dve.wait_ge(*after(l, "beta_tanh", 1))
                link(ts(sm[:, 1], sm[:, 0], 0.5, 0.5, ALU.mult, ALU.add))
                ts(sm[:, 11], sm[:, 1], 0.5).then_inc(*did("beta"))
                dtb = prb[:, PB2["dtb"]:PB2["dtb"] + DH].unsqueeze(1).to_broadcast([P, T, DH])
                link(tt(sm[:, 3], nat[:, :, O2_A:O2_A + DH], dtb, ALU.add))
                stt(sm[:, 4], sm[:, 3], -1.0, sm[:, 3], ALU.mult, ALU.min).then_inc(*did("g_abs"))
                for c in range(8):
                    dve.wait_ge(*after(l, "l2r", c + 1))
                    tt(qkv[:, c, :], qkv[:, c, :], y[:, c // 2, (c % 2) * 512:(c % 2 + 1) * 512], ALU.mult).then_inc(*did("l2n"))
                dve.wait_ge(*after(l, "g_ln", 1))
                link(stt(sm[:, 2], sm[:, 3], 0.0, sm[:, 6], ALU.max, ALU.add))
                stt(sm[:, 2], sm[:, 2], -1.0, rf[:, 3, 0:DH].unsqueeze(1).to_broadcast([P, T, DH]),
                    ALU.mult, ALU.mult).then_inc(*did("gcum_in"))
                dve.wait_ge(*after(l, "beta", 1))
                for t in range(T):
                    dve.wait_ge(*filled(l, "vn", t))
                    bank, free = reader(l, "vn", t)
                    tt(vb[:, t, :, :], heads(bank), bc(sm[:, 11, t, :], P), ALU.mult).then_inc(*free)
                dve.wait_ge(*filled(l, "gc"))
                bank, free = reader(l, "gc")
                flat = lambda n: sm[:, n, :, :].rearrange("p t h -> p (t h)")
                link(dve.tensor_copy(flat(7), bank[:, 0:T * DH]))
                ts(flat(8), bank[:, 0:T * DH], -1.0).then_inc(*free)
                dve.wait_ge(*emptied(l, "gc"))
                dve.engine_nop().then_inc(*did("gcol"))
                dve.wait_ge(*after(l, "g_exp", 1))
                link(tt(sm[:, 10], sm[:, 9], sm[:, 1], ALU.mult))
                dve.wait_ge(*after(l, "gcum_in", 1))
                for t in range(T):
                    dve.wait_ge(*emptied(l, "kn", t))
                for t in range(T):
                    tok = slice(t * P, (t + 1) * P)
                    if t:
                        dve.wait_ge(*filled(l, f"o{t - 1}"))
                        dve.wait_ge(*filled(l, f"sk{t - 1}"))
                    dve.tensor_copy(m["vnew"][:, :, :], bc(sm[:, 2, t, :], P)).then_inc(*did("g_rep"))
                    dve.wait_ge(*after(l, "eg", t + 1))
                    dve.wait_ge(*filled(l, f"gb{t}"))
                    bank, free = reader(l, f"gb{t}")
                    for h in range(DH):
                        ts(m["dn"][:, h, :], heads(bank)[:, h, :], sm[:, 8, t, h:h + 1], 0.0, ALU.add, ALU.max)
                    for h in range(DH):
                        ins = ts(m["dt"][:, h, :], heads(bank)[:, h, :], sm[:, 8, t, h:h + 1], 0.0, ALU.add, ALU.min)
                    ins.then_inc(*free)
                    dve.wait_ge(*emptied(l, f"gb{t}"))
                    dve.engine_nop().then_inc(*did("d_arg"))
                    dve.wait_ge(*after(l, "decay", t + 1))
                    dve.wait_ge(*filled(l, f"kk{t}"))
                    bank, free = reader(l, f"kk{t}")
                    tt(m["lm"], m["dn"], heads(bank), ALU.mult).then_inc(*free)
                    dve.wait_ge(*emptied(l, f"kk{t}"))
                    for h in range(DH):
                        ins = stt(m["lm"][:, h, :], m["lm"][:, h, :], sm[:, 1, t, h:h + 1], low, ALU.mult, ALU.mult)
                    ins.then_inc(*did("lm"))
                    dve.wait_ge(*filled(l, f"qk{t}"))
                    bank, free = reader(l, f"qk{t}")
                    tt(m["attT"], m["dt"], heads(bank), ALU.mult).then_inc(*free)
                    dve.wait_ge(*emptied(l, f"qk{t}"))
                    link(tt(m["attT"][:, :, :], m["attT"][:, :, :], every(upper), ALU.mult))
                    dve.wait_ge(*after(l, "lm", t + 1))
                    link(tt(m["inv"], m["lm"], every(lvl[:, 0, 0, :]), ALU.mult))
                    link(tt(m["inv"], every(ident), m["inv"], ALU.subtract))
                    dve.wait_ge(*emptied(l, f"lt{t}"))
                    link(tt(m["invT"], m["lt"], every(lvl[:, 1, 0, :]), ALU.mult))
                    tt(m["invT"], every(ident), m["invT"], ALU.subtract).then_inc(*did("inv"))
                    tt(m["kb"][:, :, :], kn[:, t, :, :], bc(sm[:, 10, t, :], P), ALU.mult).then_inc(*did("kb"))
                    link(tt(m["kdec"][:, :, :], kn[:, t, :, :], bc(m["dt"][:, :, P - 1], P), ALU.mult))
                    link(tt(m["qt"][:, :, :], qkv[:, 0:4, tok], m["eg"], ALU.mult))
                    for n in range(1, LEVELS):
                        if n < LEVELS - 1:
                            dve.wait_ge(*filled(l, f"lv{t}", 3 * (n - 1) + 2))
                        dve.wait_ge(*filled(l, f"lv{t}", 3 * (n - 1) + 1))
                        bank, free = reader(l, f"lv{t}", 3 * (n - 1) + 1)
                        tt(m["invT"], m["invT"], heads(bank), ALU.subtract).then_inc(*free)
                        if n < LEVELS - 1:
                            dve.wait_ge(*emptied(l, f"lv{t}", 3 * (n - 1) + 1))
                            dve.wait_ge(*filled(l, f"lv{t}", 3 * (n - 1) + 2))
                            bank, free = reader(l, f"lv{t}", 3 * (n - 1) + 2)
                            tt(m["inv"], m["inv"], heads(bank), ALU.subtract).then_inc(*free)
                            dve.wait_ge(*emptied(l, f"lv{t}", 3 * (n - 1) + 2))
                            dve.engine_nop().then_inc(*did("inv"))
                    dve.wait_ge(*emptied(l, f"u{t}"))
                    if t:
                        dve.wait_ge(*filled(l, f"ws{t}"))
                        bank, free = reader(l, f"ws{t}")
                        tt(m["vnew"][:, :, :], m["u"][:, :, :], heads(bank), ALU.subtract).then_inc(*free)
                        dve.wait_ge(*emptied(l, f"ws{t}"))
                        dve.engine_nop().then_inc(*did("vnew"))
                    else:
                        dve.tensor_copy(m["vnew"][:, :, :], m["u"][:, :, :]).then_inc(*did("vnew"))
                    dve.wait_ge(*filled(l, f"o{t}"))
                    if t < T - 1:
                        dve.wait_ge(*filled(l, f"sk{t}"))
                        bank, free = reader(l, f"sk{t}")
                        if t:
                            for h in range(DH):
                                ins = stt(m["st"][:, h, :], m["st"][:, h, :], m["eg"][:, h, P - 1:P],
                                          heads(bank)[:, h, :], ALU.mult, ALU.add)
                        else:
                            ins = dve.tensor_copy(m["st"][:, :, :], heads(bank))
                        ins.then_inc(*free)
                        dve.wait_ge(*emptied(l, f"sk{t}"))
                        dve.engine_nop().then_inc(*did("state"))
                    dve.engine_nop().then_inc(*did("tile"))
                dve.wait_ge(*filled(l, "grT"))
                bank, free = reader(l, "grT")
                dve.tensor_copy(grT[:, :], bank[0:GR, :]).then_inc(*free)
                for c in range(2):
                    dve.wait_ge(*filled(l, "gl", c))
                    bank, free = reader(l, "gl", c)
                    ts(qt2[:, c, :], bank[:, :], prm[:, PC2["gb"] + c:PC2["gb"] + c + 1], None, ALU.add).then_inc(*free)
                for c in range(2):
                    dve.wait_ge(*emptied(l, "gl", c))
                stt(arg[:, :, :], qt2[:, :, :], -1.0, qt2[:, :, :], ALU.mult, ALU.min).then_inc(*did("gg_abs"))
                dve.wait_ge(*after(l, "gg_ln", 1))
                link(stt(qt2[:, :, :], qt2[:, :, :], 0.0, ex[:, :, :], ALU.min, ALU.subtract))
                link(dve.memset(arg[:, :, :], 0.0))
                for c in range(2):
                    for t in range(T):
                        ins = dve.tensor_tensor_scan(bc_[:, c, t * P:(t + 1) * P], qt2[:, c, t * P:(t + 1) * P],
                                                     arg[:, c, t * P:(t + 1) * P], 0.0, ALU.add, ALU.add)
                        link(ins)
                link(ts(bc_[:, :, :], bc_[:, :, :], 1.0 / TAU))
                tiles = lambda ap, w: ap[:, :, :].rearrange("p c (t j) -> p (c t) j", j=w)
                gq = gqk[:, 0:2, :]
                gk = gqk[:, 2:4, :]
                tt(tiles(arg, P), tiles(bc_, P), bc(tiles(bc_, P)[:, :, P - 1], P), ALU.subtract).then_inc(*did("x_last"))
                dve.wait_ge(*after(l, "e_last", 1))
                tt(ex[:, :, :], ex[:, :, :], gk, ALU.mult).then_inc(*did("kd"))
                dve.wait_ge(*after(l, "e_start", 1))
                link(stt(qs[:, :, :], arg[:, :, :], GK ** -0.5, gq, ALU.mult, ALU.mult))
                link(dve.tensor_copy(rf[:, 0, 0:2 * T], tiles(arg, P)[:, :, P - 1]))
                tt(tiles(arg, 64), tiles(bc_, 64), bc(tiles(bc_, 64)[:, :, 31], 64), ALU.subtract).then_inc(*did("x_own"))
                dve.wait_ge(*after(l, "e_ownk", 1))
                link(stt(qt2[:, :, :], qt2[:, :, :], GK ** -0.5, gq, ALU.mult, ALU.mult))
                link(dve.memset(ka2[:, :, :, 0, 64:128].rearrange("p c t j -> p (c t) j"), 0.0))
                own = tiles(arg, P)
                gkt = gk.rearrange("p c (t j) -> p (c t) j", j=P)
                kaf = ka2.rearrange("p c t b j -> p (c t) b j")
                link(tt(kaf[:, :, 0, 0:64], own[:, :, 0:64], gkt[:, :, 0:64], ALU.mult))
                link(tt(kaf[:, :, 1, 64:128], own[:, :, 64:128], gkt[:, :, 64:128], ALU.mult))
                tt(kaf[:, :, 1, 0:64], tiles(bc_, P)[:, :, 0:64], bc(tiles(bc_, P)[:, :, 95], 64),
                   ALU.subtract).then_inc(*did("x_cross"))
                dve.wait_ge(*after(l, "e_cross", 1))
                tt(kaf[:, :, 1, 0:64], kaf[:, :, 1, 0:64], gkt[:, :, 0:64], ALU.mult).then_inc(*did("gla_in"))
                for t in range(T):
                    if t:
                        dve.wait_ge(*filled(l, f"go{t - 1}"))
                    for q in range(2):
                        dve.wait_ge(*filled(l, f"ga{t}", q))
                        bank, free = reader(l, f"ga{t}", q)
                        tt(m["gaT"].rearrange("p (c q) s -> p q c s", q=2)[:, q],
                           bank[:, 0:2 * P].rearrange("p (c s) -> p c s", c=2), every(upper, 2),
                           ALU.mult).then_inc(*free)
                    if t < T - 1:
                        dve.wait_ge(*filled(l, f"go{t}"))
                        dve.wait_ge(*filled(l, f"gs{t}"))
                        bank, free = reader(l, f"gs{t}")
                        for h in range(GH):
                            c, own_rows = h // 2, slice((h % 2) * GK, (h % 2 + 1) * GK)
                            src = bank[own_rows, h * P:(h + 1) * P]
                            if t:
                                ins = stt(gst[own_rows, h, :], gst[own_rows, h, :],
                                          rf[own_rows, 0, c * T + t:c * T + t + 1], src, ALU.mult, ALU.add)
                            else:
                                ins = dve.tensor_copy(gst[own_rows, h, :], src)
                        ins.then_inc(*free)
                        dve.wait_ge(*emptied(l, f"gs{t}"))
                        dve.engine_nop().then_inc(*did("gstate"))
                    dve.wait_ge(*after(l, "z_tanh", t + 1))
                    for n, o in enumerate((O2_Z, O2_GZ)):
                        ins = stt(nat[:, t, o:o + 512], actT[:, 4 * n + t, :], 1.0, nat[:, t, o:o + 512],
                                  ALU.add, ALU.mult)
                    link(ins)
                dve.wait_ge(*emptied(l, f"go{T - 1}"))
                own = lambda n: y[:, :, n * DW:(n + 1) * DW].rearrange("p t (g d) -> p t g d", d=P)
                link(tt(sq2, own(1), own(1), ALU.mult))
                dve.tensor_reduce(by_head(ss)[:, :, DH:], sq2, AX.X, ALU.add).then_inc(*did("ss_gy"))
                for n, o in enumerate((O2_Z, O2_GZ)):
                    dve.wait_ge(*after(l, "rs_y", n + 1))
                    for t in range(T):
                        ins = tt(own(n)[:, t], own(n)[:, t], bc(by_head(rs)[:, t, n * DH:(n + 1) * DH], P), ALU.mult)
                    link(ins)
                    half_y = y[:, :, n * DW:(n + 1) * DW]
                    stt(half_y, half_y, 0.5, nat[:, :, o:o + 512], ALU.mult, ALU.mult).then_inc(*did("y"))
                for k in range(1, KD, 2):
                    name = "dng" if k < DH else "glag"
                    dve.wait_ge(*filled(l, "yT", k))
                    bank, free = reader(l, "yT", k)
                    ts(actT[:, k, :], bank[:, :], prm[:, PC2[name]:PC2[name] + 1]).then_inc(*free)
                def norm(i):
                    dve.wait_ge(*after(l, "ln_rs", i + 1))
                    link(stt(x[:, i, :], x[:, i, :], rs[:, 32 + i:33 + i], prb[:, 0:D], ALU.mult, ALU.mult))
                    tt(x[:, i, :], x[:, i, :], prb[:, PB2["lnb"]:PB2["lnb"] + D], ALU.add).then_inc(*did("ln_done"))

                for i in range(T):
                    for c in range(2):
                        dve.wait_ge(*filled(l, "wo", 2 * i + c))
                        bank, free = reader(l, "wo", 2 * i + c)
                        stt(x[:, i, c * 512:(c + 1) * 512], x[:, i, c * 512:(c + 1) * 512], ALPHA, bank[:, :],
                            ALU.mult, ALU.add).then_inc(*free)
                    for c in range(2):
                        dve.wait_ge(*emptied(l, "wo", 2 * i + c))
                    link(dve.tensor_reduce(rf[:, 1, i:i + 1], x[:, i, :], AX.X, ALU.add))
                    link(ts(rf[:, 2, i:i + 1], rf[:, 1, i:i + 1], 1.0 / D))
                    ts(x[:, i, :], x[:, i, :], rf[:, 2, i:i + 1], None, ALU.subtract).then_inc(*did("ln_mean"))
                    if i:
                        norm(i - 1)
                norm(T - 1)

        once = ("const", "cst", "ones", "stored")
        per = {n: c // L for n, c in sg.counted.items() if n not in once}
        assert per == PER2, f"PER2 = {per}"


def build(nc, A, out):
    with nc.sbuf_tensor("x", [P, T, D], F32) as x:
        with ExitStack() as sems:
            used = block_one(nc, A, x, sems)
            with nc.Block() as block:
                @block.gpsimd
                def _(pool):
                    for s in used:
                        pool.sem_clear(s)
        block_two(nc, A, x, out)


def columns(parts, n):
    out = np.zeros((P, n), np.float32)
    at = 0
    for a in parts:
        out[:a.shape[0], at:at + a.shape[1]] = a
        at += a.shape[1]
    return out


def lay_out(v):
    v = {k: np.asarray(a) for k, a in v.items()}
    A = {"x": v["x"].reshape(S, D), "positions": np.ascontiguousarray(v["positions"].reshape(T, P).T),
         "consts": constants()}
    for n in ("w_in", "w_out", "a_w_uq", "a_w_ukv", "c_w_s"):
        A[n] = v[n]
    for n in ("w1", "w3", "w2"):
        A[n] = v[n].reshape(L * NE, *v[n].shape[2:])
    A["w_r"] = np.concatenate([v["w_group"], v["w_expert"]], axis=-1)
    pc, pb = [], []
    for l in range(L):
        kt = lambda a: a.reshape(-1, P).T
        conv = v["m_conv_w"][l].reshape(4, 8, MD).transpose(2, 1, 0).reshape(MD, 32)
        pc.append(columns([kt(v["attn_norm"][l]), kt(v["ffn_norm"][l]), kt(v["mix_out_norm"][l]),
                           kt(v["a_q_norm"][l]), kt(v["a_kv_norm"][l]), v["c_b_s"][l].T, conv,
                           v["m_conv_b"][l].reshape(8, MD).T, v["m_gate_bias"][l][:MH, None],
                           v["m_gate_bias"][l][MH:, None]], PCN))
        row = np.concatenate([v["a_q_head_norm"][l], v["a_k_head_norm"][l], v["c_v_norm"][l],
                              v["b_group"][l], v["b_expert"][l]])
        pb.append(np.broadcast_to(row, (P, PBN)))
    A["pc"], A["pb"] = np.stack(pc), np.ascontiguousarray(np.stack(pb))
    w = v["w_in_2"]
    o = np.cumsum([0, 3 * DW, DW, 2 * DH, 2 * GKW, 2 * GW + GR])
    A["w_in2_t"] = np.concatenate([w[:, :, o[0]:o[1]], w[:, :, o[3]:o[4]]], axis=-1)
    A["w_in2_n"] = np.concatenate([w[:, :, o[1]:o[3]], w[:, :, o[4]:o[5]]], axis=-1)
    A["w_out2"], A["w_g2"] = v["w_out_2"], v["gla_gate_w2_2"]
    A["pc2"] = np.stack([columns([v["conv_w_2"][l].reshape(4, 12, P).transpose(2, 1, 0).reshape(P, 48),
                                  v["dn_norm_g_2"][l][:, None], v["gla_norm_g_2"][l][:, None],
                                  v["gla_gate_b_2"][l].reshape(2, P).T], PC2N) for l in range(L)])
    A["pb2"] = np.stack([np.broadcast_to(np.concatenate([v[n][l] for n in (
        "ln_g_2", "ln_b_2", "dn_a_log_2", "dn_dt_bias_2")]), (P, PB2N)) for l in range(L)])
    return {k: np.ascontiguousarray(a) for k, a in A.items()}


def kernel(**inputs):
    import concourse.bacc as bacc
    from concourse.bass_utils import run_bass_kernel_spmd

    nc = bacc.Bacc("TRN2", target_bir_lowering=False, num_devices=1, dynamic_dma_scratch_size=2048)
    arrays = {f"in_{k}": a for k, a in lay_out(inputs).items()}
    A = {k[3:]: nc.dram_tensor(k, a.shape, mybir.dt.from_np(a.dtype), kind="ExternalInput").ap()
         for k, a in arrays.items()}
    out = nc.dram_tensor("out", (S, D), F32, kind="ExternalOutput").ap()
    build(nc, A, out)
    r = run_bass_kernel_spmd(nc, [arrays], core_ids=[0])
    return r.results[0]["out"].reshape(1, S, D)
```
